# Optimizing a Trainium2 kernel written in Bass

```python
import jax, jax.numpy as jnp
from jax import lax
import numpy as np

D_MODEL = 1024
BATCH = 1
SEQ = 2048
DEPTH = 1
DEC_BATCH = 8
DEC_SEQ = 16
PAST_LEN = 4096

CHUNK = 64
POOL_WINDOWS = (2, 4, 8, 16)
POOL_PAST = max(POOL_WINDOWS) - 1
POOL_WIDTH = D_MODEL // 4
POOL_GROUP = POOL_WIDTH // len(POOL_WINDOWS)
CONV_WIDTH = 3 * D_MODEL // 8
CONV_K = 31
SCONV_WIDTH = D_MODEL - POOL_WIDTH - CONV_WIDTH
SCONV_K = 3
MIX_WIDTH = POOL_WIDTH + CONV_WIDTH + SCONV_WIDTH
IN_WIDTH = POOL_WIDTH + 2 * CONV_WIDTH + 3 * SCONV_WIDTH
D_FF = -(-8 * D_MODEL // (3 * 256)) * 256
EPS = 1e-6

kernel_name = 'hybrid_pool_conv_streaming_step'

def _rmsnorm(x, g):
    xf = x.astype(jnp.float32)
    y = xf * lax.rsqrt(jnp.mean(xf * xf, axis=-1, keepdims=True) + EPS) * g.astype(jnp.float32)
    return y.astype(x.dtype)

def _depthwise_causal(ext, w):
    C = ext.shape[-1]
    return lax.conv_general_dilated(ext, w.astype(ext.dtype)[:, None, :], (1,), 'VALID',
                                    dimension_numbers=('NWC', 'WIO', 'NWC'),
                                    feature_group_count=C)

def _pool_mixer(xa, past, start, w_pool, s_pool):
    B, T, _ = xa.shape
    ext = jnp.concatenate([past.astype(xa.dtype), xa], axis=1)
    cs = jnp.pad(jnp.cumsum(ext.astype(jnp.float32), axis=1), ((0, 0), (1, 0), (0, 0)))
    pos = jnp.arange(T, dtype=jnp.float32) + start
    means = []
    for g, w in enumerate(POOL_WINDOWS):
        lo, hi = g * POOL_GROUP, (g + 1) * POOL_GROUP
        wsum = (cs[:, POOL_PAST + 1:POOL_PAST + 1 + T, lo:hi]
                - cs[:, POOL_PAST + 1 - w:POOL_PAST + 1 - w + T, lo:hi])
        cnt = jnp.minimum(pos + 1.0, float(w))[None, :, None]
        means.append(wsum / cnt)
    pooled = jnp.concatenate(means, axis=-1) - xa.astype(jnp.float32)
    pooled = pooled.reshape(B, T, len(POOL_WINDOWS), POOL_GROUP)
    mixed = jnp.einsum('btgc,gcd->btgd', pooled, w_pool.astype(jnp.float32)).reshape(B, T, POOL_WIDTH)
    y = (mixed * s_pool.astype(jnp.float32)).astype(xa.dtype)
    return y, ext[:, -POOL_PAST:]

def _conformer_conv(xb, past, w_dw, b_dw, ln_g, ln_b):
    a, g = jnp.split(xb, 2, axis=-1)
    u = a * jax.nn.sigmoid(g)
    ext = jnp.concatenate([past.astype(u.dtype), u], axis=1)
    z = (_depthwise_causal(ext, w_dw) + b_dw.astype(u.dtype)).astype(jnp.float32)
    mu = jnp.mean(z, axis=-1, keepdims=True)
    zc = z - mu
    var = jnp.mean(zc * zc, axis=-1, keepdims=True)
    z = zc * lax.rsqrt(var + EPS) * ln_g.astype(jnp.float32) + ln_b.astype(jnp.float32)
    return jax.nn.silu(z).astype(xb.dtype), ext[:, -(CONV_K - 1):]

def _short_conv(xc, past, w_sc):
    h, bg, cg = jnp.split(xc, 3, axis=-1)
    u = cg * h
    ext = jnp.concatenate([past.astype(u.dtype), u], axis=1)
    y = bg * _depthwise_causal(ext, w_sc)
    return y, ext[:, -(SCONV_K - 1):]

def _layer(x, c, pool_past, conv_past, sconv_past, start,
           w_ada, b_ada, g_pre_mix, g_post_mix, g_pre_ffn, g_post_ffn,
           w_in, w_pool, s_pool, w_dw, b_dw, ln_g, ln_b, w_sc, w_out,
           w_gate, w_up, w_down):
    mod = jax.nn.silu(c) @ w_ada + b_ada
    sh1, sc1, gt1, sh2, sc2, gt2 = [m[:, None, :] for m in jnp.split(mod, 6, axis=-1)]
    h = _rmsnorm(x, g_pre_mix) * (1 + sc1) + sh1
    proj = h @ w_in
    xa = proj[..., :POOL_WIDTH]
    xb = proj[..., POOL_WIDTH:POOL_WIDTH + 2 * CONV_WIDTH]
    xc = proj[..., POOL_WIDTH + 2 * CONV_WIDTH:]
    ya, pool_new = _pool_mixer(xa, pool_past, start, w_pool, s_pool)
    yb, conv_new = _conformer_conv(xb, conv_past, w_dw, b_dw, ln_g, ln_b)
    yc, sconv_new = _short_conv(xc, sconv_past, w_sc)
    mix = jnp.concatenate([ya, yb, yc], axis=-1) @ w_out
    x = x + gt1 * _rmsnorm(mix, g_post_mix)
    h = _rmsnorm(x, g_pre_ffn) * (1 + sc2) + sh2
    f = (jax.nn.silu(h @ w_gate) * (h @ w_up)) @ w_down
    x = x + gt2 * _rmsnorm(f, g_post_ffn)
    return x, pool_new, conv_new, sconv_new

def setup_inputs(seed: int = 0) -> dict:
    key = jax.random.key(seed)
    ks = jax.random.split(key, 25)
    f32 = jnp.float32

    def nrm(k, shape, s):
        return jax.random.normal(k, shape, f32) * s

    D = D_MODEL
    return {
        'x_prompt': nrm(ks[0], (BATCH, SEQ, D), 1.0),
        'x_sample': nrm(ks[1], (DEC_BATCH, DEC_SEQ, D), 1.0),
        'c_prompt': nrm(ks[2], (BATCH, D), 1.0),
        'c_sample': nrm(ks[3], (DEC_BATCH, D), 1.0),
        'state_pool': nrm(ks[4], (DEPTH, DEC_BATCH, POOL_PAST, POOL_WIDTH), 1.0),
        'state_conv': nrm(ks[5], (DEPTH, DEC_BATCH, CONV_K - 1, CONV_WIDTH), 0.5),
        'state_sconv': nrm(ks[6], (DEPTH, DEC_BATCH, SCONV_K - 1, SCONV_WIDTH), 1.0),
        'w_ada': nrm(ks[7], (DEPTH, D, 6 * D), 0.5 * D ** -0.5),
        'b_ada': nrm(ks[8], (DEPTH, 6 * D), 0.02),
        'g_pre_mix': 1.0 + nrm(ks[9], (DEPTH, D), 0.05),
        'g_post_mix': 1.0 + nrm(ks[10], (DEPTH, D), 0.05),
        'g_pre_ffn': 1.0 + nrm(ks[11], (DEPTH, D), 0.05),
        'g_post_ffn': 1.0 + nrm(ks[12], (DEPTH, D), 0.05),
        'w_in': nrm(ks[13], (DEPTH, D, IN_WIDTH), D ** -0.5),
        'w_pool': nrm(ks[14], (DEPTH, len(POOL_WINDOWS), POOL_GROUP, POOL_GROUP), POOL_GROUP ** -0.5),
        's_pool': 1.0 + nrm(ks[15], (DEPTH, POOL_WIDTH), 0.05),
        'w_dw': nrm(ks[16], (DEPTH, CONV_K, CONV_WIDTH), CONV_K ** -0.5),
        'b_dw': nrm(ks[17], (DEPTH, CONV_WIDTH), 0.02),
        'ln_g': 1.0 + nrm(ks[18], (DEPTH, CONV_WIDTH), 0.05),
        'ln_b': nrm(ks[19], (DEPTH, CONV_WIDTH), 0.02),
        'w_sc': nrm(ks[20], (DEPTH, SCONV_K, SCONV_WIDTH), SCONV_K ** -0.5),
        'w_out': nrm(ks[21], (DEPTH, MIX_WIDTH, D), MIX_WIDTH ** -0.5),
        'w_gate': nrm(ks[22], (DEPTH, D, D_FF), D ** -0.5),
        'w_up': nrm(ks[23], (DEPTH, D, D_FF), D ** -0.5),
        'w_down': nrm(ks[24], (DEPTH, D_FF, D), D_FF ** -0.5),
    }

def reference(x_prompt, x_sample, c_prompt, c_sample, state_pool, state_conv, state_sconv,
              w_ada, b_ada, g_pre_mix, g_post_mix, g_pre_ffn, g_post_ffn,
              w_in, w_pool, s_pool, w_dw, b_dw, ln_g, ln_b, w_sc, w_out,
              w_gate, w_up, w_down):
    xp, xs = x_prompt, x_sample
    bp = xp.shape[0]
    pool_p, conv_p, sconv_p = [], [], []
    pool_s, conv_s, sconv_s = [], [], []
    for l in range(DEPTH):
        lp = [w[l] for w in (w_ada, b_ada, g_pre_mix, g_post_mix, g_pre_ffn, g_post_ffn,
                             w_in, w_pool, s_pool, w_dw, b_dw, ln_g, ln_b, w_sc, w_out,
                             w_gate, w_up, w_down)]
        zp = jnp.zeros((bp, POOL_PAST, POOL_WIDTH), xp.dtype)
        zc = jnp.zeros((bp, CONV_K - 1, CONV_WIDTH), xp.dtype)
        zs = jnp.zeros((bp, SCONV_K - 1, SCONV_WIDTH), xp.dtype)
        xp, a, b, c = _layer(xp, c_prompt, zp, zc, zs, 0, *lp)
        pool_p.append(a); conv_p.append(b); sconv_p.append(c)
        xs, a, b, c = _layer(xs, c_sample, state_pool[l], state_conv[l], state_sconv[l], PAST_LEN, *lp)
        pool_s.append(a); conv_s.append(b); sconv_s.append(c)
    return (xp, xs,
            jnp.stack(pool_p), jnp.stack(conv_p), jnp.stack(sconv_p),
            jnp.stack(pool_s), jnp.stack(conv_s), jnp.stack(sconv_s))


_drawn_inputs = setup_inputs


def setup_inputs(seed=0):
    import zlib

    import numpy as np

    out = dict(_drawn_inputs(seed))
    spreads = {}
    factors = {'g_post_mix': 3.474,
     'g_pre_ffn': 2.9,
     'g_post_ffn': 4.042,
     's_pool': 7.748,
     'b_dw': 8.0,
     'ln_g': 7.315,
     'ln_b': 37.401}
    for name, (base, spread) in spreads.items():
        noise = np.random.default_rng([zlib.crc32(name.encode()), seed]).standard_normal(out[name].shape)
        drawn = base * np.exp(spread * noise) if base else spread * noise
        out[name] = __import__('jax').numpy.asarray(drawn.astype(out[name].dtype))
    for name, factor in factors.items():
        out[name] = (out[name] * factor).astype(out[name].dtype)
    return out
```

```python
from contextlib import ExitStack

import concourse.bass as bass
from concourse import mybir

F32 = mybir.dt.float32
F32R = mybir.dt.float32r
BF16 = mybir.dt.bfloat16
ALU = mybir.AluOpType
ACT = mybir.ActivationFunctionType

P = 128
D = 1024
KD = D // P
T_SAMPLE, T_PROMPT = 128, 2048
SEQS, STEPS = 8, 16
TILES = (T_SAMPLE + T_PROMPT) // P
TB = 3
NB = -(-TILES // TB)
LAST_TB = TILES - TB * (NB - 1)
N = TB * P
EPS = 1e-6
ROWS = 1 + SEQS
MOD_K = 2 * ROWS + 1

WINDOWS = (2, 4, 8, 16)
PAST = max(WINDOWS) - 1
NPOOL, NCONV, NSC = 2, 3, 3
TAPS, STAPS = 31, 3
HIST, SHIST = TAPS - 1, STAPS - 1
NMIX = NPOOL + NCONV + NSC
FF = 2816
NF = FF // P

ORDER = [("a", 0), ("g", 0), ("a", 1), ("g", 1), ("a", 2), ("g", 2),
         ("h", 0), ("c", 0), ("b", 0), ("h", 1), ("c", 1), ("b", 1), ("h", 2), ("c", 2), ("b", 2),
         ("x", 0), ("x", 1)]
NIN = len(ORDER)
SLOT = {"a": 0, "g": 3, "h": 6, "c": 9, "b": 12}
COL0 = {"x": 0, "a": 256, "g": 640, "h": 1024, "b": 1408, "c": 1792}

RING = 5
ADA_RING = 4
UNITS = NIN + NMIX
assert UNITS % RING == 0
NADA = 6 * KD

STAGE = ["t0", "t1", "t2", "t3", "mean", "t4", "t5", "pool0", "pool1", "t6", "var", "t7"]
STAGE_LAST = ["mean", "pool0", "pool1", "var"]
GROUPS = NIN + len(STAGE)

C_ID, C_EPS, C_NHALF = 0, P, P + TB
C_END = C_NHALF + TB
E_ONES, E_SELP, E_SELS, E_SELF, E_CNT = 0, P, 2 * P, 3 * P, 3 * P + ROWS
E_END = E_CNT + NPOOL * PAST
Q_G1, Q_G2, Q_SP, Q_WDW, Q_BDW, Q_LG, Q_LB, Q_WSC = 0, 8, 16, 18, 18 + 93, 114, 117, 120
Q_END = Q_WSC + 9


ACT_STEPS, ACT_STEPS_B, POOL_STEPS, VEC_STEPS_A, VEC_STEPS_B = 5, 4, 2, 130, 5


class Steps:

    def __init__(self, sem):
        self.sem, self.base, self.n = sem, 0, 0

    def step(self, instruction):
        instruction.then_inc(self.sem, 1)
        self.n += 1
        return self.base + self.n

    def enter_loop(self):
        self.before, self.base, self.n = self.base + self.n, None, 0

    def in_loop(self, i, per_pass):
        self.base = i * per_pass + self.before

    def leave_loop(self, passes, per_pass):
        assert self.n == per_pass, (self.n, per_pass)
        self.base, self.n = self.before + passes * per_pass, 0


def tiles_of(b):
    return LAST_TB if isinstance(b, int) and b == NB - 1 else TB


def unit_in(b, j):
    return j if isinstance(b, int) and b == 0 else UNITS * b - NMIX + j


def unit_out(b, k):
    if isinstance(b, int) and b == NB - 1:
        return UNITS * NB - NMIX + k
    return UNITS * (b + 1) - NMIX + NIN + k


def slot_in(j, first=False):
    return (j if first else j - NMIX) % RING


def slot_out(k, last=False):
    return (k - NMIX + (0 if last else NIN)) % RING


def build(nc, x_all, c_all, consts, consts_a, cols, gpost, b_ada, w_ada, w_mix, w_pool, w_gu, w_dn,
          st_pool, st_conv, st_sconv, y_all, o_pool_p, o_conv_p, o_sconv_p,
          o_pool_s, o_conv_s, o_sconv_s, x1_all):
    ctx = ExitStack()
    with ctx:
        def sb(name, shape, dt=F32, scope=ctx):
            return scope.enter_context(nc.sbuf_tensor(name, shape, dt))

        def sem(name):
            return ctx.enter_context(nc.semaphore(name))

        con = sb("con", [P, C_END])
        col = sb("col", [P, Q_END])
        shsc = sb("shsc", [P, 4, KD, ROWS])
        gate2 = sb("gate2", [P, D])
        gate2_first = sb("gate2_first", [P, D])
        raw = sb("raw", [P, RING, D])
        whi = sb("whi", [P, RING, D], F32R)
        wlo = sb("wlo", [P, RING, D], F32R)
        h_hi = sb("h_hi", [P, KD, N], F32R)
        h_lo = sb("h_lo", [P, KD, N], F32R)
        h_f = sb("h_f", [P, 2, N])
        xt = sb("xt", [P, TB, D])
        xr = sb("xr", [P, TB, D])
        junk = sb("junk", [P, D], BF16)
        ssq_x = sb("ssq_x", [P, TB])
        rstd_x = sb("rstd_x", [P, TB])
        ssq_m = sb("ssq_m", [P, TB])
        rstd_m = sb("rstd_m", [P, TB])
        ps = ctx.enter_context(nc.psum_tensor("ps", [P, 8, 512], F32))

        ident = con[:, C_ID:C_ID + P]
        eps = con[:, C_EPS:C_EPS + 1]

        const_landed = sem("const_landed")
        gpost_landed = sem("gpost_landed")
        c_landed = sem("c_landed")
        bias_landed = sem("bias_landed")
        pad_zeroed = sem("pad_zeroed")
        silu_c = sem("silu_c")
        c_hi_ready = sem("c_hi_ready")
        c_ready = sem("c_ready")
        ada_hi = sem("ada_hi")
        ada_lo = sem("ada_lo")
        ada_used = sem("ada_used")
        ada_read = sem("ada_read")
        cols_full = sem("cols_full")
        gates_full = sem("gates_full")
        mod_ready = sem("mod_ready")
        w_pool_zeroed = sem("w_pool_zeroed")
        hist_zeroed = sem("hist_zeroed")
        state_landed = sem("state_landed")
        w_hi = sem("w_hi")
        w_lo = sem("w_lo")
        w_used = sem("w_used")
        x_landed = sem("x_landed")
        x_ssq = sem("x_ssq")
        pool_step = sem("pool_step")
        x_rstd = sem("x_rstd")
        xn_ready = sem("xn_ready")
        sample_mod = sem("sample_mod")
        h_hi_ready = sem("h_hi_ready")
        h_lo_ready = sem("h_lo_ready")
        work_full = sem("work_full")
        work_read = sem("work_read")
        act_step = sem("act_step")
        vec_step = sem("vec_step")
        z_ready = sem("z_ready")
        zc_ready = sem("zc_ready")
        zsq_ready = sem("zsq_ready")
        seed_ready = sem("seed_ready")
        zn_ready = sem("zn_ready")
        pooled_ready = sem("pooled_ready")
        yb_ready = sem("yb_ready")
        yc_ready = sem("yc_ready")
        y_hi_ready = sem("y_hi_ready")
        y_lo_ready = sem("y_lo_ready")
        mix_ssq = sem("mix_ssq")
        mix_rstd = sem("mix_rstd")
        res_landed = sem("res_landed")
        res_first = sem("res_first")
        res_ready = sem("res_ready")
        stored = sem("stored")
        states_stored = sem("states_stored")
        gu_hi = sem("gu_hi")
        gate_lo = sem("gate_lo")
        up_lo = sem("up_lo")
        gu_used = sem("gu_used")
        dn_hi = sem("dn_hi")
        dn_lo = sem("dn_lo")
        dn_used = sem("dn_used")
        silu_ready = sem("silu_ready")
        g_ready = sem("g_ready")
        g_hi_ready = sem("g_hi_ready")
        g_lo_ready = sem("g_lo_ready")
        ada_landed = [sem(f"ada_landed{i}") for i in range(ADA_RING)]
        w_landed = [sem(f"w_landed{i}") for i in range(RING)]
        gu_landed = [sem(f"gu_landed{i}") for i in range(4)]
        dn_landed = [sem(f"dn_landed{i}") for i in range(2)]

        x_v = x_all.rearrange("(n p) d -> p n d", p=P)
        x1_v = x1_all.rearrange("(n p) d -> p n d", p=P)
        y_v = y_all.rearrange("(n p) d -> p n d", p=P)

        def group(b, name):
            if isinstance(name, int):
                at = name
            elif isinstance(b, int) and b == NB - 1:
                at = NIN + STAGE_LAST.index(name)
            else:
                at = NIN + STAGE.index(name)
            return KD + GROUPS * b + at

        WORK_A = KD + GROUPS * (NB - 1) + NIN + len(STAGE_LAST)

        def bank_of(local):
            return local % 2

        def full_count(b, name):
            names = STAGE_LAST if isinstance(b, int) and b == NB - 1 else STAGE
            return KD + len(STAGE) * b + names.index(name) + 1

        FULL_A = KD + len(STAGE) * (NB - 1) + len(STAGE_LAST)

        A = ExitStack()
        mod_scope = ExitStack()
        con_a = sb("con_a", [P, E_END], scope=A)
        c_sb = sb("c_sb", [P, KD, ROWS], scope=A)
        c_s = sb("c_s", [P, KD, ROWS], scope=A)
        gate1 = sb("gate1", [P, D], scope=A)
        gate1_first = sb("gate1_first", [P, D], scope=A)
        mod = sb("mod", [MOD_K, 6 * D], scope=mod_scope)
        c_hl = sb("c_hl", [P, KD, P], F32R, scope=mod_scope)
        c_h0 = sb("c_h0", [P, KD, P], F32R, scope=mod_scope)
        gp = sb("gp", [P, 2, D], scope=mod_scope)
        mod_scope.close()
        y_hi = sb("y_hi", [P, NMIX, N], F32R, scope=A)
        y_lo = sb("y_lo", [P, NMIX, N], F32R, scope=A)
        pr = sb("pr", [P, 15, N], scope=A)
        xa = sb("xa", [P, NPOOL, PAST + N], scope=A)
        u = sb("u", [P, NCONV, HIST + N], scope=A)
        su = sb("su", [P, NSC, SHIST + N], scope=A)
        wsum = sb("wsum", [P, 2, PAST + N], scope=A)
        xa_s = sb("xa_s", [P, NPOOL, SEQS, PAST + STEPS], scope=A)
        u_s = sb("u_s", [P, NCONV, SEQS, HIST + STEPS], scope=A)
        su_s = sb("su_s", [P, NSC, SEQS, SHIST + STEPS], scope=A)
        w_pl = sb("w_pl", [P, NPOOL, P], scope=A)
        A.close()
        ones = con_a[:, E_ONES:E_ONES + P]
        B = ExitStack()
        g_hi = sb("g_hi", [P, NF, N], F32R, scope=B)
        g_lo = sb("g_lo", [P, NF, N], F32R, scope=B)
        s_buf = sb("s_buf", [P, 2, N], scope=B)
        g_f = sb("g_f", [P, 2, N], scope=B)
        raw5 = sb("raw5", [P, D], scope=B)
        whi5 = sb("whi5", [P, D], F32R, scope=B)
        wlo5 = sb("wlo5", [P, D], F32R, scope=B)
        B.close()
        dn_raw = [raw[:, 4, :], raw5[:, :]]
        dn_whi = [whi[:, 4, :], whi5[:, :]]
        dn_wlo = [wlo[:, 4, :], wlo5[:, :]]

        def chan(ap):
            return ap.rearrange("p (k m) -> p k m", k=KD)

        def pslot(kind, j):
            return pr[:, SLOT[kind] + j, :]

        def y_src(c):
            if c < NPOOL:
                return pslot("g", c)
            return pslot("a", c - NPOOL) if c < NPOOL + NCONV else pslot("h", c - NPOOL - NCONV)

        def mix_ps(t):
            return ps[:, 2 + 2 * t:4 + 2 * t, :].rearrange("p a n -> p (a n)")

        def is_last(b):
            return isinstance(b, int) and b == NB - 1

        def norm_group(q, k):
            if isinstance(q, int) and q == 0:
                return k
            if isinstance(q, int) and q < NB:
                return group(q - 1, f"t{k}")
            return WORK_A + KD * (q - NB) + k

        def norm_full(q, k):
            if isinstance(q, int) and q == 0:
                return k + 1
            if isinstance(q, int) and q < NB:
                return full_count(q - 1, f"t{k}")
            return FULL_A + KD * (q - NB) + k + 1

        block = ctx.enter_context(nc.Block())

        @block.sync
        def _(sp):
            sp.dma_start(c_sb[:, :, :], c_all).then_inc(c_landed, 16)
            for i in range(ADA_RING):
                sp.dma_start(raw[:, i, :], w_ada[i]).then_inc(ada_landed[i], 16)
            sp.dma_start(con[:, :], consts).then_inc(const_landed, 16)
            sp.dma_start(con_a[:, :], consts_a).then_inc(const_landed, 16)
            sp.dma_start(col[:, :], cols).then_inc(const_landed, 16)
            sp.dma_start(mod[2 * ROWS:MOD_K, :], b_ada).then_inc(bias_landed, 16)
            for i in range(2):
                sp.dma_start(gp[:, i, :], gpost[i:i + 1, :].to_broadcast([P, D])).then_inc(gpost_landed, 16)
            sp.dma_start(xt[:, :, :], x_v[:, 0:TB, :]).then_inc(x_landed, 16)
            with sp.Fori(1, NADA // ADA_RING) as r:
                for i in range(ADA_RING):
                    sp.wait_ge(ada_lo, r * ADA_RING + (i + 1 - ADA_RING))
                    sp.dma_start(raw[:, i, :], w_ada[r * ADA_RING + i]).then_inc(ada_landed[i], 16)

            def load_w(n, s, row):
                if not isinstance(n, int) or n >= RING:
                    sp.wait_ge(w_lo, n - RING + 1)
                sp.dma_start(raw[:, s, :], w_mix[row]).then_inc(w_landed[s], 16)

            for j in range(RING):
                if j < ADA_RING:
                    sp.wait_ge(ada_lo, NADA - ADA_RING + j + 1)
                load_w(j, slot_in(j, True), j)
            sp.wait_ge(mod_ready, 8)
            sp.wait_ge(w_pool_zeroed, 1)
            for g in range(len(WINDOWS)):
                h = 64 * (g % 2)
                sp.dma_start(w_pl[h:h + 64, g // 2, h:h + 64], w_pool[g]).then_inc(state_landed, 16)
            for c in range(NPOOL):
                sp.dma_start(xa_s[:, c, :, 0:PAST], st_pool[:, c]).then_inc(state_landed, 16)
            for j in range(NCONV):
                sp.dma_start(u_s[:, j, :, 0:HIST], st_conv[:, j]).then_inc(state_landed, 16)
            for j in range(NSC):
                sp.dma_start(su_s[:, j, :, 0:SHIST], st_sconv[:, j]).then_inc(state_landed, 16)
            for j in range(RING, NIN):
                load_w(j, slot_in(j, True), j)
                if j == 8:
                    sp.wait_ge(work_full, KD)
                    sp.dma_start(xt[:, :, :], x_v[:, TB:2 * TB, :]).then_inc(x_landed, 16)
            AHEAD = 8
            for j in range(AHEAD):
                load_w(unit_in(1, j), slot_in(j), j)

            def mixer_loads(b, nt_next):
                for j in range(AHEAD, UNITS):
                    if j < NIN:
                        load_w(unit_in(b, j), slot_in(j), j)
                    else:
                        load_w(unit_out(b - 1, j - NIN), slot_out(j - NIN), j)
                    if j == 10:
                        if nt_next:
                            sp.wait_ge(work_full, full_count(b - 1, "t7"))
                            sp.dma_start(xt[:, 0:nt_next, :], x_v[:, bass.ds(TB * b + TB, nt_next), :])\
                              .then_inc(x_landed, 16)
                        else:
                            sp.wait_ge(work_full, full_count(b - 2, "t7"))
                            sp.wait_ge(stored, 16)
                            sp.dma_start(xt[:, :, :], x1_v[:, 0:TB, :]).then_inc(x_landed, 16)
                    if j == 12:
                        if not (isinstance(b, int) and b == 1):
                            sp.wait_ge(stored, 16 * (b - 1))
                        sp.dma_start(xr[:, :, :], x_v[:, bass.ds(TB * b - TB, TB), :]).then_inc(res_landed, 16)
                for j in range(NMIX if is_last(b) else AHEAD):
                    if is_last(b):
                        load_w(unit_out(b, j), slot_out(j, True), NIN + j)
                    else:
                        load_w(unit_in(b + 1, j), slot_in(j), j)
                sp.wait_ge(res_ready, b)
                sp.dma_start(x1_v[:, bass.ds(TB * b - TB, TB), :], xr[:, :, :]).then_inc(stored, 16)

            mixer_loads(1, TB)
            with sp.Fori(2, NB - 2) as b:
                mixer_loads(b, TB)
            mixer_loads(NB - 2, LAST_TB)
            mixer_loads(NB - 1, 0)

            last_n = LAST_TB * P
            sp.wait_ge(y_lo_ready, NMIX * NB)
            for c in range(NPOOL):
                sp.dma_start(o_pool_p[:, c], xa[:, c, last_n:last_n + PAST]).then_inc(states_stored, 16)
                sp.dma_start(o_pool_s[:, c], xa_s[:, c, :, STEPS:]).then_inc(states_stored, 16)
            for j in range(NCONV):
                sp.dma_start(o_conv_p[:, j], u[:, j, last_n:last_n + HIST]).then_inc(states_stored, 16)
                sp.dma_start(o_conv_s[:, j], u_s[:, j, :, STEPS:]).then_inc(states_stored, 16)
            for j in range(NSC):
                sp.dma_start(o_sconv_p[:, j], su[:, j, last_n:last_n + SHIST]).then_inc(states_stored, 16)
                sp.dma_start(o_sconv_s[:, j], su_s[:, j, :, STEPS:]).then_inc(states_stored, 16)

            sp.wait_ge(stored, 16 * (NB - 1))
            sp.dma_start(xr[:, 0:LAST_TB, :], x_v[:, TB * (NB - 1):TILES, :]).then_inc(res_landed, 16)
            for i in range(4):
                sp.wait_ge(w_lo, UNITS * NB - 5 + i + 1)
                sp.dma_start(raw[:, i, :], w_gu[i]).then_inc(gu_landed[i], 16)
            sp.wait_ge(w_lo, UNITS * NB)

            def load_gu(b, m, par):
                sp.wait_ge(gate_lo, NF * b + m - 1)
                sp.dma_start(raw[:, 2 * par, :], w_gu[2 * m]).then_inc(gu_landed[2 * par], 16)
                sp.wait_ge(up_lo, NF * b + m - 1)
                sp.dma_start(raw[:, 2 * par + 1, :], w_gu[2 * m + 1]).then_inc(gu_landed[2 * par + 1], 16)

            def load_dn(b, k):
                if not (isinstance(b, int) and b == 0 and k < 2):
                    sp.wait_ge(dn_lo, NF * b + (k - 1))
                sp.dma_start(dn_raw[k % 2], w_dn[k]).then_inc(dn_landed[k % 2], 16)

            def ffn_loads(b, nt_next):
                nt_prev = LAST_TB if isinstance(b, int) and b == 0 else TB
                nt = tiles_of(b)
                with sp.Fori(1, NF // 4 + 1) as i:
                    for par in range(2):
                        load_gu(b, 2 * i + par, par)
                sp.wait_ge(res_ready, NB + b)
                if isinstance(b, int) and b == 0:
                    sp.dma_start(x1_v[:, TB * (NB - 1):TILES, :], xr[:, 0:LAST_TB, :]).then_inc(stored, 16)
                    sp.wait_ge(states_stored, 16 * 2 * NMIX)
                    sp.wait_ge(w_used, UNITS * NB)
                else:
                    sp.dma_start(y_v[:, bass.ds(TB * b - TB, TB), :], xr[:, :, :]).then_inc(stored, 16)
                load_dn(b, 0)
                load_dn(b, 1)
                with sp.Fori(NF // 4 + 1, NF // 2) as i:
                    for par in range(2):
                        load_gu(b, 2 * i + par, par)
                sp.wait_ge(stored, 16 * NB + 16 * b)
                sp.dma_start(xr[:, 0:nt, :], x1_v[:, bass.ds(TB * b, nt), :]).then_inc(res_landed, 16)
                if nt_next:
                    sp.wait_ge(work_full, norm_full(NB + b, KD - 1))
                    sp.dma_start(xt[:, 0:nt_next, :], x1_v[:, bass.ds(TB * b + TB, nt_next), :])\
                      .then_inc(x_landed, 16)
                for k in range(2, NF):
                    load_dn(b, k)
                    if k == 9 and nt_next:
                        for i in range(4):
                            sp.wait_ge(up_lo if i % 2 else gate_lo, NF * b + NF - 1 + i // 2)
                            sp.dma_start(raw[:, i, :], w_gu[i]).then_inc(gu_landed[i], 16)

            ffn_loads(0, TB)
            with sp.Fori(1, NB - 2) as b:
                ffn_loads(b, TB)
            ffn_loads(NB - 2, LAST_TB)
            ffn_loads(NB - 1, 0)
            sp.wait_ge(res_ready, 2 * NB)
            sp.dma_start(y_v[:, TB * (NB - 1):TILES, :], xr[:, 0:LAST_TB, :]).then_inc(stored, 16)
            sp.wait_ge(stored, 16 * 2 * NB)

        @block.tensor
        def _(pe):
            def mm(out, lhsT, rhs, start, stop):
                return nc.tensor.matmul(out, lhsT, rhs, start=start, stop=stop, skip_group_check=True)

            pe.wait_ge(c_ready, 2)
            with pe.Fori(0, 6) as g:
                for k in range(KD):
                    pe.wait_ge(ada_lo, g * KD + (k + 1))
                    s = k % ADA_RING
                    for h in range(2):
                        w = slice(512 * h, 512 * h + 512)
                        mm(ps[:, 2 + h, :], c_hl[:, k, :], whi[:, s, w], k == 0, False)
                        last = mm(ps[:, 2 + h, :], c_h0[:, k, :], wlo[:, s, w], False, k == KD - 1)
                    last.then_inc(ada_used, 1)
                pe.wait_ge(ada_read, g + 1)
            pe.wait_ge(bias_landed, 16)
            pe.wait_ge(const_landed, 48)
            for i, g in enumerate((0, 1, 3, 4)):
                for k in range(KD):
                    c0 = g * D + k * P
                    last = mm(ps[:, 0, (i * KD + k) * ROWS:(i * KD + k + 1) * ROWS], mod[:, c0:c0 + P],
                              con_a[0:MOD_K, E_SELF:E_SELF + ROWS], True, True)
            last.then_inc(cols_full, 1)
            for i, (g, e) in enumerate(((2, E_SELP), (2, E_SELS), (5, E_SELP), (5, E_SELS))):
                if i == 3:
                    pe.wait_ge(mod_ready, 5)
                for h in range(2):
                    c0 = g * D + 512 * h
                    last = mm(ps[:, 2 + 2 * (i % 3) + h, :], con_a[0:MOD_K, e:e + P], mod[:, c0:c0 + 512], True, True)
                last.then_inc(gates_full, 1)

            def transposes(q, k, nt, bank, wait):
                if k == 0:
                    pe.wait_ge(xn_ready, q + 1)
                if wait is not None:
                    pe.wait_ge(work_read, wait)
                for t in range(nt):
                    last = nc.tensor.transpose(ps[:, bank, t * P:(t + 1) * P], xt[:, t, k * P:(k + 1) * P], ident)
                last.then_inc(work_full, 1)

            pe.wait_ge(mod_ready, 4)
            for k in range(KD):
                transposes(0, k, TB, k % 2, k - 1 if k >= 2 else None)

            def project(b, j, nt):
                n, s = unit_in(b, j), slot_in(j, isinstance(b, int) and b == 0)
                g = group(b, j)
                pe.wait_ge(work_read, g if j == 0 else g - 1)
                pe.wait_ge(w_lo, n + 1)
                if j == 0:
                    pe.wait_ge(h_lo_ready, KD * (b + 1))
                w_h, w_l = chan(whi[:, s, :]), chan(wlo[:, s, :])
                out = ps[:, bank_of(j), 0:nt * P]
                for k in range(KD):
                    mm(out, w_h[:, k, :], h_hi[:, k, 0:nt * P], k == 0, False)
                    mm(out, w_h[:, k, :], h_lo[:, k, 0:nt * P], False, False)
                    last = mm(out, w_l[:, k, :], h_hi[:, k, 0:nt * P], False, k == KD - 1)
                last.then_inc(w_used, 1)

            def token_major(a_hi, a_lo, b_hi, b_lo, k, nk, nt):
                for t in range(nt):
                    c = slice(t * P, (t + 1) * P)
                    for st, mv, first, end in ((a_hi, b_hi, k == 0, False), (a_hi, b_lo, False, False),
                                               (a_lo, b_hi, False, k == nk - 1)):
                        for h in range(2):
                            w = slice(512 * h, 512 * h + 512)
                            last = mm(ps[:, 2 + 2 * t + h, :], st[:, k, c], mv[:, w], first, end)
                return last

            def mix_out(b, k, nt):
                n, s = unit_out(b, k), slot_out(k, is_last(b))
                if k == 0:
                    pe.wait_ge(y_lo_ready, NMIX * (b + 1))
                    if not (isinstance(b, int) and b == 0):
                        pe.wait_ge(res_ready, b)
                    else:
                        pe.wait_ge(mod_ready, 8)
                pe.wait_ge(w_lo, n + 1)
                token_major(y_hi, y_lo, whi[:, s, :], wlo[:, s, :], k, NMIX, nt).then_inc(w_used, 1)

            def stage_group(b, name, nt, nt_next):
                g = group(b, name)
                bank = bank_of(g - group(b, 0)) if isinstance(b, int) else \
                    bank_of(NIN + STAGE.index(name))
                out = ps[:, bank, 0:nt * P]
                if name[0] == "t":
                    transposes(b + 1, int(name[1]), nt_next, bank, g - 1)
                    return
                pe.wait_ge(work_read, g - 1)
                if name == "mean":
                    pe.wait_ge(z_ready, NCONV * (b + 1))
                    for j in range(NCONV):
                        last = mm(out, ones, pslot("a", j)[:, 0:nt * P], j == 0, j == NCONV - 1)
                elif name == "var":
                    pe.wait_ge(zsq_ready, NCONV * (b + 1))
                    for j in range(NCONV):
                        last = mm(out, ones, pslot("c", j)[:, 0:nt * P], j == 0, j == NCONV - 1)
                else:
                    c = int(name[-1])
                    pe.wait_ge(pooled_ready, NPOOL * b + (c + 1))
                    last = mm(out, w_pl[:, c, :], pslot("g", c)[:, 0:nt * P], True, True)
                last.then_inc(work_full, 1)

            def mixer_block(b, nt_next, before):
                nt = tiles_of(b)
                for j in range(NIN):
                    project(b, j, nt)
                names = STAGE if nt_next else STAGE_LAST
                after = {0: ["t0"], 1: ["t1"], 2: ["t2"], 3: ["t3", "mean"], 4: ["t4"],
                         5: ["t5", "pool0", "pool1"], 6: ["t6", "var"], 7: ["t7"]}
                for k in range(NMIX):
                    if before:
                        mix_out(b - 1, k, TB)
                    for name in after[k]:
                        if name in names:
                            stage_group(b, name, nt, nt_next)

            pe.wait_ge(state_landed, 16 * (len(WINDOWS) + NMIX))
            mixer_block(0, TB, False)
            with pe.Fori(1, NB - 2) as b:
                mixer_block(b, TB, True)
            mixer_block(NB - 2, LAST_TB, True)
            mixer_block(NB - 1, 0, True)
            for k in range(NMIX):
                mix_out(NB - 1, k, LAST_TB)
                transposes(NB, k, TB, k % 2, WORK_A + k - 1)

            def gate_up(b, m, par, nt):
                for i in range(2):
                    s = 2 * par + i
                    pe.wait_ge(gate_lo if i == 0 else up_lo, NF * b + m + 1)
                    w_h, w_l = chan(whi[:, s, :]), chan(wlo[:, s, :])
                    out = ps[:, s, 0:nt * P]
                    for k in range(KD):
                        mm(out, w_h[:, k, :], h_hi[:, k, 0:nt * P], k == 0, False)
                        mm(out, w_h[:, k, :], h_lo[:, k, 0:nt * P], False, False)
                        last = mm(out, w_l[:, k, :], h_hi[:, k, 0:nt * P], False, k == KD - 1)
                    last.then_inc(gu_used, 1)

            def ffn_block(b, nt_next):
                nt = tiles_of(b)
                pe.wait_ge(h_lo_ready, KD * NB + KD * (b + 1))
                pe.wait_ge(work_read, norm_group(NB + b, KD - 1) + 1)
                gate_up(b, 0, 0, nt)
                pe.wait_ge(res_first, NB + b)
                gate_up(b, 1, 1, nt)
                with pe.Fori(1, NF // 2) as i:
                    for par in range(2):
                        pe.wait_ge(silu_ready, NF * b + 2 * i + par - 1)
                        pe.wait_ge(g_ready, NF * b + 2 * i + par - 1)
                        gate_up(b, 2 * i + par, par, nt)
                pe.wait_ge(silu_ready, NF * b + NF)
                pe.wait_ge(g_ready, NF * b + NF)
                pe.wait_ge(res_ready, NB + b)
                for k in range(NF):
                    pe.wait_ge(dn_lo, NF * b + k + 1)
                    pe.wait_ge(g_lo_ready, NF * b + k + 1)
                    token_major(g_hi, g_lo, dn_whi[k % 2], dn_wlo[k % 2], k, NF, nt).then_inc(dn_used, 1)
                    c = (k - 3) // 2
                    if nt_next and k % 2 and 0 <= c < KD:
                        q = NB + 1 + b
                        transposes(q, c, nt_next, c % 2, None if c < 2 else norm_group(q, c) - 1)

            ffn_block(0, TB)
            with pe.Fori(1, NB - 2) as b:
                ffn_block(b, TB)
            ffn_block(NB - 2, LAST_TB)
            ffn_block(NB - 1, 0)

        @block.scalar
        def _(act):
            own = Steps(act_step)

            act.wait_ge(c_landed, 16)
            nc.scalar.activation(c_s[:, :, :], c_sb[:, :, :], ACT.Silu).then_inc(silu_c, 1)
            act.wait_ge(silu_c, 1)
            act.wait_ge(pad_zeroed, 2)
            nc.scalar.activation(c_hl[:, :, 0:ROWS], c_s[:, :, :], ACT.Copy).then_inc(c_hi_ready, 1)

            def ada_group(g, first):
                for k in range(KD):
                    s = k % ADA_RING
                    act.wait_ge(ada_landed[s], 32 * g + 16 * (k // ADA_RING + 1))
                    if not first or k >= ADA_RING:
                        act.wait_ge(ada_used, KD * g + (k - ADA_RING + 1))
                    nc.scalar.activation(whi[:, s, :], raw[:, s, :], ACT.Copy).then_inc(ada_hi, 1)
                act.wait_ge(ada_used, KD * g + KD)
                nc.scalar.activation(mod[0:2 * ROWS, bass.ds(g * D, D)],
                                     mix_ps(0)[0:2 * ROWS, :], ACT.Copy).then_inc(ada_read, 1)

            ada_group(0, True)
            with act.Fori(1, 6) as g:
                ada_group(g, False)

            def split_unit(b, j):
                if isinstance(b, int) and b == 0:
                    n, s, landed = j, j % RING, 16 * (j // RING + 1)
                elif isinstance(b, int) and b == NB:
                    n = unit_out(NB - 1, j)
                    s, landed = n % RING, 16 * (n // RING + 1)
                else:
                    n = UNITS * b - NMIX + j
                    s = (j - NMIX) % RING
                    landed = 16 * (UNITS // RING) * b + 16 * ((j - NMIX) // RING + 1)
                act.wait_ge(w_landed[s], landed)
                if isinstance(n, int) and n < RING:
                    if s < ADA_RING:
                        act.wait_ge(ada_used, NADA - ADA_RING + s + 1)
                else:
                    act.wait_ge(w_used, n - RING + 1)
                nc.scalar.activation(whi[:, s, :], raw[:, s, :], ACT.Copy).then_inc(w_hi, 1)

            LEAD = RING - 1

            def split_ahead(b, j):
                units = NIN if isinstance(b, int) and b == 0 else UNITS
                if j + LEAD < units:
                    split_unit(b, j + LEAD)
                elif is_last(b):
                    split_unit(NB, j + LEAD - units)
                else:
                    split_unit(b + 1, j + LEAD - units)

            def mean_squares(src, dst, nt, done):
                for t in range(nt):
                    i = nc.scalar.activation(junk[:, :], src(t), ACT.Square, scale=D ** -0.5,
                                             accum_out=dst[:, t:t + 1])
                    if t == nt - 1:
                        i.then_inc(done, 1)
                    else:
                        act.wait_ge(act_step, own.step(i))

            def x_squares(q, nt):
                act.wait_ge(x_landed, 16 * (q + 1))
                mean_squares(lambda t: xt[:, t, :], ssq_x, nt, x_ssq)

            def mix_squares(nt):
                mean_squares(mix_ps, ssq_m, nt, mix_ssq)

            def modulate(q, k, nt, bank, ph, sample):
                act.wait_ge(work_full, norm_full(q, k) if isinstance(q, int) else full_of_loop[0](k))
                if k >= 2 or not (isinstance(q, int) and q == 0):
                    act.wait_ge(h_lo_ready, KD * q + (k - 1))
                c = P if sample else 0
                if sample:
                    act.wait_ge(sample_mod, KD * (q // NB) + k + 1)
                nc.scalar.activation(h_f[:, k % 2, c:nt * P], ps[:, bank, c:nt * P], ACT.Identity,
                                     scale=shsc[:, 2 * ph + 1, k, 0:1], bias=shsc[:, 2 * ph, k, 0:1])\
                  .then_inc(work_read, 1)

            full_of_loop = [None]

            def h_split(q, k, nt, read):
                act.wait_ge(work_read, read)
                nc.scalar.activation(h_hi[:, k, 0:nt * P], h_f[:, k % 2, 0:nt * P], ACT.Copy).then_inc(h_hi_ready, 1)

            x_squares(0, TB)
            for j in range(LEAD):
                split_unit(0, j)
            act.wait_ge(mod_ready, 4)
            for k in range(KD):
                modulate(0, k, TB, k % 2, 0, True)
                h_split(0, k, TB, k + 1)

            def evacuate(b, j, nt):
                kind, c = ORDER[j]
                act.wait_ge(w_used, unit_in(b, j) + 1)
                src = ps[:, bank_of(j), 0:nt * P]
                if kind != "x":
                    f = ACT.Sigmoid if kind == "g" else ACT.Copy
                    nc.scalar.activation(pslot(kind, c)[:, 0:nt * P], src, f).then_inc(work_read, 1)
                    return
                if isinstance(b, int) and b == 0:
                    own.step(nc.scalar.activation(
                        xa_s[:, c, :, PAST:], src[:, 0:P].rearrange("p (s t) -> p s t", s=SEQS), ACT.Copy))
                    nc.scalar.activation(xa[:, c, PAST:PAST + (nt - 1) * P], src[:, P:], ACT.Copy).then_inc(work_read, 1)
                else:
                    nc.scalar.activation(xa[:, c, PAST:PAST + nt * P], src, ACT.Copy).then_inc(work_read, 1)

            def stage_group(b, name, nt, nt_next, split=None):
                g = group(b, name)
                at = (STAGE_LAST if is_last(b) else STAGE).index(name)
                bank = bank_of(NIN + at)
                src = ps[:, bank, 0:nt * P]
                full_of_loop[0] = lambda k: full_count(b, f"t{k}")
                if name[0] == "t":
                    k = int(name[1])
                    if k == 0:
                        act.wait_ge(w_used, unit_in(b, NIN - 1) + 1)
                    act.wait_ge(work_full, full_count(b, name))
                    act.wait_ge(h_lo_ready, KD * (b + 1) + (k - 1))
                    nc.scalar.activation(h_f[:, k % 2, 0:nt_next * P], ps[:, bank, 0:nt_next * P], ACT.Identity,
                                         scale=shsc[:, 1, k, 0:1], bias=shsc[:, 0, k, 0:1]).then_inc(work_read, 1)
                    if split is not None:
                        split()
                    h_split(b + 1, k, nt_next, g + 1)
                    return
                act.wait_ge(work_full, full_count(b, name))
                if name == "mean":
                    nc.scalar.activation(pslot("g", 2)[:, 0:nt * P], src, ACT.Copy, scale=1.0 / (NCONV * P))\
                      .then_inc(work_read, 1)
                elif name == "var":
                    lnv, v = pslot("b", 0)[:, 0:nt * P], pslot("b", 1)[:, 0:nt * P]
                    at_ln = own.step(nc.scalar.activation(lnv, src, ACT.Ln, scale=1.0 / (NCONV * P), bias=eps))
                    nc.scalar.activation(v, src, ACT.Identity, scale=1.0 / (NCONV * P), bias=eps)\
                      .then_inc(work_read, 1)
                    act.wait_ge(act_step, at_ln)
                    nc.scalar.activation(lnv, lnv, ACT.Exp, scale=-0.5).then_inc(seed_ready, 1)
                else:
                    c = int(name[-1])
                    nc.scalar.activation(pslot("g", c)[:, 0:nt * P], src, ACT.Copy,
                                         scale=col[:, Q_SP + c:Q_SP + c + 1]).then_inc(work_read, 1)

            def mixer_block(b, nt_next, before):
                nt = tiles_of(b)
                first = isinstance(b, int) and b == 0
                if first:
                    act.wait_ge(mod_ready, 8)
                else:
                    act.wait_ge(y_lo_ready, NMIX * b)
                for j in range(NIN):
                    split_ahead(b, j)
                    evacuate(b, j, nt)
                    if j == 9 and (nt_next or is_last(b)):
                        x_squares(b + 1, nt_next or TB)
                names = STAGE if nt_next else STAGE_LAST
                after = {0: ["t0"], 1: ["t1"], 2: ["t2"], 3: ["t3", "mean"], 4: ["t4", "zsq"],
                         5: ["t5", "pool0", "pool1"], 6: ["t6", "var"], 7: ["t7"]}
                for k in range(NMIX):
                    ahead = (lambda k=k: split_ahead(b, NIN + k)) if before else None
                    for name in after[k]:
                        if name in names:
                            t = name[0] == "t"
                            stage_group(b, name, nt, nt_next, ahead if t else None)
                            if t:
                                ahead = None
                        elif name == "zsq":
                            for j in range(NCONV):
                                act.wait_ge(zc_ready, NCONV * b + (j + 1))
                                nc.scalar.activation(pslot("c", j)[:, 0:nt * P], pslot("a", j)[:, 0:nt * P],
                                                     ACT.Square).then_inc(zsq_ready, 1)
                    if ahead is not None:
                        ahead()
                for j in range(NCONV):
                    act.wait_ge(zn_ready, NCONV * b + (j + 1))
                    nc.scalar.activation(pslot("a", j)[:, 0:nt * P], pslot("a", j)[:, 0:nt * P], ACT.Silu,
                                         scale=col[:, Q_LG + j:Q_LG + j + 1],
                                         bias=col[:, Q_LB + j:Q_LB + j + 1]).then_inc(yb_ready, 1)
                if before:
                    act.wait_ge(w_used, unit_out(b - 1, NMIX - 1) + 1)
                    mix_squares(TB)
                act.wait_ge(yb_ready, NCONV * (b + 1))
                act.wait_ge(yc_ready, NSC * (b + 1))
                act.wait_ge(work_read, group(b, "pool1") + 1)
                for c in range(NMIX):
                    nc.scalar.activation(y_hi[:, c, 0:nt * P], y_src(c)[:, 0:nt * P], ACT.Copy).then_inc(y_hi_ready, 1)

            mixer_block(0, TB, False)
            own.enter_loop()
            with act.Fori(1, NB - 2) as b:
                own.in_loop(b - 1, ACT_STEPS)
                mixer_block(b, TB, True)
            own.leave_loop(NB - 3, ACT_STEPS)
            mixer_block(NB - 2, LAST_TB, True)
            mixer_block(NB - 1, 0, True)
            for k in range(NMIX):
                if k == 0:
                    act.wait_ge(w_used, unit_in(NB - 1, NIN - 1) + 1)
                modulate(NB, k, TB, k % 2, 1, True)
                if k + LEAD < NMIX:
                    split_unit(NB, k + LEAD)
                h_split(NB, k, TB, WORK_A + k + 1)

            def split_dn(b, k):
                act.wait_ge(dn_landed[k % 2], 16 * (NF // 2) * b + 16 * (k // 2 + 1))
                if not (isinstance(b, int) and b == 0 and k < 2):
                    act.wait_ge(dn_used, NF * b + (k - 1))
                elif k == 0:
                    act.wait_ge(w_used, UNITS * NB)
                nc.scalar.activation(dn_whi[k % 2], dn_raw[k % 2], ACT.Copy).then_inc(dn_hi, 1)

            def hidden(b, m, par, nt, split):
                act.wait_ge(gu_used, 2 * NF * b + 2 * m + 1)
                nc.scalar.activation(s_buf[:, par, 0:nt * P], ps[:, 2 * par, 0:nt * P], ACT.Silu).then_inc(silu_ready, 1)
                split()
                act.wait_ge(g_ready, NF * b + m + 1)
                nc.scalar.activation(g_hi[:, bass.ds(m, 1), 0:nt * P].rearrange("p a n -> p (a n)"),
                                     g_f[:, par, 0:nt * P], ACT.Copy).then_inc(g_hi_ready, 1)

            def ffn_block(b, nt_next):
                nt = tiles_of(b)
                mix_nt = LAST_TB if isinstance(b, int) and b == 0 else TB

                def split_two_on(m, par, i_times=None):
                    count = 16 * (NF // 2) * b + (i_times + 32 if i_times is not None else 16 * (m // 2) + 32)
                    act.wait_ge(gu_landed[2 * par], count)
                    nc.scalar.activation(whi[:, 2 * par, :], raw[:, 2 * par, :], ACT.Copy).then_inc(gu_hi, 1)
                    act.wait_ge(gu_used, 2 * NF * b + 2 * m + 2)
                    act.wait_ge(gu_landed[2 * par + 1], count)
                    nc.scalar.activation(whi[:, 2 * par + 1, :], raw[:, 2 * par + 1, :], ACT.Copy).then_inc(gu_hi, 1)

                with act.Fori(0, NF // 2 - 1) as i:
                    for par in range(2):
                        hidden(b, 2 * i + par, par, nt, lambda: split_two_on(2 * i + par, par, 16 * i))
                for par in range(2):
                    hidden(b, NF - 2 + par, par, nt, lambda: split_dn(b, par))
                if nt_next:
                    x_squares(NB + 1 + b, nt_next)
                for k in range(NF):
                    if k + 2 < NF:
                        split_dn(b, k + 2)
                    c = (k - 3) // 2
                    if nt_next and k % 2 and 0 <= c < KD:
                        q = NB + 1 + b
                        if c == 0:
                            act.wait_ge(gu_used, 2 * NF * b + 2 * NF)
                        act.wait_ge(work_full, FULL_A + KD * (b + 1) + (c + 1))
                        act.wait_ge(h_lo_ready, KD * q + (c - 1))
                        nc.scalar.activation(h_f[:, c % 2, 0:nt_next * P], ps[:, c % 2, 0:nt_next * P], ACT.Identity,
                                             scale=shsc[:, 3, c, 0:1], bias=shsc[:, 2, c, 0:1]).then_inc(work_read, 1)
                    if nt_next and k % 2 == 0 and 0 <= (k - 4) // 2 < KD and k >= 4:
                        c = (k - 4) // 2
                        h_split(NB + 1 + b, c, nt_next, WORK_A + KD * (b + 1) + c + 1)
                    if nt_next and k >= NF - 4:
                        s = k - (NF - 4)
                        act.wait_ge(gu_landed[s], 16 * (NF // 2) * (b + 1) + 16)
                        nc.scalar.activation(whi[:, s, :], raw[:, s, :], ACT.Copy).then_inc(gu_hi, 1)
                act.wait_ge(dn_used, NF * (b + 1))
                mix_squares(nt)

            for s in range(4):
                act.wait_ge(gu_landed[s], 16)
                act.wait_ge(w_used, UNITS * NB - RING + s + 1)
                nc.scalar.activation(whi[:, s, :], raw[:, s, :], ACT.Copy).then_inc(gu_hi, 1)
            act.wait_ge(w_used, UNITS * NB)
            mix_squares(LAST_TB)
            act.wait_ge(states_stored, 16 * 2 * NMIX)
            ffn_block(0, TB)
            own.enter_loop()
            with act.Fori(1, NB - 2) as b:
                own.in_loop(b - 1, ACT_STEPS_B)
                ffn_block(b, TB)
            own.leave_loop(NB - 3, ACT_STEPS_B)
            ffn_block(NB - 2, LAST_TB)
            ffn_block(NB - 1, 0)

        @block.gpsimd
        def _(pool):
            nc.gpsimd.memset(c_hl[:, :, :].bitcast(F32), 0.0).then_inc(pad_zeroed, 1)
            nc.gpsimd.memset(c_h0[:, :, :].bitcast(F32), 0.0).then_inc(pad_zeroed, 1)
            steps = Steps(pool_step)

            def rstd(ssq, out, nt, done):
                at = steps.step(nc.gpsimd.tensor_tensor(ssq[:, 0:nt], ssq[:, 0:nt], con[:, C_EPS:C_EPS + nt], ALU.add))
                pool.wait_ge(pool_step, at)
                nc.gpsimd.tensor_tensor(out[:, 0:nt], ssq[:, 0:nt], con[:, C_NHALF:C_NHALF + nt], ALU.pow)\
                  .then_inc(done, 1)

            def lo(n, s):
                pool.wait_ge(w_hi, n + 1)
                nc.gpsimd.tensor_tensor(wlo[:, s, :], raw[:, s, :], whi[:, s, :].bitcast(F32), ALU.subtract)\
                  .then_inc(w_lo, 1)

            pool.wait_ge(const_landed, 48)
            pool.wait_ge(x_ssq, 1)
            rstd(ssq_x, rstd_x, TB, x_rstd)
            for j in range(4):
                lo(j, j)
            pool.wait_ge(mod_ready, 8)
            nc.gpsimd.memset(w_pl[:, :, :], 0.0).then_inc(w_pool_zeroed, 1)
            LEAD = RING - 1
            for j in range(LEAD, NIN + LEAD):
                lo(j, j % RING)
                if j == 9 + LEAD:
                    pool.wait_ge(x_ssq, 2)
                    rstd(ssq_x, rstd_x, TB, x_rstd)

            def mixer_block(b, nt_next):
                for j in range(LEAD, UNITS + LEAD):
                    if is_last(b) and j >= UNITS + NMIX:
                        break
                    lo(UNITS * b - NMIX + j, (j - NMIX) % RING)
                    if j == 9 + LEAD:
                        pool.wait_ge(x_ssq, b + 2)
                        rstd(ssq_x, rstd_x, nt_next or TB, x_rstd)
                pool.wait_ge(mix_ssq, b)
                rstd(ssq_m, rstd_m, TB, mix_rstd)

            steps.enter_loop()
            with pool.Fori(1, NB - 2) as b:
                steps.in_loop(b - 1, POOL_STEPS)
                mixer_block(b, TB)
            steps.leave_loop(NB - 3, POOL_STEPS)
            mixer_block(NB - 2, LAST_TB)
            mixer_block(NB - 1, 0)
            for k in range(LEAD, NMIX):
                lo(unit_out(NB - 1, k), slot_out(k, True))

            def lo_gate(b, m, par):
                pool.wait_ge(gu_hi, 2 * NF * b + 2 * m + 1)
                nc.gpsimd.tensor_tensor(wlo[:, 2 * par, :], raw[:, 2 * par, :], whi[:, 2 * par, :].bitcast(F32),
                                        ALU.subtract).then_inc(gate_lo, 1)

            def ffn_block(b, nt_next):
                with pool.Fori(1, NF // 2) as i:
                    for par in range(2):
                        lo_gate(b, 2 * i + par, par)
                if nt_next:
                    pool.wait_ge(x_ssq, NB + b + 2)
                    rstd(ssq_x, rstd_x, nt_next, x_rstd)
                    for par in range(2):
                        lo_gate(b + 1, par, par)
                pool.wait_ge(mix_ssq, NB + b + 1)
                rstd(ssq_m, rstd_m, tiles_of(b), mix_rstd)

            for par in range(2):
                lo_gate(0, par, par)
            pool.wait_ge(mix_ssq, NB)
            rstd(ssq_m, rstd_m, LAST_TB, mix_rstd)
            ffn_block(0, TB)
            steps.enter_loop()
            with pool.Fori(1, NB - 2) as b:
                steps.in_loop(b - 1, 2)
                ffn_block(b, TB)
            steps.leave_loop(NB - 3, 2)
            ffn_block(NB - 2, LAST_TB)
            ffn_block(NB - 1, 0)

        @block.vector
        def _(dve):
            own = Steps(vec_step)

            def after(at):
                if at is not None:
                    dve.wait_ge(vec_step, at)

            tt = nc.vector.tensor_tensor
            stt = nc.vector.scalar_tensor_tensor

            dve.wait_ge(c_hi_ready, 1)
            tt(c_hl[:, :, ROWS:2 * ROWS], c_s[:, :, :], c_hl[:, :, 0:ROWS].bitcast(F32), ALU.subtract)\
                .then_inc(c_ready, 1)
            nc.vector.tensor_copy(c_h0[:, :, 0:ROWS], c_hl[:, :, 0:ROWS].bitcast(F32)).then_inc(c_ready, 1)
            with dve.Fori(0, 6) as g:
                for k in range(KD):
                    s = k % ADA_RING
                    dve.wait_ge(ada_hi, g * KD + (k + 1))
                    tt(wlo[:, s, :], raw[:, s, :], whi[:, s, :].bitcast(F32), ALU.subtract).then_inc(ada_lo, 1)
            dve.wait_ge(cols_full, 1)
            dve.wait_ge(const_landed, 48)
            cols_ps = ps[:, 0, 0:4 * KD * ROWS].rearrange("p (i k r) -> p i k r", i=4, k=KD)
            for i in range(2):
                nc.vector.tensor_copy(shsc[:, 2 * i, :, :], cols_ps[:, 2 * i]).then_inc(mod_ready, 1)
                g0 = (Q_G1, Q_G2)[i]
                stt(shsc[:, 2 * i + 1, :, :], cols_ps[:, 2 * i + 1], 1.0,
                    col[:, g0:g0 + KD].unsqueeze(2).to_broadcast([P, KD, ROWS]), ALU.add, ALU.mult)\
                    .then_inc(mod_ready, 1)
            dve.wait_ge(gpost_landed, 32)
            for i, dst in enumerate((gate1, gate1_first, gate2, gate2_first)):
                dve.wait_ge(gates_full, i + 1)
                tt(dst[:, :], mix_ps(i % 3), gp[:, i // 2, :], ALU.mult).then_inc(mod_ready, 1)

            def normalise(q, nt):
                dve.wait_ge(x_rstd, q + 1)
                for t in range(nt):
                    i = nc.vector.tensor_scalar(xt[:, t, :], xt[:, t, :], rstd_x[:, t:t + 1], None, ALU.mult)
                    if t == nt - 1:
                        i.then_inc(xn_ready, 1)

            def seqs(ap):
                return ap.rearrange("p (s t) -> p s t", s=SEQS)

            def modulate_samples(q, k, full, ph):
                dve.wait_ge(work_full, full)
                if k >= 2 or q:
                    dve.wait_ge(h_hi_ready, KD * q + (k - 1))
                    dve.wait_ge(h_lo_ready, KD * q + (k - 1))
                dst = seqs(h_f[:, k % 2, 0:P])
                at = own.step(tt(dst, seqs(ps[:, k % 2, 0:P]),
                                 shsc[:, 2 * ph + 1, k, 1:ROWS].unsqueeze(2).to_broadcast([P, SEQS, STEPS]), ALU.mult))
                after(at)
                tt(dst, dst, shsc[:, 2 * ph, k, 1:ROWS].unsqueeze(2).to_broadcast([P, SEQS, STEPS]), ALU.add)\
                    .then_inc(sample_mod, 1)

            def h_rest(q, k, nt):
                dve.wait_ge(h_hi_ready, KD * q + (k + 1))
                tt(h_lo[:, k, 0:nt * P], h_f[:, k % 2, 0:nt * P], h_hi[:, k, 0:nt * P].bitcast(F32), ALU.subtract)\
                    .then_inc(h_lo_ready, 1)

            dve.wait_ge(mod_ready, 4)
            normalise(0, TB)
            for k in range(KD):
                modulate_samples(0, k, k + 1, 0)
                if k:
                    h_rest(0, k - 1, TB)
            h_rest(0, KD - 1, TB)
            dve.wait_ge(mod_ready, 8)
            for t_, n_ in ((xa, PAST), (u, HIST), (su, SHIST)):
                nc.vector.memset(t_[:, :, 0:n_], 0.0).then_inc(hist_zeroed, 1)
            dve.wait_ge(hist_zeroed, 3)

            def mixers(b, nt_next, before):
                nt = tiles_of(b)
                first = isinstance(b, int) and b == 0
                c0 = P if first else 0
                np_ = nt * P - c0
                pc = slice(c0, c0 + np_)
                if first:
                    dve.wait_ge(state_landed, 16 * (len(WINDOWS) + NMIX))

                def both(samples, prompt):
                    if first:
                        own.step(samples())
                    return prompt()

                def glu(j):
                    dve.wait_ge(work_read, group(b, 2 * j + 1) + 1)
                    a, g = pslot("a", j), pslot("g", j)
                    return own.step(both(
                        lambda: tt(u_s[:, j, :, HIST:], seqs(a[:, 0:P]), seqs(g[:, 0:P]), ALU.mult),
                        lambda: tt(u[:, j, HIST:HIST + np_], a[:, pc], g[:, pc], ALU.mult)))

                def tap(j, k, at):
                    z = pslot("a", j)
                    w = col[:, Q_WDW + j * TAPS + k:Q_WDW + j * TAPS + k + 1]
                    after(at)
                    if k == 0:
                        bias = col[:, Q_BDW + j:Q_BDW + j + 1]
                        i = both(
                            lambda: nc.vector.tensor_scalar(seqs(z[:, 0:P]), u_s[:, j, :, 0:STEPS], w, bias,
                                                            ALU.mult, ALU.add),
                            lambda: nc.vector.tensor_scalar(z[:, pc], u[:, j, 0:np_], w, bias, ALU.mult, ALU.add))
                    else:
                        i = both(
                            lambda: stt(seqs(z[:, 0:P]), u_s[:, j, :, k:k + STEPS], w, seqs(z[:, 0:P]),
                                        ALU.mult, ALU.add),
                            lambda: stt(z[:, pc], u[:, j, k:k + np_], w, z[:, pc], ALU.mult, ALU.add))
                    if k == TAPS - 1:
                        i.then_inc(z_ready, 1)
                        return None
                    return own.step(i)

                def keep_history(buf, j, n_hist, at):
                    after(at)
                    return own.step(nc.vector.tensor_copy(buf[:, j, 0:n_hist], buf[:, j, np_:np_ + n_hist]))

                at0, at1 = glu(0), glu(1)
                for k in range(TAPS):
                    at0 = tap(0, k, at0)
                    at1 = tap(1, k, at1)
                if nt_next or is_last(b):
                    normalise(b + 1, nt_next or TB)
                at2 = [glu(2), 0]

                def tap2():
                    if at2[1] < TAPS:
                        at2[0] = tap(2, at2[1], at2[0])
                        at2[1] += 1

                def short_conv(j):
                    dve.wait_ge(work_read, group(b, ORDER.index(("b", j))) + 1)
                    h, c, g = pslot("h", j), pslot("c", j), pslot("b", j)
                    at = own.step(both(lambda: tt(su_s[:, j, :, SHIST:], seqs(c[:, 0:P]), seqs(h[:, 0:P]), ALU.mult),
                                       lambda: tt(su[:, j, SHIST:SHIST + np_], c[:, pc], h[:, pc], ALU.mult)))
                    tap2()
                    for k in range(STAPS):
                        w = col[:, Q_WSC + j * STAPS + k:Q_WSC + j * STAPS + k + 1]
                        after(at)
                        if k == 0:
                            at = own.step(both(
                                lambda: nc.vector.tensor_scalar(seqs(c[:, 0:P]), su_s[:, j, :, 0:STEPS], w, None, ALU.mult),
                                lambda: nc.vector.tensor_scalar(c[:, pc], su[:, j, 0:np_], w, None, ALU.mult)))
                        else:
                            at = own.step(both(
                                lambda: stt(seqs(c[:, 0:P]), su_s[:, j, :, k:k + STEPS], w, seqs(c[:, 0:P]),
                                            ALU.mult, ALU.add),
                                lambda: stt(c[:, pc], su[:, j, k:k + np_], w, c[:, pc], ALU.mult, ALU.add)))
                        tap2()
                    after(at)
                    tt(h[:, 0:nt * P], c[:, 0:nt * P], g[:, 0:nt * P], ALU.mult).then_inc(yc_ready, 1)
                    tap2()
                    if not is_last(b):
                        keep_history(su, j, SHIST, None)

                def window_sums(c, x, w0, w1, n_, at):
                    after(at)
                    at = own.step(tt(w0(1, n_), x(1, n_), x(0, n_ - 1), ALU.add))
                    tap2()
                    half = slice(64, P) if c == 0 else slice(0, P)
                    after(at)
                    at = own.step(tt(w1(3, n_)[half], w0(3, n_)[half], w0(1, n_ - 2)[half], ALU.add))
                    tap2()
                    if c == 1:
                        after(at)
                        at = own.step(tt(w0(7, n_), w1(7, n_), w1(3, n_ - 4), ALU.add))
                        tap2()
                        after(at)
                        at = own.step(tt(w1(15, n_)[64:P], w0(15, n_)[64:P], w0(7, n_ - 8)[64:P], ALU.add))
                        tap2()
                    return at

                def pooling(c):
                    dve.wait_ge(work_read, group(b, ORDER.index(("x", c))) + 1)
                    at = None
                    if not first or c:
                        dve.wait_ge(pooled_ready, NPOOL * b + c)
                    out = pslot("g", c)
                    if first:
                        ext = PAST + STEPS
                        x = lambda lo, hi: xa_s[:, c, :, lo:hi]
                        ws = [wsum[:, i, 0:SEQS * ext].rearrange("p (s t) -> p s t", s=SEQS) for i in range(2)]
                        at = window_sums(c, x, lambda lo, hi: ws[0][:, :, lo:hi], lambda lo, hi: ws[1][:, :, lo:hi],
                                         ext, None)
                        after(at)
                        for i in range(2):
                            h = slice(64 * i, 64 * i + 64)
                            at = own.step(stt(seqs(out[:, 0:P])[h], ws[i][h, :, PAST:], 1.0 / WINDOWS[2 * c + i],
                                              xa_s[h, c, :, PAST:], ALU.mult, ALU.subtract))
                    x = lambda lo, hi: xa[:, c, lo:hi]
                    at = window_sums(c, x, lambda lo, hi: wsum[:, 0, lo:hi], lambda lo, hi: wsum[:, 1, lo:hi],
                                     PAST + np_, at)
                    if first:
                        after(at)
                        for i in range(2):
                            h = slice(64 * i, 64 * i + 64)
                            e = slice(E_CNT + c * PAST, E_CNT + (c + 1) * PAST)
                            at = own.step(tt(wsum[h, i, PAST:2 * PAST], wsum[h, i, PAST:2 * PAST], con_a[h, e], ALU.mult))
                    after(at)
                    for i in range(2):
                        h = slice(64 * i, 64 * i + 64)
                        ins = stt(out[h, pc], wsum[h, i, PAST:PAST + np_], 1.0 / WINDOWS[2 * c + i],
                                  xa[h, c, PAST:PAST + np_], ALU.mult, ALU.subtract)
                        if i == 0:
                            at = own.step(ins)
                        else:
                            ins.then_inc(pooled_ready, 1)
                    tap2()
                    if not is_last(b):
                        dve.wait_ge(pooled_ready, NPOOL * b + (c + 1))
                        keep_history(xa, c, PAST, None)

                for j in range(NSC):
                    short_conv(j)
                for c in range(NPOOL):
                    pooling(c)
                while at2[1] < TAPS:
                    tap2()
                if not is_last(b):
                    dve.wait_ge(z_ready, NCONV * (b + 1))
                    for j in range(NCONV):
                        keep_history(u, j, HIST, None)
                if nt_next:
                    for k in range(4):
                        h_rest(b + 1, k, nt_next)
                dve.wait_ge(work_read, group(b, "mean") + 1)
                for j in range(NCONV):
                    z = pslot("a", j)[:, 0:nt * P]
                    tt(z, z, pslot("g", 2)[:, 0:nt * P], ALU.subtract).then_inc(zc_ready, 1)
                if nt_next:
                    for k in range(4, KD):
                        h_rest(b + 1, k, nt_next)
                dve.wait_ge(seed_ready, b + 1)
                r, v, w = (pslot("b", i)[:, 0:nt * P] for i in range(3))
                after(own.step(tt(w, v, r, ALU.mult)))
                after(own.step(tt(w, w, r, ALU.mult)))
                after(own.step(nc.vector.tensor_scalar(w, w, -0.5, 1.5, ALU.mult, ALU.add)))
                after(own.step(tt(r, r, w, ALU.mult)))
                for j in range(NCONV):
                    z = pslot("a", j)[:, 0:nt * P]
                    tt(z, z, r, ALU.mult).then_inc(zn_ready, 1)
                if before:
                    residual(b, TB, gate1, gate1_first)
                for c in range(NMIX):
                    dve.wait_ge(y_hi_ready, NMIX * b + (c + 1))
                    tt(y_lo[:, c, 0:nt * P], y_src(c)[:, 0:nt * P], y_hi[:, c, 0:nt * P].bitcast(F32), ALU.subtract)\
                        .then_inc(y_lo_ready, 1)

            def residual(r, nt, gate, gate_first):
                dve.wait_ge(mix_rstd, r)
                dve.wait_ge(res_landed, 16 * r)

                def scaled(t):
                    return own.step(stt(mix_ps(t), mix_ps(t), rstd_m[:, t:t + 1],
                                        (gate if t else gate_first)[:, :], ALU.mult, ALU.mult))

                def added(t, at):
                    after(at)
                    i = tt(xr[:, t, :], mix_ps(t), xr[:, t, :], ALU.add)
                    if t == 0:
                        i.then_inc(res_first, 1)
                    elif t == nt - 1:
                        i.then_inc(res_ready, 1)
                    else:
                        own.step(i)

                ats = [scaled(0)]
                after(ats[0])
                own.step(nc.vector.tensor_copy(gate_first[:, :], gate[:, :]))
                for t in range(nt):
                    if t + 1 < nt:
                        ats.append(scaled(t + 1))
                    added(t, ats[t])

            mixers(0, TB, False)
            own.enter_loop()
            with dve.Fori(1, NB - 2) as b:
                own.in_loop(b - 1, VEC_STEPS_A)
                mixers(b, TB, True)
            own.leave_loop(NB - 3, VEC_STEPS_A)
            mixers(NB - 2, LAST_TB, True)
            mixers(NB - 1, 0, True)
            for k in range(KD):
                modulate_samples(NB, k, FULL_A + k + 1, 1)
                if k:
                    h_rest(NB, k - 1, TB)
            h_rest(NB, KD - 1, TB)

            def lo_up(b, m, par):
                s = 2 * par + 1
                dve.wait_ge(gu_hi, 2 * NF * b + 2 * m + 2)
                tt(wlo[:, s, :], raw[:, s, :], whi[:, s, :].bitcast(F32), ALU.subtract).then_inc(up_lo, 1)

            def lo_dn(b, k):
                dve.wait_ge(dn_hi, NF * b + k + 1)
                tt(dn_wlo[k % 2], dn_raw[k % 2], dn_whi[k % 2].bitcast(F32), ALU.subtract).then_inc(dn_lo, 1)

            def hidden(b, m, par, nt, split):
                dve.wait_ge(silu_ready, NF * b + m + 1)
                dve.wait_ge(gu_used, 2 * NF * b + 2 * m + 2)
                tt(g_f[:, par, 0:nt * P], ps[:, 2 * par + 1, 0:nt * P], s_buf[:, par, 0:nt * P], ALU.mult)\
                    .then_inc(g_ready, 1)
                split()
                dve.wait_ge(g_hi_ready, NF * b + m + 1)
                one = bass.ds(m, 1)
                tt(g_lo[:, one, 0:nt * P].rearrange("p a n -> p (a n)"), g_f[:, par, 0:nt * P],
                   g_hi[:, one, 0:nt * P].rearrange("p a n -> p (a n)").bitcast(F32), ALU.subtract)\
                    .then_inc(g_lo_ready, 1)

            def ffn_block(b, nt_next):
                nt = tiles_of(b)
                with dve.Fori(0, NF // 2 - 1) as i:
                    for par in range(2):
                        hidden(b, 2 * i + par, par, nt, lambda: lo_up(b, 2 * i + par + 2, par))
                for par in range(2):
                    hidden(b, NF - 2 + par, par, nt, lambda: lo_dn(b, par))
                for k in range(NF):
                    if k + 2 < NF:
                        lo_dn(b, k + 2)
                    if nt_next:
                        if k == 1:
                            normalise(NB + 1 + b, nt_next)
                        if k >= 5 and k % 2 and (k - 5) // 2 < KD:
                            h_rest(NB + 1 + b, (k - 5) // 2, nt_next)
                if nt_next:
                    for par in range(2):
                        lo_up(b + 1, par, par)
                residual(NB + 1 + b, nt, gate2, gate2_first)

            for par in range(2):
                lo_up(0, par, par)
            residual(NB, LAST_TB, gate1, gate1_first)
            dve.wait_ge(states_stored, 16 * 2 * NMIX)
            ffn_block(0, TB)
            own.enter_loop()
            with dve.Fori(1, NB - 2) as b:
                own.in_loop(b - 1, VEC_STEPS_B)
                ffn_block(b, TB)
            own.leave_loop(NB - 3, VEC_STEPS_B)
            ffn_block(NB - 2, LAST_TB)
            ffn_block(NB - 1, 0)


def kernel(x_prompt, x_sample, c_prompt, c_sample, state_pool, state_conv, state_sconv,
           w_ada, b_ada, g_pre_mix, g_post_mix, g_pre_ffn, g_post_ffn,
           w_in, w_pool, s_pool, w_dw, b_dw, ln_g, ln_b, w_sc, w_out,
           w_gate, w_up, w_down):
    import numpy as np
    import concourse.bacc as bacc
    from concourse.bass_utils import run_bass_kernel_spmd

    def c(a):
        return np.ascontiguousarray(a)

    def channel_cols(a):
        n, ch = a.shape
        return a.T.reshape(ch // P, P, n).transpose(1, 0, 2)

    x_all = np.concatenate([np.asarray(x_sample).reshape(-1, D), np.asarray(x_prompt).reshape(-1, D)])
    c_all = c(channel_cols(np.concatenate([np.asarray(c_prompt), np.asarray(c_sample)])))

    consts = np.zeros((P, C_END), np.float32)
    consts[:, C_ID:C_ID + P] = np.eye(P)
    consts[:, C_EPS:C_EPS + TB] = EPS
    consts[:, C_NHALF:C_NHALF + TB] = -0.5
    consts_a = np.zeros((P, E_END), np.float32)
    consts_a[:, E_ONES:E_ONES + P] = 1
    for part in range(2):
        consts_a[part * ROWS, E_SELP:E_SELP + P] = 1
        for s in range(SEQS):
            consts_a[part * ROWS + 1 + s, E_SELS + s * STEPS:E_SELS + (s + 1) * STEPS] = 1
        for r in range(ROWS):
            consts_a[part * ROWS + r, E_SELF + r] = 1
    consts_a[2 * ROWS, E_SELP:E_CNT] = 1
    for g, w in enumerate(WINDOWS):
        h, e = 64 * (g % 2), E_CNT + (g // 2) * PAST
        consts_a[h:h + 64, e:e + PAST] = w / np.minimum(np.arange(PAST) + 1, w)

    cols = np.concatenate([
        channel_cols(np.asarray(g_pre_mix)).reshape(P, -1), channel_cols(np.asarray(g_pre_ffn)).reshape(P, -1),
        channel_cols(np.asarray(s_pool)).reshape(P, -1), channel_cols(np.asarray(w_dw)[0]).reshape(P, -1),
        channel_cols(np.asarray(b_dw)).reshape(P, -1), channel_cols(np.asarray(ln_g)).reshape(P, -1),
        channel_cols(np.asarray(ln_b)).reshape(P, -1), channel_cols(np.asarray(w_sc)[0]).reshape(P, -1)], axis=1)
    gpost = np.concatenate([np.asarray(g_post_mix), np.asarray(g_post_ffn)])

    def stationary_units(w):
        return w.reshape(KD, P, -1, P).transpose(2, 1, 0, 3).reshape(-1, P, D)

    wi = stationary_units(np.asarray(w_in)[0])
    w_mix = np.concatenate([np.stack([wi[COL0[kind] // P + j] for kind, j in ORDER]),
                            np.asarray(w_out)[0].reshape(NMIX, P, D)])
    w_gu = np.stack([stationary_units(np.asarray(w_gate)[0]), stationary_units(np.asarray(w_up)[0])], axis=1)\
        .reshape(2 * NF, P, D)
    w_dn = np.asarray(w_down)[0].reshape(NF, P, D)
    wa = np.asarray(w_ada)[0].reshape(KD, P, 6, D).transpose(2, 0, 1, 3).reshape(NADA, P, D)

    def state_cols(a):
        bb, rows, ch = a.shape
        return a.transpose(2, 0, 1).reshape(ch // P, P, bb, rows).transpose(1, 0, 2, 3)

    ins = dict(x_all=x_all, c_all=c_all, consts=consts, consts_a=consts_a, cols=cols, gpost=gpost,
               b_ada=np.asarray(b_ada), w_ada=wa, w_mix=w_mix, w_pool=np.asarray(w_pool)[0], w_gu=w_gu, w_dn=w_dn,
               st_pool=state_cols(np.asarray(state_pool)[0]), st_conv=state_cols(np.asarray(state_conv)[0]),
               st_sconv=state_cols(np.asarray(state_sconv)[0]))
    outs = dict(y_all=(TILES * P, D), o_pool_p=(P, NPOOL, PAST), o_conv_p=(P, NCONV, HIST),
                o_sconv_p=(P, NSC, SHIST), o_pool_s=(P, NPOOL, SEQS, PAST), o_conv_s=(P, NCONV, SEQS, HIST),
                o_sconv_s=(P, NSC, SEQS, SHIST))
    nc = bacc.Bacc("TRN2", target_bir_lowering=False, num_devices=1)
    ins = {k: c(v) for k, v in ins.items()}
    aps = [nc.dram_tensor(f"in_{k}", v.shape, F32, kind="ExternalInput").ap() for k, v in ins.items()]
    aps += [nc.dram_tensor(f"out_{k}", s, F32, kind="ExternalOutput").ap() for k, s in outs.items()]
    aps.append(nc.dram_tensor("x1_all", (TILES * P, D), F32, kind="Internal").ap())
    build(nc, *aps)
    r = run_bass_kernel_spmd(nc, [{f"in_{k}": v for k, v in ins.items()}], core_ids=[0]).results[0]

    def state_rows(a, seqs):
        a = a.reshape(P, a.shape[1], seqs, -1)
        return c(a.transpose(2, 3, 1, 0).reshape(1, seqs, a.shape[3], -1))

    y = r["out_y_all"]
    return (c(y[T_SAMPLE:].reshape(1, T_PROMPT, D)), c(y[:T_SAMPLE].reshape(SEQS, STEPS, D)),
            state_rows(r["out_o_pool_p"], 1), state_rows(r["out_o_conv_p"], 1), state_rows(r["out_o_sconv_p"], 1),
            state_rows(r["out_o_pool_s"], SEQS), state_rows(r["out_o_conv_s"], SEQS),
            state_rows(r["out_o_sconv_s"], SEQS))
```

```python
from contextlib import ExitStack

import concourse.bass as bass
from concourse import mybir

F32 = mybir.dt.float32
F32R = mybir.dt.float32r
BF16 = mybir.dt.bfloat16
ALU = mybir.AluOpType
ACT = mybir.ActivationFunctionType

P = 128
D = 1024
KD = D // P
T_SAMPLE, T_PROMPT = 128, 2048
SEQS, STEPS = 8, 16
TILES = (T_SAMPLE + T_PROMPT) // P
TB = 3
NB = -(-TILES // TB)
LAST_TB = TILES - TB * (NB - 1)
N = TB * P
EPS = 1e-6
ROWS = 1 + SEQS
MOD_K = 2 * ROWS + 1

WINDOWS = (2, 4, 8, 16)
PAST = max(WINDOWS) - 1
NPOOL, NCONV, NSC = 2, 3, 3
TAPS, STAPS = 31, 3
HIST, SHIST = TAPS - 1, STAPS - 1
NMIX = NPOOL + NCONV + NSC
FF = 2816
NF = FF // P

ORDER = [("h", 0), ("c", 0), ("b", 0), ("a", 0), ("g", 0), ("h", 1), ("c", 1), ("b", 1),
         ("a", 1), ("g", 1), ("a", 2), ("g", 2), ("h", 2), ("c", 2), ("b", 2), ("x", 0), ("x", 1)]
NIN = len(ORDER)
SLOT = {"a": 0, "g": 3, "h": 6, "c": 9, "b": 12}
COL0 = {"x": 0, "a": 256, "g": 640, "h": 1024, "b": 1408, "c": 1792}

RING = 5
ADA_RING = 4
UNITS = NIN + NMIX
assert UNITS % RING == 0
ADA_FIRST = 2 * KD
ADA_REST = 4 * KD
UNITS0 = NIN + ADA_REST
OFF = UNITS0 - UNITS
assert OFF % RING == RING - 1 and ADA_REST == 2 * (NIN - 1)
TOTAL = OFF + UNITS * NB + NMIX

ROT = 2
STAGE = ["t0", "t1", "t2", "t3", "t4", "t5", "t6", "t7", "pool0", "pool1", "mean"]
STAGE_AFTER = {0: ["t0", "t1"], 1: ["t2"], 2: ["t3"], 3: ["t4"], 4: ["t5"], 5: ["t6", "t7"],
               6: ["pool0", "pool1"], 7: ["mean"]}
STAGE_LAST = ["pool0", "pool1", "mean"]
GROUPS = NIN + len(STAGE) + 1

C_ID, C_EPS, C_NHALF = 0, P, P + TB
C_END = C_NHALF + TB
E_ONES, E_SELP, E_SELS, E_SELF, E_CNT = 0, P, 2 * P, 3 * P, 3 * P + ROWS
E_END = E_CNT + NPOOL * PAST
Q_G1, Q_G2, Q_SP, Q_WDW, Q_BDW, Q_LG, Q_LB, Q_WSC = 0, 8, 16, 18, 18 + 93, 114, 117, 120
Q_END = Q_WSC + 9
HEAD, HEAD_FIRST = 8, 20

ACT_STEPS_A, ACT_STEPS_B, POOL_STEPS_A, POOL_STEPS_B, VEC_STEPS_A, VEC_STEPS_B = 5, 4, 2, 2, 130, 5


class Steps:

    def __init__(self, sem):
        self.sem, self.base, self.n = sem, 0, 0

    def step(self, instruction):
        instruction.then_inc(self.sem, 1)
        self.n += 1
        return self.base + self.n

    def enter_loop(self):
        self.before, self.base, self.n = self.base + self.n, None, 0

    def in_loop(self, i, per_pass):
        self.base = i * per_pass + self.before

    def leave_loop(self, passes, per_pass):
        assert self.n == per_pass, (self.n, per_pass)
        self.base, self.n = self.before + passes * per_pass, 0


def is_first(b):
    return isinstance(b, int) and b == 0


def is_last(b):
    return isinstance(b, int) and b == NB - 1


def tiles_of(b):
    return LAST_TB if is_last(b) else TB


def stream_len(b):
    return UNITS0 if is_first(b) else NMIX if isinstance(b, int) and b == NB else UNITS


def unit(b, pos):
    return pos if is_first(b) else UNITS * b + (OFF + pos)


def slot(b, pos):
    return (pos if is_first(b) else OFF + pos) % RING


def landed(b, pos):
    return 16 * (pos // RING + 1) if is_first(b) else 16 * (UNITS // RING) * b + 16 * ((OFF + pos) // RING + 1)


def pos_in(b, j):
    return 3 * j if is_first(b) else j


def unit_in(b, j):
    return unit(b, pos_in(b, j))


def at_out(b, k):
    return (NB, k) if is_last(b) else (b + 1, NIN + k)


def unit_out(b, k):
    return unit(*at_out(b, k))


def by_vector(n):
    return isinstance(n, int) and n < UNITS0 and n % 3 == 2


def lo_count(n):
    if by_vector(n):
        return n // 3 + 1
    if isinstance(n, int) and n < UNITS0:
        return n - n // 3 + 1
    return n - (UNITS0 // 3 - 1)


assert UNITS0 // 3 == 16


def build(nc, x_all, c_all, consts, consts_a, cols, gpost, b_ada, w_ada, w_mix, w_pool, w_gu, w_dn,
          st_pool, st_conv, st_sconv, y_all, o_pool_p, o_conv_p, o_sconv_p,
          o_pool_s, o_conv_s, o_sconv_s, x1_all):
    ctx = ExitStack()
    with ctx:
        def sb(name, shape, dt=F32, scope=ctx):
            return scope.enter_context(nc.sbuf_tensor(name, shape, dt))

        def sem(name):
            return ctx.enter_context(nc.semaphore(name))

        con = sb("con", [P, C_END])
        col = sb("col", [P, Q_END])
        shsc = sb("shsc", [P, 4, KD, ROWS])
        gate2 = sb("gate2", [P, D])
        gate2_first = sb("gate2_first", [P, D])
        raw = sb("raw", [P, RING, D])
        whi = sb("whi", [P, RING, D], F32R)
        wlo = sb("wlo", [P, RING, D], F32R)
        h_hi = sb("h_hi", [P, KD, N], F32R)
        h_lo = sb("h_lo", [P, KD, N], F32R)
        h_f = sb("h_f", [P, 2, N])
        xt = sb("xt", [P, TB, D])
        xr = sb("xr", [P, TB, D])
        junk = sb("junk", [P, D], BF16)
        ssq_x = sb("ssq_x", [P, TB])
        rstd_x = sb("rstd_x", [P, TB])
        ssq_m = sb("ssq_m", [P, TB])
        rstd_m = sb("rstd_m", [P, TB])
        ps = ctx.enter_context(nc.psum_tensor("ps", [P, 8, 512], F32))

        ident = con[:, C_ID:C_ID + P]
        eps = con[:, C_EPS:C_EPS + 1]

        const_landed = sem("const_landed")
        gpost_landed = sem("gpost_landed")
        c_landed = sem("c_landed")
        bias_landed = sem("bias_landed")
        pad_zeroed = sem("pad_zeroed")
        silu_c = sem("silu_c")
        c_hi_ready = sem("c_hi_ready")
        c_ready = sem("c_ready")
        ada_hi = sem("ada_hi")
        ada_lo = sem("ada_lo")
        ada_used = sem("ada_used")
        ada_read = sem("ada_read")
        cols_full = sem("cols_full")
        gates_full = sem("gates_full")
        mod_ready = sem("mod_ready")
        w_pool_zeroed = sem("w_pool_zeroed")
        hist_zeroed = sem("hist_zeroed")
        state_landed = sem("state_landed")
        w_hi = sem("w_hi")
        w_lo = sem("w_lo")
        w_used = sem("w_used")
        x_landed = sem("x_landed")
        x_ssq = sem("x_ssq")
        pool_step = sem("pool_step")
        x_rstd = sem("x_rstd")
        xn_ready = sem("xn_ready")
        sample_mod = sem("sample_mod")
        h_hi_ready = sem("h_hi_ready")
        h_lo_ready = sem("h_lo_ready")
        work_full = sem("work_full")
        work_read = sem("work_read")
        act_step = sem("act_step")
        vec_step = sem("vec_step")
        z_ready = sem("z_ready")
        zc_ready = sem("zc_ready")
        zsq_ready = sem("zsq_ready")
        seed_ready = sem("seed_ready")
        zn_ready = sem("zn_ready")
        pooled_ready = sem("pooled_ready")
        yb_ready = sem("yb_ready")
        yc_ready = sem("yc_ready")
        y_hi_ready = sem("y_hi_ready")
        y_lo_ready = sem("y_lo_ready")
        yb_lo_ready = sem("yb_lo_ready")
        w_lo_vec = sem("w_lo_vec")
        w_pool_landed = sem("w_pool_landed")
        mix_ssq = sem("mix_ssq")
        mix_rstd = sem("mix_rstd")
        res_landed = sem("res_landed")
        res_first = sem("res_first")
        res_ready = sem("res_ready")
        stored = sem("stored")
        states_stored = sem("states_stored")
        gu_hi = sem("gu_hi")
        gate_lo = sem("gate_lo")
        up_lo = sem("up_lo")
        gu_used = sem("gu_used")
        dn_hi = sem("dn_hi")
        dn_lo = sem("dn_lo")
        dn_used = sem("dn_used")
        silu_ready = sem("silu_ready")
        g_ready = sem("g_ready")
        g_hi_ready = sem("g_hi_ready")
        g_lo_ready = sem("g_lo_ready")
        ada_landed = [sem(f"ada_landed{i}") for i in range(ADA_RING)]
        w_landed = [sem(f"w_landed{i}") for i in range(RING)]
        gu_landed = [sem(f"gu_landed{i}") for i in range(4)]
        dn_landed = [sem(f"dn_landed{i}") for i in range(2)]

        x_v = x_all.rearrange("(n p) d -> p n d", p=P)
        x1_v = x1_all.rearrange("(n p) d -> p n d", p=P)
        y_v = y_all.rearrange("(n p) d -> p n d", p=P)

        def group_base(b):
            return KD + ROT + GROUPS * b

        def group(b, name):
            if isinstance(name, int):
                if name >= ROT:
                    return group_base(b) + (name - ROT)
                return KD + name if is_first(b) else group_base(b) + (name - ROT - 1)
            names = (STAGE_LAST if is_last(b) else STAGE)
            if name == "var":
                return group_base(b) + (NIN - ROT + len(names) + (0 if is_last(b) else ROT))
            return group_base(b) + (NIN - ROT + names.index(name))

        def bank_of(b, name):
            if isinstance(name, int) and name < ROT:
                return (GROUPS - ROT - 1 + name) % 2
            names = (STAGE_LAST if is_last(b) else STAGE)
            at = name - ROT if isinstance(name, int) else NIN - ROT + (
                len(names) + (0 if is_last(b) else ROT) if name == "var" else names.index(name))
            return at % 2

        WORK_A = group(NB - 1, "var") + 1

        def full_count(b, name):
            names = (STAGE_LAST if is_last(b) else STAGE) + ["var"]
            return KD + (len(STAGE) + 1) * b + (names.index(name) + 1)

        FULL_A = full_count(NB - 1, "var")

        A = ExitStack()
        mod_scope = ExitStack()
        con_a = sb("con_a", [P, E_END], scope=A)
        c_sb = sb("c_sb", [P, KD, ROWS], scope=A)
        c_s = sb("c_s", [P, KD, ROWS], scope=A)
        gate1 = sb("gate1", [P, D], scope=A)
        gate1_first = sb("gate1_first", [P, D], scope=A)
        mod = sb("mod", [MOD_K, 6 * D], scope=mod_scope)
        c_hl = sb("c_hl", [P, KD, P], F32R, scope=mod_scope)
        mod_scope.close()
        y_hi = sb("y_hi", [P, NMIX, N], F32R, scope=A)
        y_lo = sb("y_lo", [P, NMIX, N], F32R, scope=A)
        wsum = sb("wsum", [P, 2, PAST + N], scope=A)
        w_pl = sb("w_pl", [P, NPOOL, P], scope=A)
        pr = sb("pr", [P, 15, N], scope=A)
        xa = sb("xa", [P, NPOOL, PAST + N], scope=A)
        u = sb("u", [P, NCONV, HIST + N], scope=A)
        su = sb("su", [P, NSC, SHIST + N], scope=A)
        xa_s = sb("xa_s", [P, NPOOL, SEQS, PAST + STEPS], scope=A)
        u_s = sb("u_s", [P, NCONV, SEQS, HIST + STEPS], scope=A)
        su_s = sb("su_s", [P, NSC, SEQS, SHIST + STEPS], scope=A)
        A.close()
        ones = con_a[:, E_ONES:E_ONES + P]
        B = ExitStack()
        g_hi = sb("g_hi", [P, NF, N], F32R, scope=B)
        g_lo = sb("g_lo", [P, NF, N], F32R, scope=B)
        s_buf = sb("s_buf", [P, 2, N], scope=B)
        g_f = sb("g_f", [P, 2, N], scope=B)
        raw5 = sb("raw5", [P, D], scope=B)
        whi5 = sb("whi5", [P, D], F32R, scope=B)
        wlo5 = sb("wlo5", [P, D], F32R, scope=B)
        B.close()
        dn_raw = [raw[:, 4, :], raw5[:, :]]
        dn_whi = [whi[:, 4, :], whi5[:, :]]
        dn_wlo = [wlo[:, 4, :], wlo5[:, :]]

        def chan(ap):
            return ap.rearrange("p (k m) -> p k m", k=KD)

        def pslot(kind, j):
            return pr[:, SLOT[kind] + j, :]

        Y_ORDER = list(range(NPOOL)) + [NPOOL + NCONV + j for j in range(NSC)] + [NPOOL + j for j in range(NCONV)]
        def zsq(j):
            return pslot(*(("c", 1), ("c", 2), ("b", 1))[j])

        NY1 = NPOOL + NSC

        def y_src(c):
            if c < NPOOL:
                return pslot("g", c)
            return pslot("a", c - NPOOL) if c < NPOOL + NCONV else pslot("h", c - NPOOL - NCONV)

        def mix_ps(t):
            return ps[:, 2 + 2 * t:4 + 2 * t, :].rearrange("p a n -> p (a n)")

        def norm_group(q, k):
            if isinstance(q, int) and q == 0:
                return k
            if isinstance(q, int) and q < NB:
                return group(q - 1, f"t{k}")
            return WORK_A + KD * (q - NB) + k

        def norm_full(q, k):
            if isinstance(q, int) and q == 0:
                return k + 1
            if isinstance(q, int) and q < NB:
                return full_count(q - 1, f"t{k}")
            return FULL_A + KD * (q - NB) + k + 1

        def last_unit_in(s):
            return TOTAL - 1 - (TOTAL - 1 - s) % RING

        block = ctx.enter_context(nc.Block())

        @block.sync
        def _(sp):
            sp.dma_start(c_sb[:, :, :], c_all).then_inc(c_landed, 16)
            for i in range(ADA_RING):
                sp.dma_start(raw[:, i, :], w_ada[i]).then_inc(ada_landed[i], 16)
            sp.dma_start(con[:, :], consts).then_inc(const_landed, 16)
            sp.dma_start(con_a[:, :], consts_a).then_inc(const_landed, 16)
            sp.dma_start(col[:, :], cols).then_inc(const_landed, 16)
            sp.dma_start(xt[:, :, :], x_v[:, 0:TB, :]).then_inc(x_landed, 16)
            for r in range(1, ADA_FIRST // ADA_RING):
                for i in range(ADA_RING):
                    sp.wait_ge(ada_lo, (r - 1) * ADA_RING + i + 1)
                    sp.dma_start(raw[:, i, :], w_ada[r * ADA_RING + i]).then_inc(ada_landed[i], 16)
                if r == 1:
                    sp.dma_start(mod[2 * ROWS:MOD_K, :], b_ada).then_inc(bias_landed, 16)

            def load_w(b, pos, src):
                n, s = unit(b, pos), slot(b, pos)
                if not isinstance(n, int) or n >= RING:
                    last = n - RING
                    sp.wait_ge(w_lo_vec if by_vector(last) else w_lo, lo_count(last))
                elif s < ADA_RING:
                    sp.wait_ge(ada_lo, ADA_FIRST - ADA_RING + s + 1)
                sp.dma_start(raw[:, s, :], src).then_inc(w_landed[s], 16)

            for j in range(NIN):
                load_w(0, 3 * j, w_mix[j])
                if j < NIN - 1:
                    for i in range(2):
                        load_w(0, 3 * j + 1 + i, w_ada[ADA_FIRST + 2 * j + i])
                if j == 1:
                    for i in range(2):
                        sp.dma_start(xr[:, i, :], gpost[i:i + 1, :].to_broadcast([P, D])).then_inc(gpost_landed, 16)
                    for c in range(NPOOL):
                        sp.dma_start(xa_s[:, c, :, 0:PAST], st_pool[:, c]).then_inc(state_landed, 16)
                    for c in range(NCONV):
                        sp.dma_start(u_s[:, c, :, 0:HIST], st_conv[:, c]).then_inc(state_landed, 16)
                    for c in range(NSC):
                        sp.dma_start(su_s[:, c, :, 0:SHIST], st_sconv[:, c]).then_inc(state_landed, 16)
                if j == 6:
                    sp.wait_ge(work_full, KD)
                    sp.dma_start(xt[:, :, :], x_v[:, TB:2 * TB, :]).then_inc(x_landed, 16)
            AHEAD = 8
            for j in range(RING - 1):
                load_w(1, j, w_mix[j])
            sp.wait_ge(w_pool_zeroed, 1)
            for g in range(len(WINDOWS)):
                h = 64 * (g % 2)
                sp.dma_start(w_pl[h:h + 64, g // 2, h:h + 64], w_pool[g]).then_inc(w_pool_landed, 16)
            for j in range(RING - 1, AHEAD):
                load_w(1, j, w_mix[j])

            def mixer_loads(b, nt_next):
                for j in range(AHEAD, UNITS):
                    load_w(b, j, w_mix[j])
                    if j == 10:
                        if nt_next:
                            sp.wait_ge(work_full, full_count(b - 1, "t7"))
                            sp.dma_start(xt[:, 0:nt_next, :], x_v[:, bass.ds(TB * b + TB, nt_next), :])\
                              .then_inc(x_landed, 16)
                        else:
                            sp.wait_ge(work_full, full_count(b - 1, "t7"))
                            sp.wait_ge(stored, 16)
                            sp.dma_start(xt[:, :, :], x1_v[:, 0:TB, :]).then_inc(x_landed, 16)
                    if j == 12:
                        if not (isinstance(b, int) and b == 1):
                            sp.wait_ge(stored, 16 * (b - 1))
                        else:
                            sp.wait_ge(mod_ready, 8)
                        sp.dma_start(xr[:, :, :], x_v[:, bass.ds(TB * b - TB, TB), :]).then_inc(res_landed, 16)
                for j in range(NMIX if is_last(b) else AHEAD):
                    load_w(b + 1, j, w_mix[NIN + j] if is_last(b) else w_mix[j])
                sp.wait_ge(res_ready, b)
                sp.dma_start(x1_v[:, bass.ds(TB * b - TB, TB), :], xr[:, :, :]).then_inc(stored, 16)

            mixer_loads(1, TB)
            with sp.Fori(2, NB - 2) as b:
                mixer_loads(b, TB)
            mixer_loads(NB - 2, LAST_TB)
            mixer_loads(NB - 1, 0)

            last_n = LAST_TB * P
            sp.wait_ge(z_ready, NCONV * NB)
            sp.wait_ge(pooled_ready, NPOOL * NB)
            sp.wait_ge(yc_ready, NSC * NB)
            for c in range(NPOOL):
                sp.dma_start(o_pool_p[:, c], xa[:, c, last_n:last_n + PAST]).then_inc(states_stored, 16)
                sp.dma_start(o_pool_s[:, c], xa_s[:, c, :, STEPS:]).then_inc(states_stored, 16)
            for j in range(NCONV):
                sp.dma_start(o_conv_p[:, j], u[:, j, last_n:last_n + HIST]).then_inc(states_stored, 16)
                sp.dma_start(o_conv_s[:, j], u_s[:, j, :, STEPS:]).then_inc(states_stored, 16)
            for j in range(NSC):
                sp.dma_start(o_sconv_p[:, j], su[:, j, last_n:last_n + SHIST]).then_inc(states_stored, 16)
                sp.dma_start(o_sconv_s[:, j], su_s[:, j, :, STEPS:]).then_inc(states_stored, 16)

            sp.wait_ge(stored, 16 * (NB - 1))
            sp.dma_start(xr[:, 0:LAST_TB, :], x_v[:, TB * (NB - 1):TILES, :]).then_inc(res_landed, 16)
            for i in range(4):
                sp.wait_ge(w_lo, lo_count(last_unit_in(i)))
                sp.dma_start(raw[:, i, :], w_gu[i]).then_inc(gu_landed[i], 16)
            sp.wait_ge(w_lo, lo_count(TOTAL - 1))

            def load_gu(b, m, par):
                sp.wait_ge(gate_lo, NF * b + m - 1)
                sp.dma_start(raw[:, 2 * par, :], w_gu[2 * m]).then_inc(gu_landed[2 * par], 16)
                sp.wait_ge(up_lo, NF * b + m - 1)
                sp.dma_start(raw[:, 2 * par + 1, :], w_gu[2 * m + 1]).then_inc(gu_landed[2 * par + 1], 16)

            def load_dn(b, k):
                if not (isinstance(b, int) and b == 0 and k < 2):
                    sp.wait_ge(dn_lo, NF * b + (k - 1))
                sp.dma_start(dn_raw[k % 2], w_dn[k]).then_inc(dn_landed[k % 2], 16)

            def ffn_loads(b, nt_next):
                nt_prev = LAST_TB if isinstance(b, int) and b == 0 else TB
                nt = tiles_of(b)
                with sp.Fori(1, NF // 4 + 1) as i:
                    for par in range(2):
                        load_gu(b, 2 * i + par, par)
                sp.wait_ge(res_ready, NB + b)
                if isinstance(b, int) and b == 0:
                    sp.dma_start(x1_v[:, TB * (NB - 1):TILES, :], xr[:, 0:LAST_TB, :]).then_inc(stored, 16)
                    sp.wait_ge(states_stored, 16 * 2 * NMIX)
                    sp.wait_ge(w_used, TOTAL)
                else:
                    sp.dma_start(y_v[:, bass.ds(TB * b - TB, TB), :], xr[:, :, :]).then_inc(stored, 16)
                load_dn(b, 0)
                load_dn(b, 1)
                with sp.Fori(NF // 4 + 1, NF // 2) as i:
                    for par in range(2):
                        load_gu(b, 2 * i + par, par)
                sp.wait_ge(stored, 16 * NB + 16 * b)
                sp.dma_start(xr[:, 0:nt, :], x1_v[:, bass.ds(TB * b, nt), :]).then_inc(res_landed, 16)
                if nt_next:
                    sp.wait_ge(work_full, norm_full(NB + b, KD - 1))
                    sp.dma_start(xt[:, 0:nt_next, :], x1_v[:, bass.ds(TB * b + TB, nt_next), :])\
                      .then_inc(x_landed, 16)
                for k in range(2, NF):
                    load_dn(b, k)
                    if k == 9 and nt_next:
                        for i in range(4):
                            sp.wait_ge(up_lo if i % 2 else gate_lo, NF * b + NF - 1 + i // 2)
                            sp.dma_start(raw[:, i, :], w_gu[i]).then_inc(gu_landed[i], 16)

            ffn_loads(0, TB)
            with sp.Fori(1, NB - 2) as b:
                ffn_loads(b, TB)
            ffn_loads(NB - 2, LAST_TB)
            ffn_loads(NB - 1, 0)
            sp.wait_ge(res_ready, 2 * NB)
            sp.dma_start(y_v[:, TB * (NB - 1):TILES, :], xr[:, 0:LAST_TB, :]).then_inc(stored, 16)
            sp.wait_ge(stored, 16 * 2 * NB)

        @block.tensor
        def _(pe):
            def mm(out, lhsT, rhs, start, stop):
                return nc.tensor.matmul(out, lhsT, rhs, start=start, stop=stop, skip_group_check=True)

            def ada_unit(k, s, pair):
                for h in range(2):
                    w = slice(512 * h, 512 * h + 512)
                    out = ps[:, 2 + 2 * pair + h, :]
                    mm(out, c_hl[:, k, :], whi[:, s, w], k == 0, False)
                    last = mm(out, c_hl[:, k, :], wlo[:, s, w], False, k == KD - 1)
                return last

            def ada_columns(first, bank):
                for i in range(2):
                    for k in range(KD):
                        c0 = (first + i) * D + k * P
                        last = mm(ps[:, bank, (i * KD + k) * ROWS:(i * KD + k + 1) * ROWS], mod[:, c0:c0 + P],
                                  con_a[0:MOD_K, E_SELF:E_SELF + ROWS], True, True)
                last.then_inc(cols_full, 1)

            def gate_rows(i):
                g, e = (2, 5)[i // 2], (E_SELP, E_SELS)[i % 2]
                if i >= 2:
                    pe.wait_ge(mod_ready, 4 + i - 1)
                for h in range(2):
                    c0 = g * D + 512 * h
                    last = mm(ps[:, 2 + 2 * (i % 2) + h, :], con_a[0:MOD_K, e:e + P], mod[:, c0:c0 + 512], True, True)
                last.then_inc(gates_full, 1)

            pe.wait_ge(c_ready, 1)
            for g in range(2):
                for k in range(KD):
                    pe.wait_ge(ada_lo, KD * g + k + 1)
                    ada_unit(k, k % ADA_RING, g).then_inc(ada_used, 1)
            pe.wait_ge(bias_landed, 16)
            pe.wait_ge(const_landed, 48)
            pe.wait_ge(ada_read, 2)
            ada_columns(0, 0)

            def transposes(q, k, nt, bank, wait):
                if k == 0:
                    pe.wait_ge(xn_ready, q + 1)
                if wait is not None:
                    pe.wait_ge(work_read, wait)
                for t in range(nt):
                    last = nc.tensor.transpose(ps[:, bank, t * P:(t + 1) * P], xt[:, t, k * P:(k + 1) * P], ident)
                last.then_inc(work_full, 1)

            pe.wait_ge(mod_ready, 2)
            for k in range(KD):
                transposes(0, k, TB, k % 2, k - 1 if k >= 2 else None)

            def wait_unit(n):
                pe.wait_ge(w_lo_vec if by_vector(n) else w_lo, lo_count(n))

            def project(b, j):
                n, s, nt = unit_in(b, j), slot(b, pos_in(b, j)), tiles_of(b)
                g = group(b, j)
                pe.wait_ge(work_read, g if j == ROT else g - 1)
                wait_unit(n)
                if j == 0:
                    pe.wait_ge(h_lo_ready, KD * (b + 1))
                w_h, w_l = chan(whi[:, s, :]), chan(wlo[:, s, :])
                out = ps[:, bank_of(b, j), 0:nt * P]
                for k in range(KD):
                    mm(out, w_h[:, k, :], h_hi[:, k, 0:nt * P], k == 0, False)
                    mm(out, w_h[:, k, :], h_lo[:, k, 0:nt * P], False, False)
                    last = mm(out, w_l[:, k, :], h_hi[:, k, 0:nt * P], False, k == KD - 1)
                last.then_inc(w_used, 1)

            def project_first(j):
                project(0, j)
                if j == NIN - 1:
                    return
                for i in range(2):
                    n, k, g = 3 * j + 1 + i, (2 * j + i) % KD, j // 4
                    if k == 0 and g == 3:
                        pe.wait_ge(ada_read, 3)
                    elif k == 0 and g < 2:
                        pe.wait_ge(ada_read, g + 1)
                    wait_unit(n)
                    ada_unit(k, n % RING, g % 3).then_inc(w_used, 1)

            def token_major(a_hi, a_lo, b_hi, b_lo, k, nk, nt):
                for t in range(nt):
                    c = slice(t * P, (t + 1) * P)
                    for st, mv, first, end in ((a_hi, b_hi, k == 0, False), (a_hi, b_lo, False, False),
                                               (a_lo, b_hi, False, k == nk - 1)):
                        for h in range(2):
                            w = slice(512 * h, 512 * h + 512)
                            last = mm(ps[:, 2 + 2 * t + h, :], st[:, k, c], mv[:, w], first, end)
                return last

            def mix_out(b, k):
                n, s = unit_out(b, k), slot(*at_out(b, k))
                if k == 0:
                    pe.wait_ge(y_lo_ready, NY1 * (b + 1))
                    pe.wait_ge(yb_lo_ready, NCONV * (b + 1))
                    if is_first(b):
                        pe.wait_ge(mod_ready, 8)
                    else:
                        pe.wait_ge(res_ready, b)
                wait_unit(n)
                token_major(y_hi, y_lo, whi[:, s, :], wlo[:, s, :], k, NMIX, tiles_of(b)).then_inc(w_used, 1)

            def stage_group(b, name, nt_next):
                nt = tiles_of(b)
                out = ps[:, bank_of(b, name), 0:nt * P]
                if name[0] == "t":
                    transposes(b + 1, int(name[1]), nt_next, bank_of(b, name), group(b, name) - 1)
                    return
                pe.wait_ge(work_read, group(b, name) - 1)
                if name == "mean":
                    pe.wait_ge(z_ready, NCONV * (b + 1))
                    for j in range(NCONV):
                        last = mm(out, ones, pslot("a", j)[:, 0:nt * P], j == 0, j == NCONV - 1)
                elif name == "var":
                    pe.wait_ge(zsq_ready, NCONV * (b + 1))
                    for j in range(NCONV):
                        last = mm(out, ones, zsq(j)[:, 0:nt * P], j == 0, j == NCONV - 1)
                else:
                    c = int(name[-1])
                    pe.wait_ge(pooled_ready, NPOOL * b + (c + 1))
                    last = mm(out, w_pl[:, c, :], pslot("g", c)[:, 0:nt * P], True, True)
                last.then_inc(work_full, 1)

            def mixer_block(b, nt_next):
                for j in range(ROT, NIN):
                    if is_first(b):
                        project_first(j)
                    else:
                        project(b, j)
                if is_first(b):
                    pe.wait_ge(ada_read, 6)
                    ada_columns(3, 7)
                    gate_rows(0)
                    gate_rows(1)
                for k in range(NMIX):
                    if not is_first(b):
                        mix_out(b - 1, k)
                    for name in STAGE_AFTER[k]:
                        if is_first(b) and name == "pool0":
                            gate_rows(2)
                            gate_rows(3)
                            pe.wait_ge(w_pool_landed, 16 * len(WINDOWS))
                        if nt_next or name in STAGE_LAST:
                            stage_group(b, name, nt_next)
                if nt_next:
                    for j in range(ROT):
                        project(b + 1, j)
                stage_group(b, "var", nt_next)

            for j in range(ROT):
                project_first(j)
            mixer_block(0, TB)
            with pe.Fori(1, NB - 2) as b:
                mixer_block(b, TB)
            mixer_block(NB - 2, LAST_TB)
            mixer_block(NB - 1, 0)
            for k in range(2):
                transposes(NB, k, TB, (k + 1) % 2, WORK_A + k - 1)
            for k in range(NMIX):
                mix_out(NB - 1, k)
                if k + 2 < KD:
                    transposes(NB, k + 2, TB, (k + 3) % 2, WORK_A + k + 1)

            def gate_up(b, m, par, nt):
                for i in range(2):
                    s = 2 * par + i
                    pe.wait_ge(gate_lo if i == 0 else up_lo, NF * b + m + 1)
                    w_h, w_l = chan(whi[:, s, :]), chan(wlo[:, s, :])
                    out = ps[:, s, 0:nt * P]
                    for k in range(KD):
                        mm(out, w_h[:, k, :], h_hi[:, k, 0:nt * P], k == 0, False)
                        mm(out, w_h[:, k, :], h_lo[:, k, 0:nt * P], False, False)
                        last = mm(out, w_l[:, k, :], h_hi[:, k, 0:nt * P], False, k == KD - 1)
                    last.then_inc(gu_used, 1)

            def ffn_block(b, nt_next):
                nt = tiles_of(b)
                pe.wait_ge(h_lo_ready, KD * NB + KD * (b + 1))
                pe.wait_ge(work_read, norm_group(NB + b, KD - 1) + 1)
                gate_up(b, 0, 0, nt)
                pe.wait_ge(res_first, NB + b)
                gate_up(b, 1, 1, nt)
                with pe.Fori(1, NF // 2) as i:
                    for par in range(2):
                        pe.wait_ge(silu_ready, NF * b + 2 * i + par - 1)
                        pe.wait_ge(g_ready, NF * b + 2 * i + par - 1)
                        gate_up(b, 2 * i + par, par, nt)
                pe.wait_ge(silu_ready, NF * b + NF)
                pe.wait_ge(g_ready, NF * b + NF)
                pe.wait_ge(res_ready, NB + b)
                for k in range(NF):
                    pe.wait_ge(dn_lo, NF * b + k + 1)
                    pe.wait_ge(g_lo_ready, NF * b + k + 1)
                    token_major(g_hi, g_lo, dn_whi[k % 2], dn_wlo[k % 2], k, NF, nt).then_inc(dn_used, 1)
                    c = (k - 3) // 2
                    if nt_next and k % 2 and 0 <= c < KD:
                        q = NB + 1 + b
                        transposes(q, c, nt_next, c % 2, None if c < 2 else norm_group(q, c) - 1)

            ffn_block(0, TB)
            with pe.Fori(1, NB - 2) as b:
                ffn_block(b, TB)
            ffn_block(NB - 2, LAST_TB)
            ffn_block(NB - 1, 0)

        @block.scalar
        def _(act):
            own = Steps(act_step)

            act.wait_ge(c_landed, 16)
            nc.scalar.activation(c_s[:, :, :], c_sb[:, :, :], ACT.Silu).then_inc(silu_c, 1)
            act.wait_ge(silu_c, 1)
            act.wait_ge(pad_zeroed, 1)
            nc.scalar.activation(c_hl[:, :, 0:ROWS], c_s[:, :, :], ACT.Copy).then_inc(c_hi_ready, 1)

            def ada_evacuate(g, pair):
                nc.scalar.activation(mod[0:2 * ROWS, g * D:(g + 1) * D], mix_ps(pair)[0:2 * ROWS, :], ACT.Copy)\
                  .then_inc(ada_read, 1)

            def ada_group(g):
                for k in range(KD):
                    s = k % ADA_RING
                    act.wait_ge(ada_landed[s], 32 * g + 16 * (k // ADA_RING + 1))
                    if g or k >= ADA_RING:
                        act.wait_ge(ada_used, KD * g + k - ADA_RING + 1)
                    nc.scalar.activation(whi[:, s, :], raw[:, s, :], ACT.Copy).then_inc(ada_hi, 1)

            def split_unit(b, pos):
                n, s = unit(b, pos), slot(b, pos)
                act.wait_ge(w_landed[s], landed(b, pos))
                if isinstance(n, int) and n < RING:
                    if s < ADA_RING:
                        act.wait_ge(ada_used, ADA_FIRST - ADA_RING + s + 1)
                else:
                    act.wait_ge(w_used, n - RING + 1)
                nc.scalar.activation(whi[:, s, :], raw[:, s, :], ACT.Copy).then_inc(w_hi, 1)

            LEAD = RING - 1

            def split_ahead(b, pos):
                n = pos + LEAD - stream_len(b)
                if n < 0:
                    split_unit(b, pos + LEAD)
                elif not (isinstance(b, int) and b == NB):
                    split_unit(b + 1, n)

            def mean_squares(src, dst, nt, done):
                for t in range(nt):
                    i = nc.scalar.activation(junk[:, :], src(t), ACT.Square, scale=D ** -0.5,
                                             accum_out=dst[:, t:t + 1])
                    if t == nt - 1:
                        i.then_inc(done, 1)
                    else:
                        act.wait_ge(act_step, own.step(i))

            def x_squares(q, nt):
                act.wait_ge(x_landed, 16 * (q + 1))
                mean_squares(lambda t: xt[:, t, :], ssq_x, nt, x_ssq)

            def mix_squares(nt):
                mean_squares(mix_ps, ssq_m, nt, mix_ssq)

            def x_normalise(q, nt):
                act.wait_ge(x_rstd, q + 1)
                for t in range(nt):
                    i = nc.scalar.activation(xt[:, t, :], xt[:, t, :], ACT.Copy, scale=rstd_x[:, t:t + 1])
                    if t == nt - 1:
                        i.then_inc(xn_ready, 1)

            def modulate(q, k, nt, bank, ph, full, free, sample=False):
                act.wait_ge(work_full, full)
                if free is not None:
                    act.wait_ge(h_lo_ready, free)
                c = P if sample else 0
                if sample:
                    act.wait_ge(sample_mod, KD * (q // NB) + k + 1)
                nc.scalar.activation(h_f[:, k % 2, c:nt * P], ps[:, bank, c:nt * P], ACT.Identity,
                                     scale=shsc[:, 2 * ph + 1, k, 0:1], bias=shsc[:, 2 * ph, k, 0:1])\
                  .then_inc(work_read, 1)

            def h_split(k, nt, read):
                act.wait_ge(work_read, read)
                nc.scalar.activation(h_hi[:, k, 0:nt * P], h_f[:, k % 2, 0:nt * P], ACT.Copy).then_inc(h_hi_ready, 1)

            ada_group(0)
            x_squares(0, TB)
            ada_group(1)
            act.wait_ge(ada_used, KD)
            ada_evacuate(0, 0)
            x_normalise(0, TB)
            act.wait_ge(ada_used, 2 * KD)
            ada_evacuate(1, 1)
            for j in range(LEAD):
                split_unit(0, j)
            act.wait_ge(mod_ready, 2)
            for k in range(KD):
                modulate(0, k, TB, k % 2, 0, k + 1, k - 1 if k >= 2 else None, True)
                h_split(k, TB, k + 1)

            def evacuate(b, j):
                kind, c = ORDER[j]
                nt = tiles_of(b)
                act.wait_ge(w_used, unit_in(b, j) + 1)
                if not is_first(b):
                    if kind == "h":
                        act.wait_ge(y_lo_ready, NY1 * b + (NPOOL + c + 1 - NY1))
                    elif kind == "a":
                        act.wait_ge(yb_lo_ready, NCONV * b + (c + 1 - NCONV))
                src = ps[:, bank_of(b, j), 0:nt * P]
                if kind != "x":
                    f = ACT.Sigmoid if kind == "g" else ACT.Copy
                    nc.scalar.activation(pslot(kind, c)[:, 0:nt * P], src, f).then_inc(work_read, 1)
                elif is_first(b):
                    own.step(nc.scalar.activation(
                        xa_s[:, c, :, PAST:], src[:, 0:P].rearrange("p (s t) -> p s t", s=SEQS), ACT.Copy))
                    nc.scalar.activation(xa[:, c, PAST:PAST + (nt - 1) * P], src[:, P:], ACT.Copy).then_inc(work_read, 1)
                else:
                    nc.scalar.activation(xa[:, c, PAST:PAST + nt * P], src, ACT.Copy).then_inc(work_read, 1)

            def y_split(b, i):
                c = Y_ORDER[i]
                if not is_first(b):
                    act.wait_ge(w_used, unit_out(b - 1, c) + 1)
                else:
                    act.wait_ge(gates_full, 4)
                if i < NPOOL:
                    act.wait_ge(work_read, group(b, f"pool{i}") + 1)
                elif i < NY1:
                    act.wait_ge(yc_ready, NSC * b + (i - NPOOL + 1))
                else:
                    act.wait_ge(yb_ready, NCONV * b + (i - NY1 + 1))
                w = slice(0, tiles_of(b) * P)
                nc.scalar.activation(y_hi[:, c, w], y_src(c)[:, w], ACT.Copy).then_inc(y_hi_ready, 1)

            def stage_group(b, name, nt_next):
                nt = tiles_of(b)
                bank = bank_of(b, name)
                src = ps[:, bank, 0:nt * P]
                if name[0] == "t":
                    k = int(name[1])
                    if k == 0:
                        act.wait_ge(w_used, unit_in(b, NIN - 1) + 1)
                    modulate(None, k, nt_next, bank, 0, full_count(b, name), KD * (b + 1) + (k - 1))
                    return
                act.wait_ge(work_full, full_count(b, name))
                if name == "mean":
                    nc.scalar.activation(pslot("g", 2)[:, 0:nt * P], src, ACT.Copy, scale=1.0 / (NCONV * P))\
                      .then_inc(work_read, 1)
                elif name == "var":
                    r, v = pslot("b", 2)[:, 0:nt * P], pslot("g", 2)[:, 0:nt * P]
                    nc.scalar.activation(v, src, ACT.Identity, scale=1.0 / (NCONV * P), bias=eps)\
                      .then_inc(work_read, 1)
                    act.wait_ge(work_read, group(b, name) + 1)
                    at = own.step(nc.scalar.activation(r, v, ACT.Ln))
                    act.wait_ge(act_step, at)
                    nc.scalar.activation(r, r, ACT.Exp, scale=-0.5).then_inc(seed_ready, 1)
                else:
                    c = int(name[-1])
                    nc.scalar.activation(pslot("g", c)[:, 0:nt * P], src, ACT.Copy,
                                         scale=col[:, Q_SP + c:Q_SP + c + 1]).then_inc(work_read, 1)

            def squares_of_centred(b):
                for j in range(NCONV):
                    w = slice(0, tiles_of(b) * P)
                    act.wait_ge(zc_ready, NCONV * b + (j + 1))
                    nc.scalar.activation(zsq(j)[:, w], pslot("a", j)[:, w], ACT.Square).then_inc(zsq_ready, 1)

            def mix_ready_squares(b):
                act.wait_ge(w_used, unit_out(b - 1, NMIX - 1) + 1)
                mix_squares(TB)

            def conformer_out(b):
                w = slice(0, tiles_of(b) * P)
                for j in range(NCONV):
                    act.wait_ge(zn_ready, NCONV * b + (j + 1))
                    nc.scalar.activation(pslot("a", j)[:, w], pslot("a", j)[:, w], ACT.Silu,
                                         scale=col[:, Q_LG + j:Q_LG + j + 1],
                                         bias=col[:, Q_LB + j:Q_LB + j + 1]).then_inc(yb_ready, 1)
                for i in range(NY1, NMIX):
                    y_split(b, i)

            def ahead_first(j):
                split_ahead(0, 3 * j)
                evacuate(0, j)
                if j < NIN - 1:
                    split_ahead(0, 3 * j + 1)
                    split_ahead(0, 3 * j + 2)
                if j % 4 == 3:
                    act.wait_ge(w_used, 3 * j + 3)
                    ada_evacuate(2 + j // 4, (j // 4) % 3)

            def mixer_block(b, nt_next):
                for j in range(ROT + 1, NIN):
                    if is_first(b):
                        ahead_first(j)
                    else:
                        split_ahead(b, j)
                        evacuate(b, j)
                    if j == 8:
                        x_squares(b + 1, nt_next or TB)
                    if j == 12:
                        x_normalise(b + 1, nt_next or TB)
                for k in range(NMIX):
                    names = [x for x in STAGE_AFTER[k] if nt_next or x in STAGE_LAST]
                    for name in names:
                        stage_group(b, name, nt_next)
                    if not is_first(b):
                        split_ahead(b, NIN + k)
                    for name in names:
                        if name[0] == "t":
                            h_split(int(name[1]), nt_next, group(b, name) + 1)
                    if k == 6:
                        for i in range(3):
                            y_split(b, i)
                    elif k == 7:
                        y_split(b, 3)
                if nt_next:
                    split_ahead(b + 1, 0)
                    evacuate(b + 1, 0)
                squares_of_centred(b)
                y_split(b, 4)
                if not is_first(b):
                    mix_ready_squares(b)
                if nt_next:
                    split_ahead(b + 1, 1)
                    evacuate(b + 1, 1)
                stage_group(b, "var", nt_next)
                if nt_next:
                    split_ahead(b + 1, 2)
                    evacuate(b + 1, 2)
                    conformer_out(b)

            for j in range(ROT + 1):
                ahead_first(j)
            mixer_block(0, TB)
            own.enter_loop()
            with act.Fori(1, NB - 2) as b:
                own.in_loop(b - 1, ACT_STEPS_A)
                mixer_block(b, TB)
            own.leave_loop(NB - 3, ACT_STEPS_A)
            mixer_block(NB - 2, LAST_TB)
            mixer_block(NB - 1, 0)
            act.wait_ge(w_used, unit_in(NB - 1, NIN - 1) + 1)
            conformer_out(NB - 1)
            for k in range(KD):
                modulate(NB, k, TB, (k + 1) % 2, 1, FULL_A + k + 1, KD * NB + k - 1, True)
                h_split(k, TB, WORK_A + k + 1)
                if k < NMIX - LEAD:
                    split_ahead(NB, k)

            def split_dn(b, k):
                act.wait_ge(dn_landed[k % 2], 16 * (NF // 2) * b + 16 * (k // 2 + 1))
                if not (isinstance(b, int) and b == 0 and k < 2):
                    act.wait_ge(dn_used, NF * b + (k - 1))
                elif k == 0:
                    act.wait_ge(w_used, TOTAL)
                nc.scalar.activation(dn_whi[k % 2], dn_raw[k % 2], ACT.Copy).then_inc(dn_hi, 1)

            def hidden(b, m, par, nt, split):
                act.wait_ge(gu_used, 2 * NF * b + 2 * m + 1)
                nc.scalar.activation(s_buf[:, par, 0:nt * P], ps[:, 2 * par, 0:nt * P], ACT.Silu).then_inc(silu_ready, 1)
                split()
                act.wait_ge(g_ready, NF * b + m + 1)
                nc.scalar.activation(g_hi[:, bass.ds(m, 1), 0:nt * P].rearrange("p a n -> p (a n)"),
                                     g_f[:, par, 0:nt * P], ACT.Copy).then_inc(g_hi_ready, 1)

            def ffn_block(b, nt_next):
                nt = tiles_of(b)
                mix_nt = LAST_TB if isinstance(b, int) and b == 0 else TB

                def split_two_on(m, par, i_times=None):
                    count = 16 * (NF // 2) * b + (i_times + 32 if i_times is not None else 16 * (m // 2) + 32)
                    act.wait_ge(gu_landed[2 * par], count)
                    nc.scalar.activation(whi[:, 2 * par, :], raw[:, 2 * par, :], ACT.Copy).then_inc(gu_hi, 1)
                    act.wait_ge(gu_used, 2 * NF * b + 2 * m + 2)
                    act.wait_ge(gu_landed[2 * par + 1], count)
                    nc.scalar.activation(whi[:, 2 * par + 1, :], raw[:, 2 * par + 1, :], ACT.Copy).then_inc(gu_hi, 1)

                with act.Fori(0, NF // 2 - 1) as i:
                    for par in range(2):
                        hidden(b, 2 * i + par, par, nt, lambda: split_two_on(2 * i + par, par, 16 * i))
                for par in range(2):
                    hidden(b, NF - 2 + par, par, nt, lambda: split_dn(b, par))
                if nt_next:
                    x_squares(NB + 1 + b, nt_next)
                    x_normalise(NB + 1 + b, nt_next)
                for k in range(NF):
                    if k + 2 < NF:
                        split_dn(b, k + 2)
                    c = (k - 3) // 2
                    if nt_next and k % 2 and 0 <= c < KD:
                        q = NB + 1 + b
                        if c == 0:
                            act.wait_ge(gu_used, 2 * NF * b + 2 * NF)
                        act.wait_ge(work_full, FULL_A + KD * (b + 1) + (c + 1))
                        act.wait_ge(h_lo_ready, KD * q + (c - 1))
                        nc.scalar.activation(h_f[:, c % 2, 0:nt_next * P], ps[:, c % 2, 0:nt_next * P], ACT.Identity,
                                             scale=shsc[:, 3, c, 0:1], bias=shsc[:, 2, c, 0:1]).then_inc(work_read, 1)
                    if nt_next and k % 2 == 0 and 0 <= (k - 4) // 2 < KD and k >= 4:
                        c = (k - 4) // 2
                        h_split(c, nt_next, WORK_A + KD * (b + 1) + c + 1)
                    if nt_next and k >= NF - 4:
                        s = k - (NF - 4)
                        act.wait_ge(gu_landed[s], 16 * (NF // 2) * (b + 1) + 16)
                        nc.scalar.activation(whi[:, s, :], raw[:, s, :], ACT.Copy).then_inc(gu_hi, 1)
                act.wait_ge(dn_used, NF * (b + 1))
                mix_squares(nt)

            for s in range(4):
                act.wait_ge(gu_landed[s], 16)
                act.wait_ge(w_used, last_unit_in(s) + 1)
                nc.scalar.activation(whi[:, s, :], raw[:, s, :], ACT.Copy).then_inc(gu_hi, 1)
            act.wait_ge(w_used, TOTAL)
            mix_squares(LAST_TB)
            act.wait_ge(states_stored, 16 * 2 * NMIX)
            ffn_block(0, TB)
            own.enter_loop()
            with act.Fori(1, NB - 2) as b:
                own.in_loop(b - 1, ACT_STEPS_B)
                ffn_block(b, TB)
            own.leave_loop(NB - 3, ACT_STEPS_B)
            ffn_block(NB - 2, LAST_TB)
            ffn_block(NB - 1, 0)

        @block.gpsimd
        def _(pool):
            nc.gpsimd.memset(c_hl[:, :, :].bitcast(F32), 0.0).then_inc(pad_zeroed, 1)
            steps = Steps(pool_step)

            def rstd(ssq, out, nt, done):
                at = steps.step(nc.gpsimd.tensor_tensor(ssq[:, 0:nt], ssq[:, 0:nt], con[:, C_EPS:C_EPS + nt], ALU.add))
                pool.wait_ge(pool_step, at)
                nc.gpsimd.tensor_tensor(out[:, 0:nt], ssq[:, 0:nt], con[:, C_NHALF:C_NHALF + nt], ALU.pow)\
                  .then_inc(done, 1)

            def lo(b, pos):
                s = slot(b, pos)
                pool.wait_ge(w_hi, unit(b, pos) + 1)
                nc.gpsimd.tensor_tensor(wlo[:, s, :], raw[:, s, :], whi[:, s, :].bitcast(F32), ALU.subtract)\
                  .then_inc(w_lo, 1)

            LEAD = RING - 1

            def lo_ahead(b, pos):
                n = pos + LEAD - stream_len(b)
                if n >= 0:
                    if not (isinstance(b, int) and b == NB):
                        lo(b + 1, n)
                elif not by_vector(unit(b, pos + LEAD)):
                    lo(b, pos + LEAD)

            def h_rest(q, k, nt):
                pool.wait_ge(h_hi_ready, KD * q + (k + 1))
                nc.gpsimd.tensor_tensor(h_lo[:, k, 0:nt * P], h_f[:, k % 2, 0:nt * P],
                                        h_hi[:, k, 0:nt * P].bitcast(F32), ALU.subtract).then_inc(h_lo_ready, 1)

            def y_rest(b, i):
                c, w = Y_ORDER[i], slice(0, tiles_of(b) * P)
                pool.wait_ge(y_hi_ready, NMIX * b + (i + 1))
                nc.gpsimd.tensor_tensor(y_lo[:, c, w], y_src(c)[:, w], y_hi[:, c, w].bitcast(F32), ALU.subtract)\
                  .then_inc(y_lo_ready, 1)

            pool.wait_ge(const_landed, 48)
            pool.wait_ge(x_ssq, 1)
            rstd(ssq_x, rstd_x, TB, x_rstd)
            for j in range(LEAD):
                if not by_vector(j):
                    lo(0, j)
            for k in range(KD):
                h_rest(0, k, TB)

            def ahead_first(j):
                lo_ahead(0, 3 * j)
                if j < NIN - 1:
                    lo_ahead(0, 3 * j + 1)
                    lo_ahead(0, 3 * j + 2)

            def mixer_block(b, nt_next):
                for j in range(ROT + 1, NIN):
                    if is_first(b):
                        ahead_first(j)
                    else:
                        lo_ahead(b, j)
                    if j == 9:
                        pool.wait_ge(x_ssq, b + 2)
                        rstd(ssq_x, rstd_x, nt_next or TB, x_rstd)
                for k in range(NMIX):
                    if not is_first(b):
                        lo_ahead(b, NIN + k)
                    if nt_next:
                        for name in STAGE_AFTER[k]:
                            if name[0] == "t":
                                h_rest(b + 1, int(name[1]), nt_next)
                    if k == 5 and is_first(b):
                        pool.wait_ge(gates_full, 4)
                        nc.gpsimd.memset(w_pl[:, :, :], 0.0).then_inc(w_pool_zeroed, 1)
                    if k == 6:
                        for i in range(3):
                            y_rest(b, i)
                    elif k == 7:
                        y_rest(b, 3)
                if nt_next:
                    lo_ahead(b + 1, 0)
                y_rest(b, 4)
                if not is_first(b):
                    pool.wait_ge(mix_ssq, b)
                    rstd(ssq_m, rstd_m, TB, mix_rstd)
                if nt_next:
                    lo_ahead(b + 1, 1)
                    lo_ahead(b + 1, 2)

            for j in range(ROT + 1):
                ahead_first(j)
            mixer_block(0, TB)
            steps.enter_loop()
            with pool.Fori(1, NB - 2) as b:
                steps.in_loop(b - 1, POOL_STEPS_A)
                mixer_block(b, TB)
            steps.leave_loop(NB - 3, POOL_STEPS_A)
            mixer_block(NB - 2, LAST_TB)
            mixer_block(NB - 1, 0)
            for k in range(KD):
                h_rest(NB, k, TB)
                if k < NMIX - LEAD:
                    lo_ahead(NB, k)

            def lo_gate(b, m, par):
                pool.wait_ge(gu_hi, 2 * NF * b + 2 * m + 1)
                nc.gpsimd.tensor_tensor(wlo[:, 2 * par, :], raw[:, 2 * par, :], whi[:, 2 * par, :].bitcast(F32),
                                        ALU.subtract).then_inc(gate_lo, 1)

            def ffn_block(b, nt_next):
                with pool.Fori(1, NF // 2) as i:
                    for par in range(2):
                        lo_gate(b, 2 * i + par, par)
                if nt_next:
                    pool.wait_ge(x_ssq, NB + b + 2)
                    rstd(ssq_x, rstd_x, nt_next, x_rstd)
                    for par in range(2):
                        lo_gate(b + 1, par, par)
                pool.wait_ge(mix_ssq, NB + b + 1)
                rstd(ssq_m, rstd_m, tiles_of(b), mix_rstd)

            for par in range(2):
                lo_gate(0, par, par)
            pool.wait_ge(mix_ssq, NB)
            rstd(ssq_m, rstd_m, LAST_TB, mix_rstd)
            ffn_block(0, TB)
            steps.enter_loop()
            with pool.Fori(1, NB - 2) as b:
                steps.in_loop(b - 1, POOL_STEPS_B)
                ffn_block(b, TB)
            steps.leave_loop(NB - 3, POOL_STEPS_B)
            ffn_block(NB - 2, LAST_TB)
            ffn_block(NB - 1, 0)

        @block.vector
        def _(dve):
            own = Steps(vec_step)

            def after(at):
                if at is not None:
                    dve.wait_ge(vec_step, at)

            tt = nc.vector.tensor_tensor
            stt = nc.vector.scalar_tensor_tensor

            dve.wait_ge(c_hi_ready, 1)
            tt(c_hl[:, :, ROWS:2 * ROWS], c_s[:, :, :], c_hl[:, :, 0:ROWS].bitcast(F32), ALU.subtract)\
                .then_inc(c_ready, 1)
            for n in range(ADA_FIRST):
                s = n % ADA_RING
                dve.wait_ge(ada_hi, n + 1)
                tt(wlo[:, s, :], raw[:, s, :], whi[:, s, :].bitcast(F32), ALU.subtract).then_inc(ada_lo, 1)

            def columns(i, bank):
                dve.wait_ge(cols_full, i + 1)
                src = ps[:, bank, 0:2 * KD * ROWS].rearrange("p (i k r) -> p i k r", i=2, k=KD)
                nc.vector.tensor_copy(shsc[:, 2 * i, :, :], src[:, 0]).then_inc(mod_ready, 1)
                g0 = (Q_G1, Q_G2)[i]
                stt(shsc[:, 2 * i + 1, :, :], src[:, 1], 1.0,
                    col[:, g0:g0 + KD].unsqueeze(2).to_broadcast([P, KD, ROWS]), ALU.add, ALU.mult)\
                    .then_inc(mod_ready, 1)

            def gate(i):
                dve.wait_ge(gates_full, i + 1)
                dst = (gate1, gate1_first, gate2, gate2_first)[i]
                tt(dst[:, :], mix_ps(i % 2), xr[:, i // 2, :], ALU.mult).then_inc(mod_ready, 1)

            dve.wait_ge(const_landed, 48)
            columns(0, 0)

            def seqs(ap):
                return ap.rearrange("p (s t) -> p s t", s=SEQS)

            def modulate_samples(q, k, full, ph):
                dve.wait_ge(work_full, full)
                if k >= 2 or q:
                    dve.wait_ge(h_hi_ready, KD * q + (k - 1))
                    dve.wait_ge(h_lo_ready, KD * q + (k - 1))
                dst = seqs(h_f[:, k % 2, 0:P])
                bank = (k + ph) % 2
                at = own.step(tt(dst, seqs(ps[:, bank, 0:P]),
                                 shsc[:, 2 * ph + 1, k, 1:ROWS].unsqueeze(2).to_broadcast([P, SEQS, STEPS]), ALU.mult))
                after(at)
                tt(dst, dst, shsc[:, 2 * ph, k, 1:ROWS].unsqueeze(2).to_broadcast([P, SEQS, STEPS]), ALU.add)\
                    .then_inc(sample_mod, 1)

            def first_lo(m):
                s = (3 * m + 2) % RING
                dve.wait_ge(w_hi, 3 * m + 3)
                tt(wlo[:, s, :], raw[:, s, :], whi[:, s, :].bitcast(F32), ALU.subtract).then_inc(w_lo_vec, 1)

            for t_, n_ in ((xa, PAST), (u, HIST), (su, SHIST)):
                nc.vector.memset(t_[:, :, 0:n_], 0.0).then_inc(hist_zeroed, 1)
            first_lo(0)
            dve.wait_ge(mod_ready, 2)
            for k in range(KD):
                modulate_samples(0, k, k + 1, 0)
            first_lo(1)
            first_lo(2)
            dve.wait_ge(hist_zeroed, 3)
            dve.wait_ge(state_landed, 16 * NMIX)

            lo_done, taps = [3], [0]

            def lo_up_to(n):
                while lo_done[0] < min(n, NIN - 1):
                    first_lo(lo_done[0])
                    lo_done[0] += 1

            def mixers(b, nt_next):
                nt = tiles_of(b)
                first = is_first(b)
                c0 = P if first else 0
                np_ = nt * P - c0
                pc = slice(c0, c0 + np_)

                def both(samples, prompt):
                    if first:
                        own.step(samples())
                    return prompt()

                def glu(j):
                    if first:
                        lo_up_to(ORDER.index(("g", j)) + 1)
                    dve.wait_ge(work_read, group(b, ORDER.index(("g", j))) + 1)
                    a, g = pslot("a", j), pslot("g", j)
                    return own.step(both(
                        lambda: tt(u_s[:, j, :, HIST:], seqs(a[:, 0:P]), seqs(g[:, 0:P]), ALU.mult),
                        lambda: tt(u[:, j, HIST:HIST + np_], a[:, pc], g[:, pc], ALU.mult)))

                def tap(j, k, at):
                    z = pslot("a", j)
                    w = col[:, Q_WDW + j * TAPS + k:Q_WDW + j * TAPS + k + 1]
                    after(at)
                    if k == 0:
                        bias = col[:, Q_BDW + j:Q_BDW + j + 1]
                        i = both(
                            lambda: nc.vector.tensor_scalar(seqs(z[:, 0:P]), u_s[:, j, :, 0:STEPS], w, bias,
                                                            ALU.mult, ALU.add),
                            lambda: nc.vector.tensor_scalar(z[:, pc], u[:, j, 0:np_], w, bias, ALU.mult, ALU.add))
                    else:
                        i = both(
                            lambda: stt(seqs(z[:, 0:P]), u_s[:, j, :, k:k + STEPS], w, seqs(z[:, 0:P]),
                                        ALU.mult, ALU.add),
                            lambda: stt(z[:, pc], u[:, j, k:k + np_], w, z[:, pc], ALU.mult, ALU.add))
                    if k == TAPS - 1:
                        i.then_inc(z_ready, 1)
                        at = None
                    else:
                        at = own.step(i)
                    if first:
                        taps[0] += 1
                        if taps[0] % 7 == 0:
                            lo_up_to(lo_done[0] + 1)
                    return at

                at0, at1, at2 = glu(0), None, None
                head = HEAD_FIRST if first else HEAD
                for k in range(head):
                    at0 = tap(0, k, at0)
                at1 = glu(1)
                for k in range(head, TAPS):
                    at0 = tap(0, k, at0)
                    at1 = tap(1, k - head, at1)
                at2 = glu(2)
                for k in range(TAPS - head, TAPS):
                    at1 = tap(1, k, at1)
                    at2 = tap(2, k - (TAPS - head), at2)
                state2 = [at2, head]

                def tap2():
                    if state2[1] < TAPS:
                        state2[0] = tap(2, state2[1], state2[0])
                        state2[1] += 1

                def window_sums(c, x, w0, w1, n_, at):
                    after(at)
                    at = own.step(tt(w0(1, n_), x(1, n_), x(0, n_ - 1), ALU.add))
                    tap2()
                    half = slice(64, P) if c == 0 else slice(0, P)
                    after(at)
                    at = own.step(tt(w1(3, n_)[half], w0(3, n_)[half], w0(1, n_ - 2)[half], ALU.add))
                    tap2()
                    if c == 1:
                        after(at)
                        at = own.step(tt(w0(7, n_), w1(7, n_), w1(3, n_ - 4), ALU.add))
                        tap2()
                        after(at)
                        at = own.step(tt(w1(15, n_)[64:P], w0(15, n_)[64:P], w0(7, n_ - 8)[64:P], ALU.add))
                        tap2()
                    return at

                def pooling(c):
                    dve.wait_ge(work_read, group(b, ORDER.index(("x", c))) + 1)
                    at = None
                    if not first or c:
                        dve.wait_ge(pooled_ready, NPOOL * b + c)
                    out = pslot("g", c)
                    if first:
                        ext = PAST + STEPS
                        x = lambda lo, hi: xa_s[:, c, :, lo:hi]
                        ws = [wsum[:, i, 0:SEQS * ext].rearrange("p (s t) -> p s t", s=SEQS) for i in range(2)]
                        at = window_sums(c, x, lambda lo, hi: ws[0][:, :, lo:hi], lambda lo, hi: ws[1][:, :, lo:hi],
                                         ext, None)
                        after(at)
                        for i in range(2):
                            h = slice(64 * i, 64 * i + 64)
                            at = own.step(stt(seqs(out[:, 0:P])[h], ws[i][h, :, PAST:], 1.0 / WINDOWS[2 * c + i],
                                              xa_s[h, c, :, PAST:], ALU.mult, ALU.subtract))
                    x = lambda lo, hi: xa[:, c, lo:hi]
                    at = window_sums(c, x, lambda lo, hi: wsum[:, 0, lo:hi], lambda lo, hi: wsum[:, 1, lo:hi],
                                     PAST + np_, at)
                    if first:
                        after(at)
                        for i in range(2):
                            h = slice(64 * i, 64 * i + 64)
                            e = slice(E_CNT + c * PAST, E_CNT + (c + 1) * PAST)
                            at = own.step(tt(wsum[h, i, PAST:2 * PAST], wsum[h, i, PAST:2 * PAST], con_a[h, e], ALU.mult))
                    after(at)
                    for i in range(2):
                        h = slice(64 * i, 64 * i + 64)
                        ins = stt(out[h, pc], wsum[h, i, PAST:PAST + np_], 1.0 / WINDOWS[2 * c + i],
                                  xa[h, c, PAST:PAST + np_], ALU.mult, ALU.subtract)
                        if i == 0:
                            at = own.step(ins)
                        else:
                            ins.then_inc(pooled_ready, 1)
                    tap2()
                    if not is_last(b):
                        dve.wait_ge(pooled_ready, NPOOL * b + (c + 1))
                        keep_history(xa, c, PAST, np_)

                if first:
                    lo_up_to(NIN - 1)
                    columns(1, 7)
                    gate_factors()
                    gate(0)
                    gate(1)
                for j in range(1, NSC):
                    short_conv(b, j, tap2)
                if first:
                    gate(2)
                    gate(3)
                for c in range(NPOOL):
                    pooling(c)
                while state2[1] < TAPS:
                    tap2()
                if not is_last(b):
                    dve.wait_ge(z_ready, NCONV * (b + 1))
                    for j in range(NCONV):
                        keep_history(u, j, HIST, np_)
                dve.wait_ge(work_read, group(b, "mean") + 1)
                for j in range(NCONV):
                    z = pslot("a", j)[:, 0:nt * P]
                    tt(z, z, pslot("g", 2)[:, 0:nt * P], ALU.subtract).then_inc(zc_ready, 1)
                if not first:
                    residual(b, TB, gate1, gate1_first)
                dve.wait_ge(seed_ready, b + 1)
                r, v, w = (pslot(*x)[:, 0:nt * P] for x in (("b", 2), ("g", 2), ("g", 0)))
                dve.wait_ge(y_lo_ready, NY1 * b + 1)
                after(own.step(tt(w, v, r, ALU.mult)))
                after(own.step(tt(w, w, r, ALU.mult)))
                after(own.step(nc.vector.tensor_scalar(w, w, -0.5, 1.5, ALU.mult, ALU.add)))
                after(own.step(tt(r, r, w, ALU.mult)))
                for j in range(NCONV):
                    z = pslot("a", j)[:, 0:nt * P]
                    tt(z, z, r, ALU.mult).then_inc(zn_ready, 1)
                if not is_last(b):
                    short_conv(b + 1, 0, lambda: None)
                for j in range(NCONV):
                    c, w = NPOOL + j, slice(0, nt * P)
                    dve.wait_ge(y_hi_ready, NMIX * b + (NY1 + j + 1))
                    tt(y_lo[:, c, w], y_src(c)[:, w], y_hi[:, c, w].bitcast(F32), ALU.subtract).then_inc(yb_lo_ready, 1)

            def gate_factors():
                dve.wait_ge(gpost_landed, 32)

            def keep_history(buf, j, n_hist, np_):
                own.step(nc.vector.tensor_copy(buf[:, j, 0:n_hist], buf[:, j, np_:np_ + n_hist]))

            def short_conv(b, j, between):
                nt, first = tiles_of(b), is_first(b)
                c0 = P if first else 0
                np_ = nt * P - c0
                pc = slice(c0, c0 + np_)

                def both(samples, prompt):
                    if first:
                        own.step(samples())
                    return prompt()

                dve.wait_ge(work_read, group(b, ORDER.index(("b", j))) + 1)
                h, c, g = pslot("h", j), pslot("c", j), pslot("b", j)
                at = own.step(both(lambda: tt(su_s[:, j, :, SHIST:], seqs(c[:, 0:P]), seqs(h[:, 0:P]), ALU.mult),
                                   lambda: tt(su[:, j, SHIST:SHIST + np_], c[:, pc], h[:, pc], ALU.mult)))
                between()
                for k in range(STAPS):
                    w = col[:, Q_WSC + j * STAPS + k:Q_WSC + j * STAPS + k + 1]
                    after(at)
                    if k == 0:
                        at = own.step(both(
                            lambda: nc.vector.tensor_scalar(seqs(c[:, 0:P]), su_s[:, j, :, 0:STEPS], w, None, ALU.mult),
                            lambda: nc.vector.tensor_scalar(c[:, pc], su[:, j, 0:np_], w, None, ALU.mult)))
                    else:
                        at = own.step(both(
                            lambda: stt(seqs(c[:, 0:P]), su_s[:, j, :, k:k + STEPS], w, seqs(c[:, 0:P]),
                                        ALU.mult, ALU.add),
                            lambda: stt(c[:, pc], su[:, j, k:k + np_], w, c[:, pc], ALU.mult, ALU.add)))
                    between()
                after(at)
                tt(h[:, 0:nt * P], c[:, 0:nt * P], g[:, 0:nt * P], ALU.mult).then_inc(yc_ready, 1)
                between()
                if not is_last(b):
                    keep_history(su, j, SHIST, np_)

            def residual(r, nt, gate_, gate_first):
                dve.wait_ge(mix_rstd, r)
                dve.wait_ge(res_landed, 16 * r)

                def scaled(t):
                    return own.step(stt(mix_ps(t), mix_ps(t), rstd_m[:, t:t + 1],
                                        (gate_ if t else gate_first)[:, :], ALU.mult, ALU.mult))

                def added(t, at):
                    after(at)
                    i = tt(xr[:, t, :], mix_ps(t), xr[:, t, :], ALU.add)
                    if t == 0:
                        i.then_inc(res_first, 1)
                    elif t == nt - 1:
                        i.then_inc(res_ready, 1)
                    else:
                        own.step(i)

                ats = [scaled(0)]
                after(ats[0])
                own.step(nc.vector.tensor_copy(gate_first[:, :], gate_[:, :]))
                for t in range(nt):
                    if t + 1 < nt:
                        ats.append(scaled(t + 1))
                    added(t, ats[t])

            short_conv(0, 0, lambda: None)
            mixers(0, TB)
            own.enter_loop()
            with dve.Fori(1, NB - 2) as b:
                own.in_loop(b - 1, VEC_STEPS_A)
                mixers(b, TB)
            own.leave_loop(NB - 3, VEC_STEPS_A)
            mixers(NB - 2, LAST_TB)
            mixers(NB - 1, 0)
            for k in range(KD):
                modulate_samples(NB, k, FULL_A + k + 1, 1)

            def h_rest(q, k, nt):
                dve.wait_ge(h_hi_ready, KD * q + (k + 1))
                tt(h_lo[:, k, 0:nt * P], h_f[:, k % 2, 0:nt * P], h_hi[:, k, 0:nt * P].bitcast(F32), ALU.subtract)\
                    .then_inc(h_lo_ready, 1)

            def lo_up(b, m, par):
                s = 2 * par + 1
                dve.wait_ge(gu_hi, 2 * NF * b + 2 * m + 2)
                tt(wlo[:, s, :], raw[:, s, :], whi[:, s, :].bitcast(F32), ALU.subtract).then_inc(up_lo, 1)

            def lo_dn(b, k):
                dve.wait_ge(dn_hi, NF * b + k + 1)
                tt(dn_wlo[k % 2], dn_raw[k % 2], dn_whi[k % 2].bitcast(F32), ALU.subtract).then_inc(dn_lo, 1)

            def hidden(b, m, par, nt, split):
                dve.wait_ge(silu_ready, NF * b + m + 1)
                dve.wait_ge(gu_used, 2 * NF * b + 2 * m + 2)
                tt(g_f[:, par, 0:nt * P], ps[:, 2 * par + 1, 0:nt * P], s_buf[:, par, 0:nt * P], ALU.mult)\
                    .then_inc(g_ready, 1)
                split()
                dve.wait_ge(g_hi_ready, NF * b + m + 1)
                one = bass.ds(m, 1)
                tt(g_lo[:, one, 0:nt * P].rearrange("p a n -> p (a n)"), g_f[:, par, 0:nt * P],
                   g_hi[:, one, 0:nt * P].rearrange("p a n -> p (a n)").bitcast(F32), ALU.subtract)\
                    .then_inc(g_lo_ready, 1)

            def ffn_block(b, nt_next):
                nt = tiles_of(b)
                with dve.Fori(0, NF // 2 - 1) as i:
                    for par in range(2):
                        hidden(b, 2 * i + par, par, nt, lambda: lo_up(b, 2 * i + par + 2, par))
                for par in range(2):
                    hidden(b, NF - 2 + par, par, nt, lambda: lo_dn(b, par))
                for k in range(NF):
                    if k + 2 < NF:
                        lo_dn(b, k + 2)
                    if nt_next and k >= 5 and k % 2 and (k - 5) // 2 < KD:
                        h_rest(NB + 1 + b, (k - 5) // 2, nt_next)
                if nt_next:
                    for par in range(2):
                        lo_up(b + 1, par, par)
                residual(NB + 1 + b, nt, gate2, gate2_first)

            for par in range(2):
                lo_up(0, par, par)
            residual(NB, LAST_TB, gate1, gate1_first)
            dve.wait_ge(states_stored, 16 * 2 * NMIX)
            ffn_block(0, TB)
            own.enter_loop()
            with dve.Fori(1, NB - 2) as b:
                own.in_loop(b - 1, VEC_STEPS_B)
                ffn_block(b, TB)
            own.leave_loop(NB - 3, VEC_STEPS_B)
            ffn_block(NB - 2, LAST_TB)
            ffn_block(NB - 1, 0)


def kernel(x_prompt, x_sample, c_prompt, c_sample, state_pool, state_conv, state_sconv,
           w_ada, b_ada, g_pre_mix, g_post_mix, g_pre_ffn, g_post_ffn,
           w_in, w_pool, s_pool, w_dw, b_dw, ln_g, ln_b, w_sc, w_out,
           w_gate, w_up, w_down):
    import numpy as np
    import concourse.bacc as bacc
    from concourse.bass_utils import run_bass_kernel_spmd

    def c(a):
        return np.ascontiguousarray(a)

    def channel_cols(a):
        n, ch = a.shape
        return a.T.reshape(ch // P, P, n).transpose(1, 0, 2)

    x_all = np.concatenate([np.asarray(x_sample).reshape(-1, D), np.asarray(x_prompt).reshape(-1, D)])
    c_all = c(channel_cols(np.concatenate([np.asarray(c_prompt), np.asarray(c_sample)])))

    consts = np.zeros((P, C_END), np.float32)
    consts[:, C_ID:C_ID + P] = np.eye(P)
    consts[:, C_EPS:C_EPS + TB] = EPS
    consts[:, C_NHALF:C_NHALF + TB] = -0.5
    consts_a = np.zeros((P, E_END), np.float32)
    consts_a[:, E_ONES:E_ONES + P] = 1
    for part in range(2):
        consts_a[part * ROWS, E_SELP:E_SELP + P] = 1
        for s in range(SEQS):
            consts_a[part * ROWS + 1 + s, E_SELS + s * STEPS:E_SELS + (s + 1) * STEPS] = 1
        for r in range(ROWS):
            consts_a[part * ROWS + r, E_SELF + r] = 1
    consts_a[2 * ROWS, E_SELP:E_CNT] = 1
    for g, w in enumerate(WINDOWS):
        h, e = 64 * (g % 2), E_CNT + (g // 2) * PAST
        consts_a[h:h + 64, e:e + PAST] = w / np.minimum(np.arange(PAST) + 1, w)

    cols = np.concatenate([
        channel_cols(np.asarray(g_pre_mix)).reshape(P, -1), channel_cols(np.asarray(g_pre_ffn)).reshape(P, -1),
        channel_cols(np.asarray(s_pool)).reshape(P, -1), channel_cols(np.asarray(w_dw)[0]).reshape(P, -1),
        channel_cols(np.asarray(b_dw)).reshape(P, -1), channel_cols(np.asarray(ln_g)).reshape(P, -1),
        channel_cols(np.asarray(ln_b)).reshape(P, -1), channel_cols(np.asarray(w_sc)[0]).reshape(P, -1)], axis=1)
    gpost = np.concatenate([np.asarray(g_post_mix), np.asarray(g_post_ffn)])

    def stationary_units(w):
        return w.reshape(KD, P, -1, P).transpose(2, 1, 0, 3).reshape(-1, P, D)

    wi = stationary_units(np.asarray(w_in)[0])
    w_mix = np.concatenate([np.stack([wi[COL0[kind] // P + j] for kind, j in ORDER]),
                            np.asarray(w_out)[0].reshape(NMIX, P, D)])
    w_gu = np.stack([stationary_units(np.asarray(w_gate)[0]), stationary_units(np.asarray(w_up)[0])], axis=1)\
        .reshape(2 * NF, P, D)
    w_dn = np.asarray(w_down)[0].reshape(NF, P, D)
    wa = np.asarray(w_ada)[0].reshape(KD, P, 6, D).transpose(2, 0, 1, 3).reshape(6 * KD, P, D)

    def state_cols(a):
        bb, rows, ch = a.shape
        return a.transpose(2, 0, 1).reshape(ch // P, P, bb, rows).transpose(1, 0, 2, 3)

    ins = dict(x_all=x_all, c_all=c_all, consts=consts, consts_a=consts_a, cols=cols, gpost=gpost,
               b_ada=np.asarray(b_ada), w_ada=wa, w_mix=w_mix, w_pool=np.asarray(w_pool)[0], w_gu=w_gu, w_dn=w_dn,
               st_pool=state_cols(np.asarray(state_pool)[0]), st_conv=state_cols(np.asarray(state_conv)[0]),
               st_sconv=state_cols(np.asarray(state_sconv)[0]))
    outs = dict(y_all=(TILES * P, D), o_pool_p=(P, NPOOL, PAST), o_conv_p=(P, NCONV, HIST),
                o_sconv_p=(P, NSC, SHIST), o_pool_s=(P, NPOOL, SEQS, PAST), o_conv_s=(P, NCONV, SEQS, HIST),
                o_sconv_s=(P, NSC, SEQS, SHIST))
    nc = bacc.Bacc("TRN2", target_bir_lowering=False, num_devices=1)
    ins = {k: c(v) for k, v in ins.items()}
    aps = [nc.dram_tensor(f"in_{k}", v.shape, F32, kind="ExternalInput").ap() for k, v in ins.items()]
    aps += [nc.dram_tensor(f"out_{k}", s, F32, kind="ExternalOutput").ap() for k, s in outs.items()]
    aps.append(nc.dram_tensor("x1_all", (TILES * P, D), F32, kind="Internal").ap())
    build(nc, *aps)
    r = run_bass_kernel_spmd(nc, [{f"in_{k}": v for k, v in ins.items()}], core_ids=[0]).results[0]

    def state_rows(a, seqs):
        a = a.reshape(P, a.shape[1], seqs, -1)
        return c(a.transpose(2, 3, 1, 0).reshape(1, seqs, a.shape[3], -1))

    y = r["out_y_all"]
    return (c(y[T_SAMPLE:].reshape(1, T_PROMPT, D)), c(y[:T_SAMPLE].reshape(SEQS, STEPS, D)),
            state_rows(r["out_o_pool_p"], 1), state_rows(r["out_o_conv_p"], 1), state_rows(r["out_o_sconv_p"], 1),
            state_rows(r["out_o_pool_s"], SEQS), state_rows(r["out_o_conv_s"], SEQS),
            state_rows(r["out_o_sconv_s"], SEQS))
```

```python
from contextlib import ExitStack

import concourse.bass as bass
from concourse import mybir

F32 = mybir.dt.float32
F32R = mybir.dt.float32r
BF16 = mybir.dt.bfloat16
ALU = mybir.AluOpType
ACT = mybir.ActivationFunctionType

P = 128
D = 1024
KD = D // P
T_SAMPLE, T_PROMPT = 128, 2048
SEQS, STEPS = 8, 16
TILES = (T_SAMPLE + T_PROMPT) // P
TB = 3
NB = -(-TILES // TB)
LAST_TB = TILES - TB * (NB - 1)
N = TB * P
EPS = 1e-6
ROWS = 1 + SEQS
MOD_K = 2 * ROWS + 1

WINDOWS = (2, 4, 8, 16)
PAST = max(WINDOWS) - 1
NPOOL, NCONV, NSC = 2, 3, 3
TAPS, STAPS = 31, 3
HIST, SHIST = TAPS - 1, STAPS - 1
NMIX = NPOOL + NCONV + NSC
FF = 2816
NF = FF // P

ORDER = [("h", 0), ("c", 0), ("b", 0), ("a", 0), ("g", 0), ("a", 1), ("g", 1), ("h", 1), ("c", 1),
         ("b", 1), ("a", 2), ("g", 2), ("h", 2), ("c", 2), ("b", 2), ("x", 0), ("x", 1)]
NIN = len(ORDER)
SLOT = {"a": 0, "g": 3, "h": 6, "c": 9, "b": 12}
COL0 = {"x": 0, "a": 256, "g": 640, "h": 1024, "b": 1408, "c": 1792}

RING = 5
ADA_RING = 4
ADA_RAW = ADA_RING + 5
UNITS = NIN + NMIX
assert UNITS % RING == 0
ADA_FIRST = 2 * KD
ADA_REST = 4 * KD
UNITS0 = NIN + ADA_REST
OFF = UNITS0 - UNITS
assert OFF % RING == RING - 1 and ADA_REST == 2 * (NIN - 1)
TOTAL = OFF + UNITS * NB + NMIX

ROT = 2
T_GROUPS = [f"t{k}" for k in range(KD)]
POOL_GROUPS = [f"pool{c}" for c in range(NPOOL)]
N_GROUPS = [f"n{j}" for j in range(ROT)]
REST = list(range(ROT, NIN))
SEQ_FIRST = REST + T_GROUPS + N_GROUPS + POOL_GROUPS + ["mean", "var"]
SEQ = REST + T_GROUPS + POOL_GROUPS + ["mean"] + N_GROUPS + ["var"]
SEQ_LAST = REST + POOL_GROUPS + ["mean", "var"]
AGAIN = "t3"
STAGE_AFTER = {0: ["t0", "t1"], 1: ["t2"], 2: ["t3"], 3: ["t4"], 4: ["t5"], 5: ["t6", "t7"],
               6: ["pool0", "pool1"], 7: ["mean"]}
STAGE_AFTER_LAST = {3: ["pool0", "pool1"], 4: ["mean"], 6: ["var"]}
GROUPS = len(SEQ)
NOT_PROJECTED = [x for x in SEQ if x not in REST + N_GROUPS]

Y = [("h", 0), ("g", 0), ("g", 1), ("h", 1), ("h", 2), ("a", 0), ("a", 1), ("a", 2)]
NY1 = NPOOL + NSC
Y_ROW = {"g": 0, "a": NPOOL, "h": NPOOL + NCONV}

C_ID, C_EPS, C_NHALF = 0, P, P + TB
C_END = C_NHALF + TB
E_ONES, E_SELP, E_SELS, E_CNT = 0, P, 2 * P, 3 * P
E_END = E_CNT + NPOOL * PAST
Q_G1, Q_G2, Q_SP, Q_WDW, Q_BDW, Q_LG, Q_LB, Q_WSC = 0, 8, 16, 18, 18 + 93, 114, 117, 120
Q_END = Q_WSC + 9
HEAD, HEAD_FIRST = 8, 12

ACT_STEPS_A, ACT_STEPS_B, POOL_STEPS_A, POOL_STEPS_B, VEC_STEPS_A, VEC_STEPS_B = 1, 0, 3, 3, 129, 4


class Steps:

    def __init__(self, sem):
        self.sem, self.base, self.n = sem, 0, 0

    def step(self, instruction):
        instruction.then_inc(self.sem, 1)
        self.n += 1
        return self.base + self.n

    def enter_loop(self):
        self.before, self.base, self.n = self.base + self.n, None, 0

    def in_loop(self, i, per_pass):
        self.base = i * per_pass + self.before

    def leave_loop(self, passes, per_pass):
        assert self.n == per_pass, (self.n, per_pass)
        self.base, self.n = self.before + passes * per_pass, 0


def is_first(b):
    return isinstance(b, int) and b == 0


def is_last(b):
    return isinstance(b, int) and b == NB - 1


def tiles_of(b):
    return LAST_TB if is_last(b) else TB


def stream_len(b):
    return UNITS0 if is_first(b) else NMIX if isinstance(b, int) and b == NB else UNITS


def unit(b, pos):
    return pos if is_first(b) else UNITS * b + (OFF + pos)


def slot(b, pos):
    return (pos if is_first(b) else OFF + pos) % RING


def landed(b, pos):
    return 16 * (pos // RING + 1) if is_first(b) else 16 * (UNITS // RING) * b + 16 * ((OFF + pos) // RING + 1)


def pos_in(b, j):
    return 3 * j if is_first(b) else j


def unit_in(b, j):
    return unit(b, pos_in(b, j))


def at_out(b, k):
    return (NB, k) if is_last(b) else (b + 1, NIN + k)


def splits_after(b, k):
    return ({4: [0, 1, 2], 5: [3, 4]} if is_last(b) else {5: [0], 6: [1, 2], 7: [3]}).get(k, [])


def after_chunk(b, k):
    return (STAGE_AFTER_LAST if is_last(b) else STAGE_AFTER).get(k, [])


def unit_out(b, k):
    return unit(*at_out(b, k))


def by_vector(n):
    return isinstance(n, int) and n < UNITS0 and n % 3 == 2


def lo_count(n):
    if by_vector(n):
        return n // 3 + 1
    if isinstance(n, int) and n < UNITS0:
        return n - n // 3 + 1
    return n - (UNITS0 // 3 - 1)


assert UNITS0 // 3 == 16


def build(nc, x_all, c_all, consts, consts_a, cols, gpost, b_ada, w_ada, w_mix, w_pool, w_gu, w_dn,
          st_pool, st_conv, st_sconv, y_all, o_pool_p, o_conv_p, o_sconv_p,
          o_pool_s, o_conv_s, o_sconv_s, x1_all):
    ctx = ExitStack()
    with ctx:
        def sb(name, shape, dt=F32, scope=ctx):
            return scope.enter_context(nc.sbuf_tensor(name, shape, dt))

        def sem(name):
            return ctx.enter_context(nc.semaphore(name))

        con = sb("con", [P, C_END])
        col = sb("col", [P, Q_END])
        shsc = sb("shsc", [P, 4, KD, ROWS])
        gate2 = sb("gate2", [P, D])
        gate2_first = sb("gate2_first", [P, D])
        raw = sb("raw", [P, RING, D])
        whi = sb("whi", [P, RING, D], F32R)
        wlo = sb("wlo", [P, RING, D], F32R)
        h_hi = sb("h_hi", [P, KD, N], F32R)
        h_lo = sb("h_lo", [P, KD, N], F32R)
        h_f = sb("h_f", [P, 2, N])
        xt = sb("xt", [P, TB, D])
        xr = sb("xr", [P, TB, D])
        junk = sb("junk", [P, D], BF16)
        ssq_x = sb("ssq_x", [P, TB])
        rstd_x = sb("rstd_x", [P, TB])
        ssq_m = sb("ssq_m", [P, TB])
        rstd_m = sb("rstd_m", [P, TB])
        ps = ctx.enter_context(nc.psum_tensor("ps", [P, 8, 512], F32))

        ident = con[:, C_ID:C_ID + P]
        eps = con[:, C_EPS:C_EPS + 1]

        const_landed = sem("const_landed")
        gpost_landed = sem("gpost_landed")
        c_landed = sem("c_landed")
        bias_landed = sem("bias_landed")
        pad_zeroed = sem("pad_zeroed")
        silu_c = sem("silu_c")
        c_hi_ready = sem("c_hi_ready")
        c_ready = sem("c_ready")
        ada_hi = sem("ada_hi")
        ada_lo = sem("ada_lo")
        ada_used = sem("ada_used")
        ada_read = sem("ada_read")
        cols_full = sem("cols_full")
        gates_full = sem("gates_full")
        mod_ready = sem("mod_ready")
        w_pool_zeroed = sem("w_pool_zeroed")
        hist_zeroed = sem("hist_zeroed")
        state_landed = sem("state_landed")
        w_hi = sem("w_hi")
        w_lo = sem("w_lo")
        w_used = sem("w_used")
        x_landed = sem("x_landed")
        x_ssq = sem("x_ssq")
        pool_step = sem("pool_step")
        x_rstd = sem("x_rstd")
        xn_ready = sem("xn_ready")
        sample_mod = sem("sample_mod")
        h_hi_ready = sem("h_hi_ready")
        h_lo_ready = sem("h_lo_ready")
        work_full = sem("work_full")
        work_read = sem("work_read")
        act_step = sem("act_step")
        vec_step = sem("vec_step")
        z_ready = sem("z_ready")
        zc_ready = sem("zc_ready")
        zsq_ready = sem("zsq_ready")
        seed_ready = sem("seed_ready")
        zn_ready = sem("zn_ready")
        pooled_ready = sem("pooled_ready")
        yb_ready = sem("yb_ready")
        yc_ready = sem("yc_ready")
        y_hi_ready = sem("y_hi_ready")
        y_lo_ready = sem("y_lo_ready")
        yb_lo_ready = sem("yb_lo_ready")
        w_lo_vec = sem("w_lo_vec")
        w_pool_landed = sem("w_pool_landed")
        mix_ssq = sem("mix_ssq")
        mix_rstd = sem("mix_rstd")
        res_landed = sem("res_landed")
        res_tiles = sem("res_tiles")
        stored = sem("stored")
        states_stored = sem("states_stored")
        gu_hi = sem("gu_hi")
        gate_lo = sem("gate_lo")
        up_lo = sem("up_lo")
        gu_used = sem("gu_used")
        dn_hi = sem("dn_hi")
        dn_lo = sem("dn_lo")
        dn_used = sem("dn_used")
        silu_ready = sem("silu_ready")
        g_ready = sem("g_ready")
        g_hi_ready = sem("g_hi_ready")
        g_lo_ready = sem("g_lo_ready")
        ada_landed = [sem(f"ada_landed{i}") for i in range(ADA_RAW)]
        w_landed = [sem(f"w_landed{i}") for i in range(RING)]
        gu_landed = [sem(f"gu_landed{i}") for i in range(4)]
        dn_landed = [sem(f"dn_landed{i}") for i in range(2)]

        x_v = x_all.rearrange("(n p) d -> p n d", p=P)
        x1_v = x1_all.rearrange("(n p) d -> p n d", p=P)
        y_v = y_all.rearrange("(n p) d -> p n d", p=P)

        def sequence(b):
            return SEQ_FIRST if is_first(b) else SEQ_LAST if is_last(b) else SEQ

        def group_base(b):
            return KD + ROT + GROUPS * b

        def group(b, name):
            if isinstance(name, int) and name < ROT:
                assert is_first(b)
                return KD + name
            return group_base(b) + sequence(b).index(name)

        def bank_of(b, name):
            if isinstance(name, int) and name < ROT:
                return name % 2
            seq = sequence(b)
            at = seq.index(name)
            return (at + (AGAIN in seq and at >= seq.index(AGAIN))) % 2

        WORK_A = group(NB - 1, "var") + 1

        def full_count(b, name):
            names = [x for x in NOT_PROJECTED if x in sequence(b)]
            return KD + len(NOT_PROJECTED) * b + (names.index(name) + 1)

        FULL_A = full_count(NB - 1, "var")

        A = ExitStack()
        mod_scope = ExitStack()
        con_a = sb("con_a", [P, E_END], scope=A)
        c_sb = sb("c_sb", [P, KD, ROWS], scope=A)
        c_s = sb("c_s", [P, KD, ROWS], scope=A)
        gate1 = sb("gate1", [P, D], scope=A)
        gate1_first = sb("gate1_first", [P, D], scope=A)
        mod = sb("mod", [MOD_K, 6 * D], scope=mod_scope)
        c_hl = sb("c_hl", [P, KD, P], F32R, scope=mod_scope)
        mod_scope.close()
        y_hi = sb("y_hi", [P, NMIX, N], F32R, scope=A)
        y_lo = sb("y_lo", [P, NMIX, N], F32R, scope=A)
        wsum = sb("wsum", [P, 2, PAST + N], scope=A)
        w_pl = sb("w_pl", [P, NPOOL, P], scope=A)
        pr = sb("pr", [P, 15, N], scope=A)
        xa = sb("xa", [P, NPOOL, PAST + N], scope=A)
        u = sb("u", [P, NCONV, HIST + N], scope=A)
        su = sb("su", [P, NSC, SHIST + N], scope=A)
        xa_s = sb("xa_s", [P, NPOOL, SEQS, PAST + STEPS], scope=A)
        u_s = sb("u_s", [P, NCONV, SEQS, HIST + STEPS], scope=A)
        su_s = sb("su_s", [P, NSC, SEQS, SHIST + STEPS], scope=A)
        A.close()
        pr_rows = pr[:, :, :].rearrange("p j n -> p (j n)")
        ada_raw = [raw[:, n, :] if n < ADA_RING else pr_rows[:, (n - ADA_RING) * D:(n - ADA_RING + 1) * D]
                   for n in range(ADA_RAW)]
        ones = con_a[:, E_ONES:E_ONES + P]
        B = ExitStack()
        g_hi = sb("g_hi", [P, NF, N], F32R, scope=B)
        g_lo = sb("g_lo", [P, NF, N], F32R, scope=B)
        s_buf = sb("s_buf", [P, 2, N], scope=B)
        g_f = sb("g_f", [P, 2, N], scope=B)
        raw5 = sb("raw5", [P, D], scope=B)
        whi5 = sb("whi5", [P, D], F32R, scope=B)
        wlo5 = sb("wlo5", [P, D], F32R, scope=B)
        B.close()
        dn_raw = [raw[:, 4, :], raw5[:, :]] + [raw[:, i, :] for i in range(4)]
        dn_whi = [whi[:, 4, :], whi5[:, :]] + [whi[:, i, :] for i in range(4)]
        dn_wlo = [wlo[:, 4, :], wlo5[:, :]] + [wlo[:, i, :] for i in range(4)]

        def dn_slot(b, k):
            return k % 6 if is_last(b) else k % 2

        def dn_before(b, k):
            return k - 6 if is_last(b) and k >= 6 else k - 2


        def tiles_before(q, in_b):
            return TB * q + (TILES - TB * NB if in_b else 0)

        def res_count(r, t):
            if isinstance(r, int) and r < NB:
                return TB * (r + 1) + (t + 1 if t is not None else tiles_of(r))
            return TB * (r - NB) + (TB + TILES + (t + 1 if t is not None else
                                             tiles_of(r - NB) if isinstance(r, int) else TB))

        def chan(ap):
            return ap.rearrange("p (k m) -> p k m", k=KD)

        def pslot(kind, j):
            return pr[:, SLOT[kind] + j, :]

        def zsq(j):
            return pslot(*(("c", 1), ("c", 2), ("b", 1))[j])

        def y_src(i):
            return pslot(*Y[i])

        def mix_ps(t):
            return ps[:, 2 + 2 * t:4 + 2 * t, :].rearrange("p a n -> p (a n)")

        def norm_group(q, k):
            if isinstance(q, int) and q == 0:
                return k
            if isinstance(q, int) and q < NB:
                return group(q - 1, f"t{k}")
            return WORK_A + KD * (q - NB) + k

        def norm_full(q, k):
            if isinstance(q, int) and q == 0:
                return k + 1
            if isinstance(q, int) and q < NB:
                return full_count(q - 1, f"t{k}")
            return FULL_A + KD * (q - NB) + k + 1

        def last_unit_in(s):
            return TOTAL - 1 - (TOTAL - 1 - s) % RING

        block = ctx.enter_context(nc.Block())

        @block.sync
        def _(sp):
            sp.dma_start(c_sb[:, :, :], c_all).then_inc(c_landed, 16)
            def one_tile(src, first, t):
                return src[:, bass.ds(first + t, 1), :].rearrange("p a d -> p (a d)")

            def load_ada(n):
                sp.dma_start(ada_raw[n % ADA_RAW], w_ada[n]).then_inc(ada_landed[n % ADA_RAW], 16)

            for n in range(ADA_RING):
                load_ada(n)
            sp.dma_start(con[:, :], consts).then_inc(const_landed, 16)
            sp.dma_start(con_a[:, :], consts_a).then_inc(const_landed, 16)
            sp.dma_start(col[:, :], cols).then_inc(const_landed, 16)
            for n in range(ADA_RING, ADA_FIRST):
                if n == KD:
                    for t in range(TB):
                        sp.dma_start(xt[:, t, :], x_v[:, t, :]).then_inc(x_landed, 16)
                    sp.dma_start(mod[2 * ROWS:MOD_K, :], b_ada).then_inc(bias_landed, 16)
                if n >= ADA_RAW:
                    sp.wait_ge(ada_lo, n - ADA_RAW + 1)
                load_ada(n)

            def load_x(src, first, nt):
                for t in range(nt):
                    sp.dma_start(xt[:, t, :], one_tile(src, first, t)).then_inc(x_landed, 16)

            def load_res(src, first, t):
                sp.dma_start(xr[:, t, :], one_tile(src, first, t)).then_inc(res_landed, 16)

            def load_w(b, pos, src):
                n, s = unit(b, pos), slot(b, pos)
                if not isinstance(n, int) or n >= RING:
                    last = n - RING
                    sp.wait_ge(w_lo_vec if by_vector(last) else w_lo, lo_count(last))
                elif s < ADA_RING:
                    sp.wait_ge(ada_lo, ADA_RAW + s + 1)
                sp.dma_start(raw[:, s, :], src).then_inc(w_landed[s], 16)

            for j in range(NIN):
                load_w(0, 3 * j, w_mix[j])
                if j < NIN - 1:
                    for i in range(2):
                        load_w(0, 3 * j + 1 + i, w_ada[ADA_FIRST + 2 * j + i])
                if j == 1:
                    for i in range(2):
                        sp.dma_start(xr[:, i, :], gpost[i:i + 1, :].to_broadcast([P, D])).then_inc(gpost_landed, 16)
                    for c in range(NPOOL):
                        sp.dma_start(xa_s[:, c, :, 0:PAST], st_pool[:, c]).then_inc(state_landed, 16)
                    for c in range(NCONV):
                        sp.dma_start(u_s[:, c, :, 0:HIST], st_conv[:, c]).then_inc(state_landed, 16)
                    for c in range(NSC):
                        sp.dma_start(su_s[:, c, :, 0:SHIST], st_sconv[:, c]).then_inc(state_landed, 16)
                if j == 6:
                    sp.wait_ge(work_full, KD)
                    load_x(x_v, TB, TB)
            AHEAD = 12
            for j in range(RING - 1):
                load_w(1, j, w_mix[j])
            sp.wait_ge(w_pool_zeroed, 1)
            for g in range(len(WINDOWS)):
                h = 64 * (g % 2)
                sp.dma_start(w_pl[h:h + 64, g // 2, h:h + 64], w_pool[g]).then_inc(w_pool_landed, 16)
            for j in range(RING - 1, AHEAD):
                load_w(1, j, w_mix[j])

            def mixer_loads(b, nt_next):
                for j in range(AHEAD, UNITS):
                    load_w(b, j, w_mix[j])
                    if j in (12, 13, 14)[0:nt_next or TB]:
                        t = j - 12
                        if t == 0:
                            if nt_next or is_last(b):
                                sp.wait_ge(work_full, full_count(b - 1, "t7"))
                            if is_last(b):
                                sp.wait_ge(stored, 16)
                        rows, tile0 = (x1_v, 0) if is_last(b) else (x_v, TB * b + TB)
                        sp.dma_start(xt[:, t, :], one_tile(rows, tile0, t)).then_inc(x_landed, 16)
                    if j in (16, 18, 20):
                        t = (j - 16) // 2
                        if t == 0:
                            if isinstance(b, int) and b == 1:
                                sp.wait_ge(res_tiles, TB)
                            else:
                                sp.wait_ge(stored, 16 * (b - 1))
                        load_res(x_v, TB * b - TB, t)
                for j in range(NMIX if is_last(b) else AHEAD):
                    load_w(b + 1, j, w_mix[NIN + j] if is_last(b) else w_mix[j])
                sp.wait_ge(res_tiles, TB * (b + 1))
                sp.dma_start(x1_v[:, bass.ds(TB * b - TB, TB), :], xr[:, :, :]).then_inc(stored, 16)

            mixer_loads(1, TB)
            with sp.Fori(2, NB - 2) as b:
                mixer_loads(b, TB)
            mixer_loads(NB - 2, LAST_TB)
            mixer_loads(NB - 1, 0)

            last_n = LAST_TB * P
            sp.wait_ge(z_ready, NCONV * NB)
            sp.wait_ge(pooled_ready, NPOOL * NB)
            sp.wait_ge(yc_ready, NSC * NB)
            for c in range(NPOOL):
                sp.dma_start(o_pool_p[:, c], xa[:, c, last_n:last_n + PAST]).then_inc(states_stored, 16)
                sp.dma_start(o_pool_s[:, c], xa_s[:, c, :, STEPS:]).then_inc(states_stored, 16)
            for j in range(NCONV):
                sp.dma_start(o_conv_p[:, j], u[:, j, last_n:last_n + HIST]).then_inc(states_stored, 16)
                sp.dma_start(o_conv_s[:, j], u_s[:, j, :, STEPS:]).then_inc(states_stored, 16)
            for j in range(NSC):
                sp.dma_start(o_sconv_p[:, j], su[:, j, last_n:last_n + SHIST]).then_inc(states_stored, 16)
                sp.dma_start(o_sconv_s[:, j], su_s[:, j, :, STEPS:]).then_inc(states_stored, 16)

            sp.wait_ge(stored, 16 * (NB - 1))
            for t in range(LAST_TB):
                load_res(x_v, TB * (NB - 1), t)
            for i in range(4):
                sp.wait_ge(w_lo, lo_count(last_unit_in(i)))
                sp.dma_start(raw[:, i, :], w_gu[i]).then_inc(gu_landed[i], 16)
            sp.wait_ge(w_lo, lo_count(TOTAL - 1))

            def load_gu(b, m, par):
                sp.wait_ge(gate_lo, NF * b + m - 1)
                sp.dma_start(raw[:, 2 * par, :], w_gu[2 * m]).then_inc(gu_landed[2 * par], 16)
                sp.wait_ge(up_lo, NF * b + m - 1)
                sp.dma_start(raw[:, 2 * par + 1, :], w_gu[2 * m + 1]).then_inc(gu_landed[2 * par + 1], 16)

            def load_dn(b, k):
                s = dn_slot(b, k)
                if is_last(b) and 2 <= k < 6:
                    sp.wait_ge(up_lo if k % 2 else gate_lo, NF * b + NF - 1 + (k - 2) // 2)
                elif not (is_first(b) and k < 2):
                    sp.wait_ge(dn_lo, NF * b + dn_before(b, k) + 1)
                sp.dma_start(dn_raw[s], w_dn[k]).then_inc((dn_landed + gu_landed)[s], 16)

            def ffn_loads(b, nt_next):
                nt_prev = LAST_TB if isinstance(b, int) and b == 0 else TB
                nt = tiles_of(b)
                with sp.Fori(1, NF // 4 + 1) as i:
                    for par in range(2):
                        load_gu(b, 2 * i + par, par)
                sp.wait_ge(res_tiles, res_count(b + NB - 1, None))
                if isinstance(b, int) and b == 0:
                    sp.dma_start(x1_v[:, TB * (NB - 1):TILES, :], xr[:, 0:LAST_TB, :]).then_inc(stored, 16)
                    sp.wait_ge(states_stored, 16 * 2 * NMIX)
                    sp.wait_ge(w_used, TOTAL)
                else:
                    sp.dma_start(y_v[:, bass.ds(TB * b - TB, TB), :], xr[:, :, :]).then_inc(stored, 16)
                load_dn(b, 0)
                load_dn(b, 1)
                if nt_next:
                    sp.wait_ge(work_full, norm_full(NB + b, KD - 1))
                    load_x(x1_v, TB * b + TB, nt_next)
                with sp.Fori(NF // 4 + 1, NF // 2) as i:
                    for par in range(2):
                        load_gu(b, 2 * i + par, par)
                for k in range(2, NF):
                    if k == 6:
                        sp.wait_ge(stored, 16 * NB + 16 * b)
                    if k in (6, 8, 10)[0:nt]:
                        load_res(x1_v, TB * b, (k - 6) // 2)
                    load_dn(b, k)
                    if k == 11 and nt_next:
                        for i in range(4):
                            sp.wait_ge(up_lo if i % 2 else gate_lo, NF * b + NF - 1 + i // 2)
                            sp.dma_start(raw[:, i, :], w_gu[i]).then_inc(gu_landed[i], 16)

            ffn_loads(0, TB)
            with sp.Fori(1, NB - 2) as b:
                ffn_loads(b, TB)
            ffn_loads(NB - 2, LAST_TB)
            ffn_loads(NB - 1, 0)
            sp.wait_ge(res_tiles, TB + 2 * TILES)
            sp.dma_start(y_v[:, TB * (NB - 1):TILES, :], xr[:, 0:LAST_TB, :]).then_inc(stored, 16)
            sp.wait_ge(stored, 16 * 2 * NB)

        @block.tensor
        def _(pe):
            def mm(out, lhsT, rhs, start, stop):
                return nc.tensor.matmul(out, lhsT, rhs, start=start, stop=stop, skip_group_check=True)

            def ada_unit(k, s, pair):
                for h in range(2):
                    w = slice(512 * h, 512 * h + 512)
                    out = ps[:, 2 + 2 * pair + h, :]
                    mm(out, c_hl[:, k, :], whi[:, s, w], k == 0, False)
                    last = mm(out, c_hl[:, k, :], wlo[:, s, w], False, k == KD - 1)
                return last

            def ada_columns(first, bank):
                for i in range(2):
                    for k in range(KD):
                        c0, o = (first + i) * D + k * P, (i * KD + k) * MOD_K
                        last = nc.tensor.transpose(ps[:, bank, o:o + MOD_K], mod[:, c0:c0 + P], ident[0:MOD_K, 0:MOD_K])
                last.then_inc(cols_full, 1)

            def gate_rows(i):
                g, e = (2, 5)[i // 2], (E_SELP, E_SELS)[i % 2]
                if i >= 2:
                    pe.wait_ge(mod_ready, 4 + i - 1)
                for h in range(2):
                    c0 = g * D + 512 * h
                    last = mm(ps[:, 2 + 2 * (i % 2) + h, :], con_a[0:MOD_K, e:e + P], mod[:, c0:c0 + 512], True, True)
                last.then_inc(gates_full, 1)

            pe.wait_ge(c_ready, 1)
            for g in range(2):
                for k in range(KD):
                    pe.wait_ge(ada_lo, KD * g + k + 1)
                    ada_unit(k, k % ADA_RING, g).then_inc(ada_used, 1)
            pe.wait_ge(bias_landed, 16)
            pe.wait_ge(const_landed, 48)
            pe.wait_ge(ada_read, 2)
            ada_columns(0, 0)

            def transposes(q, k, nt, bank, wait):
                if k == 0:
                    pe.wait_ge(xn_ready, q + 1)
                if wait is not None:
                    pe.wait_ge(work_read, wait)
                for t in range(nt):
                    last = nc.tensor.transpose(ps[:, bank, t * P:(t + 1) * P], xt[:, t, k * P:(k + 1) * P], ident)
                last.then_inc(work_full, 1)

            pe.wait_ge(mod_ready, 2)
            for k in range(KD):
                transposes(0, k, TB, k % 2, k - 1 if k >= 2 else None)

            def wait_unit(n):
                pe.wait_ge(w_lo_vec if by_vector(n) else w_lo, lo_count(n))

            def project(b, j, at=None):
                n, s, nt = unit_in(b, j), slot(b, pos_in(b, j)), tiles_of(b)
                at = at or (b, j)
                pe.wait_ge(work_read, group(*at) - 1)
                wait_unit(n)
                if j == 0 and not is_first(b):
                    pe.wait_ge(h_lo_ready, KD * (b + 1))
                w_h, w_l = chan(whi[:, s, :]), chan(wlo[:, s, :])
                out = ps[:, bank_of(*at), 0:nt * P]
                for k in range(KD):
                    if j == 0 and is_first(b):
                        pe.wait_ge(h_lo_ready, k + 1)
                    mm(out, w_h[:, k, :], h_hi[:, k, 0:nt * P], k == 0, False)
                    mm(out, w_h[:, k, :], h_lo[:, k, 0:nt * P], False, False)
                    last = mm(out, w_l[:, k, :], h_hi[:, k, 0:nt * P], False, k == KD - 1)
                last.then_inc(w_used, 1)

            def project_first(j):
                project(0, j)
                if j == NIN - 1:
                    return
                for i in range(2):
                    n, k, g = 3 * j + 1 + i, (2 * j + i) % KD, j // 4
                    if k == 0 and g == 3:
                        pe.wait_ge(ada_read, 3)
                    elif k == 0 and g < 2:
                        pe.wait_ge(ada_read, g + 1)
                    wait_unit(n)
                    ada_unit(k, n % RING, g % 3).then_inc(w_used, 1)

            def token_major(a_hi, a_lo, b_hi, b_lo, k, nk, nt, left=None):
                for t in range(nt):
                    if left is not None:
                        pe.wait_ge(res_tiles, left + t + 1)
                    c = slice(t * P, (t + 1) * P)
                    for st, mv, first, end in ((a_hi, b_hi, k == 0, False), (a_hi, b_lo, False, False),
                                               (a_lo, b_hi, False, k == nk - 1)):
                        for h in range(2):
                            w = slice(512 * h, 512 * h + 512)
                            last = mm(ps[:, 2 + 2 * t + h, :], st[:, k, c], mv[:, w], first, end)
                return last

            def mix_out(b, k):
                n, s = unit_out(b, k), slot(*at_out(b, k))
                if k < NY1:
                    pe.wait_ge(y_lo_ready, NY1 * b + (k + 1))
                else:
                    pe.wait_ge(yb_lo_ready, NCONV * b + (k + 1 - NY1))
                wait_unit(n)
                token_major(y_hi, y_lo, whi[:, s, :], wlo[:, s, :], k, NMIX, tiles_of(b),
                            None if k else TB * b).then_inc(w_used, 1)

            def stage_group(b, name, nt_next):
                nt = tiles_of(b)
                out = ps[:, bank_of(b, name), 0:nt * P]
                if name[0] == "t":
                    transposes(b + 1, int(name[1]), nt_next, bank_of(b, name), group(b, name) - (name != AGAIN))
                    return
                pe.wait_ge(work_read, group(b, name) - 1)
                if name == "mean":
                    pe.wait_ge(z_ready, NCONV * (b + 1))
                    for j in range(NCONV):
                        last = mm(out, ones, pslot("a", j)[:, 0:nt * P], j == 0, j == NCONV - 1)
                elif name == "var":
                    pe.wait_ge(zsq_ready, NCONV * (b + 1))
                    for j in range(NCONV):
                        last = mm(out, ones, zsq(j)[:, 0:nt * P], j == 0, j == NCONV - 1)
                else:
                    c = int(name[-1])
                    pe.wait_ge(pooled_ready, NPOOL * b + (c + 1))
                    last = mm(out, w_pl[:, c, :], pslot("g", c)[:, 0:nt * P], True, True)
                last.then_inc(work_full, 1)

            def mixer_block(b, nt_next):
                for j in range(ROT, NIN):
                    if is_first(b):
                        project_first(j)
                    else:
                        project(b, j)
                if is_first(b):
                    pe.wait_ge(ada_read, 6)
                    ada_columns(3, 7)
                    gate_rows(0)
                    gate_rows(1)
                    for name in T_GROUPS:
                        stage_group(b, name, nt_next)
                    gate_rows(2)
                    gate_rows(3)
                    for j in range(ROT):
                        project(b + 1, j, (b, f"n{j}"))
                    pe.wait_ge(w_pool_landed, 16 * len(WINDOWS))
                    for name in POOL_GROUPS + ["mean", "var"]:
                        stage_group(b, name, nt_next)
                    return
                for k in range(NMIX):
                    mix_out(b - 1, k)
                    for name in after_chunk(b, k):
                        stage_group(b, name, nt_next)
                if nt_next:
                    for j in range(ROT):
                        project(b + 1, j, (b, f"n{j}"))
                    stage_group(b, "var", nt_next)

            for j in range(ROT):
                project_first(j)
            mixer_block(0, TB)
            with pe.Fori(1, NB - 2) as b:
                mixer_block(b, TB)
            mixer_block(NB - 2, LAST_TB)
            mixer_block(NB - 1, 0)
            for k in range(2):
                transposes(NB, k, TB, (k + 1) % 2, WORK_A + k - 1)
            for k in range(NMIX):
                mix_out(NB - 1, k)
                if k + 2 < KD:
                    transposes(NB, k + 2, TB, (k + 3) % 2, WORK_A + k + 1)

            def gate_up(b, m, par, nt):
                for i in range(2):
                    s = 2 * par + i
                    pe.wait_ge(gate_lo if i == 0 else up_lo, NF * b + m + 1)
                    w_h, w_l = chan(whi[:, s, :]), chan(wlo[:, s, :])
                    out = ps[:, s, 0:nt * P]
                    for k in range(KD):
                        mm(out, w_h[:, k, :], h_hi[:, k, 0:nt * P], k == 0, False)
                        mm(out, w_h[:, k, :], h_lo[:, k, 0:nt * P], False, False)
                        last = mm(out, w_l[:, k, :], h_hi[:, k, 0:nt * P], False, k == KD - 1)
                    last.then_inc(gu_used, 1)

            def ffn_block(b, nt_next):
                nt = tiles_of(b)
                pe.wait_ge(h_lo_ready, KD * NB + KD * (b + 1))
                pe.wait_ge(work_read, norm_group(NB + b, KD - 1) + 1)
                gate_up(b, 0, 0, nt)
                pe.wait_ge(res_tiles, res_count(b + NB - 1, 0))
                gate_up(b, 1, 1, nt)
                with pe.Fori(1, NF // 2) as i:
                    for par in range(2):
                        pe.wait_ge(silu_ready, NF * b + 2 * i + par - 1)
                        pe.wait_ge(g_ready, NF * b + 2 * i + par - 1)
                        gate_up(b, 2 * i + par, par, nt)
                pe.wait_ge(silu_ready, NF * b + NF)
                pe.wait_ge(g_ready, NF * b + NF)
                pe.wait_ge(res_tiles, res_count(b + NB - 1, None))
                for k in range(NF):
                    pe.wait_ge(dn_lo, NF * b + k + 1)
                    pe.wait_ge(g_lo_ready, NF * b + k + 1)
                    token_major(g_hi, g_lo, dn_whi[dn_slot(b, k)], dn_wlo[dn_slot(b, k)], k, NF, nt).then_inc(dn_used, 1)
                    c = (k - 4) // 2
                    if nt_next and k % 2 == 0 and 0 <= c < KD:
                        q = NB + 1 + b
                        transposes(q, c, nt_next, c % 2, None if c < 2 else norm_group(q, c) - 1)

            ffn_block(0, TB)
            with pe.Fori(1, NB - 2) as b:
                ffn_block(b, TB)
            ffn_block(NB - 2, LAST_TB)
            ffn_block(NB - 1, 0)

        @block.scalar
        def _(act):
            own = Steps(act_step)

            act.wait_ge(c_landed, 16)
            nc.scalar.activation(c_s[:, :, :], c_sb[:, :, :], ACT.Silu).then_inc(silu_c, 1)
            act.wait_ge(silu_c, 1)
            act.wait_ge(pad_zeroed, 1)
            nc.scalar.activation(c_hl[:, :, 0:ROWS], c_s[:, :, :], ACT.Copy).then_inc(c_hi_ready, 1)

            def ada_evacuate(g, pair):
                nc.scalar.activation(mod[0:2 * ROWS, g * D:(g + 1) * D], mix_ps(pair)[0:2 * ROWS, :], ACT.Copy)\
                  .then_inc(ada_read, 1)

            def ada_group(g):
                for k in range(KD):
                    n = KD * g + k
                    act.wait_ge(ada_landed[n % ADA_RAW], 16 * (n // ADA_RAW + 1))
                    if n >= ADA_RING:
                        act.wait_ge(ada_used, n - ADA_RING + 1)
                    nc.scalar.activation(whi[:, n % ADA_RING, :], ada_raw[n % ADA_RAW], ACT.Copy).then_inc(ada_hi, 1)

            def split_unit(b, pos):
                n, s = unit(b, pos), slot(b, pos)
                act.wait_ge(w_landed[s], landed(b, pos))
                if isinstance(n, int) and n < RING:
                    if s < ADA_RING:
                        act.wait_ge(ada_used, ADA_FIRST - ADA_RING + s + 1)
                else:
                    act.wait_ge(w_used, n - RING + 1)
                nc.scalar.activation(whi[:, s, :], raw[:, s, :], ACT.Copy).then_inc(w_hi, 1)

            LEAD = RING - 1

            def split_ahead(b, pos):
                n = pos + LEAD - stream_len(b)
                if n < 0:
                    split_unit(b, pos + LEAD)
                elif not (isinstance(b, int) and b == NB):
                    split_unit(b + 1, n)

            def mean_squares(src, dst, nt, before, done):
                for t in range(nt):
                    mean_square(src(t), dst, t, before, done)

            def mean_square(src, dst, t, before, done):
                if t:
                    act.wait_ge(done, before + t)
                nc.scalar.activation(junk[:, :], src, ACT.Square, scale=D ** -0.5, accum_out=dst[:, t:t + 1])\
                  .then_inc(done, 1)

            def x_square(q, t, nt, in_b):
                before = tiles_before(q, in_b)
                if t == 0:
                    act.wait_ge(x_landed, 16 * (before + nt))
                mean_square(xt[:, t, :], ssq_x, t, before, x_ssq)

            def x_squares(q, nt, in_b):
                for t in range(nt):
                    x_square(q, t, nt, in_b)

            def mix_squares(q, nt, in_b):
                mean_squares(mix_ps, ssq_m, nt, tiles_before(q, in_b), mix_ssq)

            def x_normalise_tile(q, t, nt):
                if t == 0:
                    act.wait_ge(x_rstd, q + 1)
                i = nc.scalar.activation(xt[:, t, :], xt[:, t, :], ACT.Copy, scale=rstd_x[:, t:t + 1])
                if t == nt - 1:
                    i.then_inc(xn_ready, 1)

            def x_normalise(q, nt):
                for t in range(nt):
                    x_normalise_tile(q, t, nt)

            def modulate(q, k, nt, bank, ph, full, free, sample=False):
                act.wait_ge(work_full, full)
                if free is not None:
                    act.wait_ge(h_lo_ready, free)
                c = P if sample else 0
                if sample:
                    act.wait_ge(sample_mod, KD * (q // NB) + k + 1)
                nc.scalar.activation(h_f[:, k % 2, c:nt * P], ps[:, bank, c:nt * P], ACT.Identity,
                                     scale=shsc[:, 2 * ph + 1, k, 0:1], bias=shsc[:, 2 * ph, k, 0:1])\
                  .then_inc(work_read, 1)

            def h_split(k, nt, read):
                act.wait_ge(work_read, read)
                nc.scalar.activation(h_hi[:, k, 0:nt * P], h_f[:, k % 2, 0:nt * P], ACT.Copy).then_inc(h_hi_ready, 1)

            ada_group(0)
            x_squares(0, TB, False)
            ada_group(1)
            act.wait_ge(ada_used, KD)
            ada_evacuate(0, 0)
            x_normalise(0, TB)
            act.wait_ge(ada_used, 2 * KD)
            ada_evacuate(1, 1)
            for j in range(LEAD):
                split_unit(0, j)
            act.wait_ge(mod_ready, 2)
            for k in range(KD):
                modulate(0, k, TB, k % 2, 0, k + 1, k - 1 if k >= 2 else None, True)
                h_split(k, TB, k + 1)

            def evacuate(b, j, at=None):
                kind, c = ORDER[j]
                nt = tiles_of(b)
                act.wait_ge(w_used, unit_in(b, j) + 1)
                if not is_first(b):
                    if kind == "a":
                        act.wait_ge(yb_lo_ready, NCONV * b + (c + 1 - NCONV))
                    elif (kind, c) in Y:
                        act.wait_ge(y_lo_ready, NY1 * b + (Y.index((kind, c)) + 1 - NY1))
                src = ps[:, bank_of(*(at or (b, j))), 0:nt * P]
                if kind != "x":
                    f = ACT.Sigmoid if kind == "g" else ACT.Copy
                    nc.scalar.activation(pslot(kind, c)[:, 0:nt * P], src, f).then_inc(work_read, 1)
                elif is_first(b):
                    own.step(nc.scalar.activation(
                        xa_s[:, c, :, PAST:], src[:, 0:P].rearrange("p (s t) -> p s t", s=SEQS), ACT.Copy))
                    nc.scalar.activation(xa[:, c, PAST:PAST + (nt - 1) * P], src[:, P:], ACT.Copy).then_inc(work_read, 1)
                else:
                    nc.scalar.activation(xa[:, c, PAST:PAST + nt * P], src, ACT.Copy).then_inc(work_read, 1)

            def y_split(b, i):
                if not is_first(b):
                    act.wait_ge(w_used, unit_out(b - 1, i) + 1)
                else:
                    act.wait_ge(gates_full, 4)
                kind, c = Y[i]
                if kind == "g":
                    act.wait_ge(work_read, group(b, f"pool{c}") + 1)
                elif kind == "h":
                    act.wait_ge(yc_ready, NSC * b + (c + 1))
                else:
                    act.wait_ge(yb_ready, NCONV * b + (c + 1))
                w = slice(0, tiles_of(b) * P)
                nc.scalar.activation(y_hi[:, i, w], y_src(i)[:, w], ACT.Copy).then_inc(y_hi_ready, 1)

            def stage_group(b, name, nt_next):
                nt = tiles_of(b)
                bank = bank_of(b, name)
                src = ps[:, bank, 0:nt * P]
                if name[0] == "t":
                    k = int(name[1])
                    if k == 0:
                        act.wait_ge(w_used, unit_in(b, NIN - 1) + 1)
                    modulate(None, k, nt_next, bank, 0, full_count(b, name), KD * (b + 1) + (k - 1))
                    return
                act.wait_ge(work_full, full_count(b, name))
                if name == "mean":
                    nc.scalar.activation(pslot("g", 2)[:, 0:nt * P], src, ACT.Copy, scale=1.0 / (NCONV * P))\
                      .then_inc(work_read, 1)
                elif name == "var":
                    r, v = pslot("b", 2)[:, 0:nt * P], pslot("g", 2)[:, 0:nt * P]
                    nc.scalar.activation(v, src, ACT.Identity, scale=1.0 / (NCONV * P), bias=eps)\
                      .then_inc(work_read, 1)
                    act.wait_ge(work_read, group(b, name) + 1)
                    at = own.step(nc.scalar.activation(r, v, ACT.Ln))
                    act.wait_ge(act_step, at)
                    nc.scalar.activation(r, r, ACT.Exp, scale=-0.5).then_inc(seed_ready, 1)
                else:
                    c = int(name[-1])
                    nc.scalar.activation(pslot("g", c)[:, 0:nt * P], src, ACT.Copy,
                                         scale=col[:, Q_SP + c:Q_SP + c + 1]).then_inc(work_read, 1)

            def squares_of_centred(b):
                for j in range(NCONV):
                    w = slice(0, tiles_of(b) * P)
                    act.wait_ge(zc_ready, NCONV * b + (j + 1))
                    nc.scalar.activation(zsq(j)[:, w], pslot("a", j)[:, w], ACT.Square).then_inc(zsq_ready, 1)

            def mix_ready_squares(b):
                act.wait_ge(w_used, unit_out(b - 1, NMIX - 1) + 1)
                mix_squares(b - 1, TB, False)

            def conformer_out(b):
                w = slice(0, tiles_of(b) * P)
                for j in range(NCONV):
                    act.wait_ge(zn_ready, NCONV * b + (j + 1))
                    nc.scalar.activation(pslot("a", j)[:, w], pslot("a", j)[:, w], ACT.Silu,
                                         scale=col[:, Q_LG + j:Q_LG + j + 1],
                                         bias=col[:, Q_LB + j:Q_LB + j + 1]).then_inc(yb_ready, 1)
                for i in range(NY1, NMIX):
                    y_split(b, i)

            def ahead_first(j):
                split_ahead(0, 3 * j)
                evacuate(0, j)
                if j < NIN - 1:
                    split_ahead(0, 3 * j + 1)
                    split_ahead(0, 3 * j + 2)
                if j % 4 == 3:
                    act.wait_ge(w_used, 3 * j + 3)
                    ada_evacuate(2 + j // 4, (j // 4) % 3)

            def mixer_block(b, nt_next):
                for j in range(ROT + 1, NIN):
                    if is_first(b):
                        ahead_first(j)
                    else:
                        split_ahead(b, j)
                        evacuate(b, j)
                    if j == 10:
                        x_squares(b + 1, nt_next or TB, is_last(b))
                    if j == 13:
                        x_normalise(b + 1, nt_next or TB)
                def project_next(j):
                    split_ahead(b + 1, j)
                    evacuate(b + 1, j, (b, f"n{j}") if j < ROT else None)

                if is_first(b):
                    for name in T_GROUPS:
                        stage_group(b, name, nt_next)
                        h_split(int(name[1]), nt_next, group(b, name) + 1)
                    y_split(b, 0)
                    for j in range(ROT):
                        project_next(j)
                    for c, name in enumerate(POOL_GROUPS):
                        stage_group(b, name, nt_next)
                        y_split(b, 1 + c)
                    stage_group(b, "mean", nt_next)
                    y_split(b, 3)
                else:
                    for k in range(NMIX):
                        names = after_chunk(b, k)
                        for name in names:
                            stage_group(b, name, nt_next)
                            if name == "mean" and is_last(b):
                                squares_of_centred(b)
                        split_ahead(b, NIN + k)
                        for name in names:
                            if name[0] == "t":
                                h_split(int(name[1]), nt_next, group(b, name) + 1)
                        for i in splits_after(b, k):
                            y_split(b, i)
                    if is_last(b):
                        mix_ready_squares(b)
                        conformer_out(b)
                        return
                    project_next(0)
                squares_of_centred(b)
                y_split(b, 4)
                if not is_first(b):
                    mix_ready_squares(b)
                    project_next(1)
                stage_group(b, "var", nt_next)
                project_next(2)
                conformer_out(b)

            for j in range(ROT + 1):
                ahead_first(j)
            mixer_block(0, TB)
            own.enter_loop()
            with act.Fori(1, NB - 2) as b:
                own.in_loop(b - 1, ACT_STEPS_A)
                mixer_block(b, TB)
            own.leave_loop(NB - 3, ACT_STEPS_A)
            mixer_block(NB - 2, LAST_TB)
            mixer_block(NB - 1, 0)
            act.wait_ge(w_used, unit_in(NB - 1, NIN - 1) + 1)
            for k in range(KD):
                modulate(NB, k, TB, (k + 1) % 2, 1, FULL_A + k + 1, KD * NB + k - 1, True)
                h_split(k, TB, WORK_A + k + 1)
                if k < NMIX - LEAD:
                    split_ahead(NB, k)

            def split_dn(b, k):
                s = dn_slot(b, k)
                if is_last(b):
                    act.wait_ge((dn_landed + gu_landed)[s], 16 * (NF // 2) * (NB - 1 if s < 2 else NB) + 16 * (k // 6 + 1))
                else:
                    act.wait_ge(dn_landed[s], 16 * (NF // 2) * b + 16 * (k // 2 + 1))
                if is_last(b) and 2 <= k < 6:
                    act.wait_ge(gu_used, 2 * NF * b + 2 * NF - 4 + (k - 2) + 1)
                elif not (is_first(b) and k < 2):
                    act.wait_ge(dn_used, NF * b + dn_before(b, k) + 1)
                elif k == 0:
                    act.wait_ge(w_used, TOTAL)
                nc.scalar.activation(dn_whi[s], dn_raw[s], ACT.Copy).then_inc(dn_hi, 1)

            def hidden(b, m, par, nt, split):
                act.wait_ge(gu_used, 2 * NF * b + 2 * m + 1)
                nc.scalar.activation(s_buf[:, par, 0:nt * P], ps[:, 2 * par, 0:nt * P], ACT.Silu).then_inc(silu_ready, 1)
                split()
                act.wait_ge(g_ready, NF * b + m + 1)
                nc.scalar.activation(g_hi[:, bass.ds(m, 1), 0:nt * P].rearrange("p a n -> p (a n)"),
                                     g_f[:, par, 0:nt * P], ACT.Copy).then_inc(g_hi_ready, 1)

            def ffn_block(b, nt_next):
                nt = tiles_of(b)
                mix_nt = LAST_TB if isinstance(b, int) and b == 0 else TB

                def split_two_on(m, par, i_times=None):
                    count = 16 * (NF // 2) * b + (i_times + 32 if i_times is not None else 16 * (m // 2) + 32)
                    act.wait_ge(gu_landed[2 * par], count)
                    nc.scalar.activation(whi[:, 2 * par, :], raw[:, 2 * par, :], ACT.Copy).then_inc(gu_hi, 1)
                    act.wait_ge(gu_used, 2 * NF * b + 2 * m + 2)
                    act.wait_ge(gu_landed[2 * par + 1], count)
                    nc.scalar.activation(whi[:, 2 * par + 1, :], raw[:, 2 * par + 1, :], ACT.Copy).then_inc(gu_hi, 1)

                with act.Fori(0, NF // 2 - 1) as i:
                    for par in range(2):
                        hidden(b, 2 * i + par, par, nt, lambda: split_two_on(2 * i + par, par, 16 * i))
                for par in range(2):
                    hidden(b, NF - 2 + par, par, nt, lambda: split_dn(b, par))
                ahead = 5 if is_last(b) else 2
                for k in range(2, ahead):
                    split_dn(b, k)
                for k in range(NF):
                    if k + ahead < NF:
                        split_dn(b, k + ahead)
                    for t in {0: [0, 1], 1: [2]}.get(k, []):
                        if t < nt_next:
                            x_square(NB + 1 + b, t, nt_next, True)
                    for t in {2: [0], 3: [1, 2]}.get(k, []):
                        if t < nt_next:
                            x_normalise_tile(NB + 1 + b, t, nt_next)
                    c = (k - 4) // 2
                    if nt_next and k % 2 == 0 and 0 <= c < KD:
                        q = NB + 1 + b
                        if c == 0:
                            act.wait_ge(gu_used, 2 * NF * b + 2 * NF)
                        act.wait_ge(work_full, FULL_A + KD * (b + 1) + (c + 1))
                        act.wait_ge(h_lo_ready, KD * q + (c - 1))
                        nc.scalar.activation(h_f[:, c % 2, 0:nt_next * P], ps[:, c % 2, 0:nt_next * P], ACT.Identity,
                                             scale=shsc[:, 3, c, 0:1], bias=shsc[:, 2, c, 0:1]).then_inc(work_read, 1)
                    if nt_next and k % 2 and 0 <= (k - 5) // 2 < KD:
                        c = (k - 5) // 2
                        h_split(c, nt_next, WORK_A + KD * (b + 1) + c + 1)
                    if nt_next and k >= NF - 4:
                        s = k - (NF - 4)
                        act.wait_ge(gu_landed[s], 16 * (NF // 2) * (b + 1) + 16)
                        nc.scalar.activation(whi[:, s, :], raw[:, s, :], ACT.Copy).then_inc(gu_hi, 1)
                act.wait_ge(dn_used, NF * (b + 1))
                mix_squares(NB + b, nt, True)

            for s in range(4):
                act.wait_ge(gu_landed[s], 16)
                act.wait_ge(w_used, last_unit_in(s) + 1)
                nc.scalar.activation(whi[:, s, :], raw[:, s, :], ACT.Copy).then_inc(gu_hi, 1)
            act.wait_ge(w_used, TOTAL)
            mix_squares(NB - 1, LAST_TB, False)
            act.wait_ge(states_stored, 16 * 2 * NMIX)
            ffn_block(0, TB)
            own.enter_loop()
            with act.Fori(1, NB - 2) as b:
                own.in_loop(b - 1, ACT_STEPS_B)
                ffn_block(b, TB)
            own.leave_loop(NB - 3, ACT_STEPS_B)
            ffn_block(NB - 2, LAST_TB)
            ffn_block(NB - 1, 0)

        @block.gpsimd
        def _(pool):
            nc.gpsimd.memset(c_hl[:, :, :].bitcast(F32), 0.0).then_inc(pad_zeroed, 1)
            steps = Steps(pool_step)

            def rstd(ssq, out, t0, t1, done):
                w, n = slice(t0, t1), t1 - t0
                at = steps.step(nc.gpsimd.tensor_tensor(ssq[:, w], ssq[:, w], con[:, C_EPS:C_EPS + n], ALU.add))
                pool.wait_ge(pool_step, at)
                nc.gpsimd.tensor_tensor(out[:, w], ssq[:, w], con[:, C_NHALF:C_NHALF + n], ALU.pow)\
                  .then_inc(done, 1)

            def mix_rstds(q, nt, in_b):
                for t0, t1 in ((0, 1), (1, nt)):
                    pool.wait_ge(mix_ssq, tiles_before(q, in_b) + t1)
                    rstd(ssq_m, rstd_m, t0, t1, mix_rstd)

            def lo(b, pos):
                s = slot(b, pos)
                pool.wait_ge(w_hi, unit(b, pos) + 1)
                nc.gpsimd.tensor_tensor(wlo[:, s, :], raw[:, s, :], whi[:, s, :].bitcast(F32), ALU.subtract)\
                  .then_inc(w_lo, 1)

            LEAD = RING - 1

            def lo_ahead(b, pos):
                n = pos + LEAD - stream_len(b)
                if n >= 0:
                    if not (isinstance(b, int) and b == NB):
                        lo(b + 1, n)
                elif not by_vector(unit(b, pos + LEAD)):
                    lo(b, pos + LEAD)

            def h_rest(q, k, nt):
                pool.wait_ge(h_hi_ready, KD * q + (k + 1))
                nc.gpsimd.tensor_tensor(h_lo[:, k, 0:nt * P], h_f[:, k % 2, 0:nt * P],
                                        h_hi[:, k, 0:nt * P].bitcast(F32), ALU.subtract).then_inc(h_lo_ready, 1)

            def y_rest(b, i):
                w = slice(0, tiles_of(b) * P)
                pool.wait_ge(y_hi_ready, NMIX * b + (i + 1))
                nc.gpsimd.tensor_tensor(y_lo[:, i, w], y_src(i)[:, w], y_hi[:, i, w].bitcast(F32), ALU.subtract)\
                  .then_inc(y_lo_ready, 1)

            pool.wait_ge(const_landed, 48)
            pool.wait_ge(x_ssq, TB)
            rstd(ssq_x, rstd_x, 0, TB, x_rstd)
            for j in range(LEAD):
                if not by_vector(j):
                    lo(0, j)

            def ahead_first(j):
                lo_ahead(0, 3 * j)
                if j < NIN - 1:
                    lo_ahead(0, 3 * j + 1)
                    lo_ahead(0, 3 * j + 2)

            def mixer_block(b, nt_next):
                for j in range(ROT + 1, NIN):
                    if is_first(b):
                        ahead_first(j)
                    else:
                        lo_ahead(b, j)
                    if j == 11:
                        n = nt_next or TB
                        pool.wait_ge(x_ssq, tiles_before(b + 1, is_last(b)) + n)
                        rstd(ssq_x, rstd_x, 0, n, x_rstd)
                if is_first(b):
                    for k in range(KD):
                        h_rest(b + 1, k, nt_next)
                    pool.wait_ge(gates_full, 4)
                    nc.gpsimd.memset(w_pl[:, :, :], 0.0).then_inc(w_pool_zeroed, 1)
                    y_rest(b, 0)
                    for j in range(ROT):
                        lo_ahead(b + 1, j)
                    for i in range(1, 5):
                        y_rest(b, i)
                    lo_ahead(b + 1, 2)
                    return
                for k in range(NMIX):
                    lo_ahead(b, NIN + k)
                    for name in after_chunk(b, k):
                        if name[0] == "t":
                            h_rest(b + 1, int(name[1]), nt_next)
                    for i in splits_after(b, k):
                        y_rest(b, i)
                if nt_next:
                    lo_ahead(b + 1, 0)
                    y_rest(b, 4)
                mix_rstds(b - 1, TB, False)
                if nt_next:
                    lo_ahead(b + 1, 1)
                    lo_ahead(b + 1, 2)

            for j in range(ROT + 1):
                ahead_first(j)
            mixer_block(0, TB)
            steps.enter_loop()
            with pool.Fori(1, NB - 2) as b:
                steps.in_loop(b - 1, POOL_STEPS_A)
                mixer_block(b, TB)
            steps.leave_loop(NB - 3, POOL_STEPS_A)
            mixer_block(NB - 2, LAST_TB)
            mixer_block(NB - 1, 0)
            for k in range(KD):
                h_rest(NB, k, TB)
                if k < NMIX - LEAD:
                    lo_ahead(NB, k)

            def lo_gate(b, m, par):
                pool.wait_ge(gu_hi, 2 * NF * b + 2 * m + 1)
                nc.gpsimd.tensor_tensor(wlo[:, 2 * par, :], raw[:, 2 * par, :], whi[:, 2 * par, :].bitcast(F32),
                                        ALU.subtract).then_inc(gate_lo, 1)

            def ffn_block(b, nt_next):
                with pool.Fori(1, NF // 2) as i:
                    for par in range(2):
                        lo_gate(b, 2 * i + par, par)
                if nt_next:
                    pool.wait_ge(x_ssq, tiles_before(NB + 1 + b, True) + nt_next)
                    rstd(ssq_x, rstd_x, 0, nt_next, x_rstd)
                    for par in range(2):
                        lo_gate(b + 1, par, par)
                mix_rstds(NB + b, tiles_of(b), True)

            for par in range(2):
                lo_gate(0, par, par)
            mix_rstds(NB - 1, LAST_TB, False)
            ffn_block(0, TB)
            steps.enter_loop()
            with pool.Fori(1, NB - 2) as b:
                steps.in_loop(b - 1, POOL_STEPS_B)
                ffn_block(b, TB)
            steps.leave_loop(NB - 3, POOL_STEPS_B)
            ffn_block(NB - 2, LAST_TB)
            ffn_block(NB - 1, 0)

        @block.vector
        def _(dve):
            own = Steps(vec_step)

            def after(at):
                if at is not None:
                    dve.wait_ge(vec_step, at)

            tt = nc.vector.tensor_tensor
            stt = nc.vector.scalar_tensor_tensor

            dve.wait_ge(c_hi_ready, 1)
            tt(c_hl[:, :, ROWS:2 * ROWS], c_s[:, :, :], c_hl[:, :, 0:ROWS].bitcast(F32), ALU.subtract)\
                .then_inc(c_ready, 1)
            for n in range(ADA_FIRST):
                s = n % ADA_RING
                dve.wait_ge(ada_hi, n + 1)
                tt(wlo[:, s, :], ada_raw[n % ADA_RAW], whi[:, s, :].bitcast(F32), ALU.subtract).then_inc(ada_lo, 1)

            def columns(i, bank):
                dve.wait_ge(cols_full, i + 1)
                src = ps[:, bank, 0:2 * KD * MOD_K].rearrange("p (n m) -> p n m", m=MOD_K)
                dst = shsc[:, 2 * i:2 * i + 2, :, :].rearrange("p i k r -> p (i k) r")
                after(own.step(nc.vector.tensor_copy(dst, src[:, :, 0:ROWS])))
                after(own.step(tt(dst, dst, src[:, :, ROWS:2 * ROWS], ALU.add)))
                tt(dst, dst, src[:, :, 2 * ROWS:MOD_K].to_broadcast([P, 2 * KD, ROWS]), ALU.add).then_inc(mod_ready, 1)
                g0 = (Q_G1, Q_G2)[i]
                dve.wait_ge(mod_ready, (1, 3)[i])
                stt(shsc[:, 2 * i + 1, :, :], shsc[:, 2 * i + 1, :, :], 1.0,
                    col[:, g0:g0 + KD].unsqueeze(2).to_broadcast([P, KD, ROWS]), ALU.add, ALU.mult)\
                    .then_inc(mod_ready, 1)

            def gate(i):
                dve.wait_ge(gates_full, i + 1)
                dst = (gate1, gate1_first, gate2, gate2_first)[i]
                made = tt(dst[:, :], mix_ps(i % 2), xr[:, i // 2, :], ALU.mult)
                if i < 3:
                    made.then_inc(mod_ready, 1)
                else:
                    made.then_inc(res_tiles, TB)

            dve.wait_ge(const_landed, 48)
            columns(0, 0)

            def seqs(ap):
                return ap.rearrange("p (s t) -> p s t", s=SEQS)

            def modulate_samples(q, k, full, ph):
                dve.wait_ge(work_full, full)
                if k >= 2 or q:
                    dve.wait_ge(h_hi_ready, KD * q + (k - 1))
                    dve.wait_ge(h_lo_ready, KD * q + (k - 1))
                dst = seqs(h_f[:, k % 2, 0:P])
                bank = (k + ph) % 2
                at = own.step(tt(dst, seqs(ps[:, bank, 0:P]),
                                 shsc[:, 2 * ph + 1, k, 1:ROWS].unsqueeze(2).to_broadcast([P, SEQS, STEPS]), ALU.mult))
                after(at)
                tt(dst, dst, shsc[:, 2 * ph, k, 1:ROWS].unsqueeze(2).to_broadcast([P, SEQS, STEPS]), ALU.add)\
                    .then_inc(sample_mod, 1)

            def first_lo(m):
                s = (3 * m + 2) % RING
                dve.wait_ge(w_hi, 3 * m + 3)
                tt(wlo[:, s, :], raw[:, s, :], whi[:, s, :].bitcast(F32), ALU.subtract).then_inc(w_lo_vec, 1)

            for t_, n_ in ((xa, PAST), (u, HIST), (su, SHIST)):
                nc.vector.memset(t_[:, :, 0:n_], 0.0).then_inc(hist_zeroed, 1)
            first_lo(0)
            dve.wait_ge(mod_ready, 2)
            def h_rest(q, k, nt):
                dve.wait_ge(h_hi_ready, KD * q + (k + 1))
                tt(h_lo[:, k, 0:nt * P], h_f[:, k % 2, 0:nt * P], h_hi[:, k, 0:nt * P].bitcast(F32), ALU.subtract)\
                    .then_inc(h_lo_ready, 1)

            modulate_samples(0, 0, 1, 0)
            for k in range(KD):
                if k + 1 < KD:
                    modulate_samples(0, k + 1, k + 2, 0)
                h_rest(0, k, TB)
            first_lo(1)
            first_lo(2)
            dve.wait_ge(hist_zeroed, 3)
            dve.wait_ge(state_landed, 16 * NMIX)

            lo_done, taps = [3], [0]

            def lo_up_to(n):
                while lo_done[0] < min(n, NIN - 1):
                    first_lo(lo_done[0])
                    lo_done[0] += 1

            def mixers(b, nt_next):
                nt = tiles_of(b)
                first = is_first(b)
                c0 = P if first else 0
                np_ = nt * P - c0
                pc = slice(c0, c0 + np_)

                def both(samples, prompt):
                    if first:
                        own.step(samples())
                    return prompt()

                def glu(j):
                    if first:
                        lo_up_to(ORDER.index(("g", j)) + 1)
                    dve.wait_ge(work_read, group(b, ORDER.index(("g", j))) + 1)
                    a, g = pslot("a", j), pslot("g", j)
                    return own.step(both(
                        lambda: tt(u_s[:, j, :, HIST:], seqs(a[:, 0:P]), seqs(g[:, 0:P]), ALU.mult),
                        lambda: tt(u[:, j, HIST:HIST + np_], a[:, pc], g[:, pc], ALU.mult)))

                def tap(j, k, at):
                    z = pslot("a", j)
                    w = col[:, Q_WDW + j * TAPS + k:Q_WDW + j * TAPS + k + 1]
                    after(at)
                    if k == 0:
                        bias = col[:, Q_BDW + j:Q_BDW + j + 1]
                        i = both(
                            lambda: nc.vector.tensor_scalar(seqs(z[:, 0:P]), u_s[:, j, :, 0:STEPS], w, bias,
                                                            ALU.mult, ALU.add),
                            lambda: nc.vector.tensor_scalar(z[:, pc], u[:, j, 0:np_], w, bias, ALU.mult, ALU.add))
                    else:
                        i = both(
                            lambda: stt(seqs(z[:, 0:P]), u_s[:, j, :, k:k + STEPS], w, seqs(z[:, 0:P]),
                                        ALU.mult, ALU.add),
                            lambda: stt(z[:, pc], u[:, j, k:k + np_], w, z[:, pc], ALU.mult, ALU.add))
                    if k == TAPS - 1:
                        i.then_inc(z_ready, 1)
                        at = None
                    else:
                        at = own.step(i)
                    if first:
                        taps[0] += 1
                        if taps[0] % 7 == 0:
                            lo_up_to(lo_done[0] + 1)
                    return at

                at0, at1, at2 = glu(0), None, None
                head = HEAD_FIRST if first else HEAD
                for k in range(head):
                    at0 = tap(0, k, at0)
                at1 = glu(1)
                for k in range(head, TAPS):
                    at0 = tap(0, k, at0)
                    at1 = tap(1, k - head, at1)
                at2 = glu(2)
                for k in range(TAPS - head, TAPS):
                    at1 = tap(1, k, at1)
                    at2 = tap(2, k - (TAPS - head), at2)
                state2 = [at2, head]

                def tap2():
                    if state2[1] < TAPS:
                        state2[0] = tap(2, state2[1], state2[0])
                        state2[1] += 1

                def window_sums(c, x, w0, w1, n_, at):
                    after(at)
                    at = own.step(tt(w0(1, n_), x(1, n_), x(0, n_ - 1), ALU.add))
                    tap2()
                    half = slice(64, P) if c == 0 else slice(0, P)
                    after(at)
                    at = own.step(tt(w1(3, n_)[half], w0(3, n_)[half], w0(1, n_ - 2)[half], ALU.add))
                    tap2()
                    if c == 1:
                        after(at)
                        at = own.step(tt(w0(7, n_), w1(7, n_), w1(3, n_ - 4), ALU.add))
                        tap2()
                        after(at)
                        at = own.step(tt(w1(15, n_)[64:P], w0(15, n_)[64:P], w0(7, n_ - 8)[64:P], ALU.add))
                        tap2()
                    return at

                def pooling(c):
                    dve.wait_ge(work_read, group(b, ORDER.index(("x", c))) + 1)
                    at = None
                    if not first or c:
                        dve.wait_ge(pooled_ready, NPOOL * b + c)
                    out = pslot("g", c)
                    if first:
                        ext = PAST + STEPS
                        x = lambda lo, hi: xa_s[:, c, :, lo:hi]
                        ws = [wsum[:, i, 0:SEQS * ext].rearrange("p (s t) -> p s t", s=SEQS) for i in range(2)]
                        at = window_sums(c, x, lambda lo, hi: ws[0][:, :, lo:hi], lambda lo, hi: ws[1][:, :, lo:hi],
                                         ext, None)
                        after(at)
                        for i in range(2):
                            h = slice(64 * i, 64 * i + 64)
                            at = own.step(stt(seqs(out[:, 0:P])[h], ws[i][h, :, PAST:], 1.0 / WINDOWS[2 * c + i],
                                              xa_s[h, c, :, PAST:], ALU.mult, ALU.subtract))
                    x = lambda lo, hi: xa[:, c, lo:hi]
                    at = window_sums(c, x, lambda lo, hi: wsum[:, 0, lo:hi], lambda lo, hi: wsum[:, 1, lo:hi],
                                     PAST + np_, at)
                    if first:
                        after(at)
                        for i in range(2):
                            h = slice(64 * i, 64 * i + 64)
                            e = slice(E_CNT + c * PAST, E_CNT + (c + 1) * PAST)
                            at = own.step(tt(wsum[h, i, PAST:2 * PAST], wsum[h, i, PAST:2 * PAST], con_a[h, e], ALU.mult))
                    after(at)
                    for i in range(2):
                        h = slice(64 * i, 64 * i + 64)
                        ins = stt(out[h, pc], wsum[h, i, PAST:PAST + np_], 1.0 / WINDOWS[2 * c + i],
                                  xa[h, c, PAST:PAST + np_], ALU.mult, ALU.subtract)
                        if i == 0:
                            at = own.step(ins)
                        else:
                            ins.then_inc(pooled_ready, 1)
                    tap2()
                    if not is_last(b):
                        dve.wait_ge(pooled_ready, NPOOL * b + (c + 1))
                        keep_history(xa, c, PAST, np_)

                if first:
                    lo_up_to(NIN - 1)
                    columns(1, 7)
                    gate_factors()
                    gate(0)
                    gate(1)
                for j in range(1, NSC):
                    short_conv(b, j, tap2)
                    if first and j == 1:
                        gate(2)
                        gate(3)
                for c in range(NPOOL):
                    pooling(c)
                while state2[1] < TAPS:
                    tap2()
                if not is_last(b):
                    dve.wait_ge(z_ready, NCONV * (b + 1))
                    for j in range(NCONV):
                        keep_history(u, j, HIST, np_)
                dve.wait_ge(work_read, group(b, "mean") + 1)
                for j in range(NCONV):
                    z = pslot("a", j)[:, 0:nt * P]
                    tt(z, z, pslot("g", 2)[:, 0:nt * P], ALU.subtract).then_inc(zc_ready, 1)
                dve.wait_ge(seed_ready, b + 1)
                r, v, w = (pslot(*x)[:, 0:nt * P] for x in (("b", 2), ("g", 2), ("g", 0)))
                dve.wait_ge(y_lo_ready, NY1 * b + (Y.index(("g", 0)) + 1))
                after(own.step(tt(w, v, r, ALU.mult)))
                after(own.step(tt(w, w, r, ALU.mult)))
                after(own.step(nc.vector.tensor_scalar(w, w, -0.5, 1.5, ALU.mult, ALU.add)))
                after(own.step(tt(r, r, w, ALU.mult)))
                for j in range(NCONV):
                    z = pslot("a", j)[:, 0:nt * P]
                    tt(z, z, r, ALU.mult).then_inc(zn_ready, 1)
                if not is_last(b):
                    short_conv(b + 1, 0, lambda: None)
                if is_last(b):
                    residual(b, TB, gate1, gate1_first)
                w = slice(0, nt * P)
                for i in range(NY1, NMIX):
                    dve.wait_ge(y_hi_ready, NMIX * b + (i + 1))
                    tt(y_lo[:, i, w], y_src(i)[:, w], y_hi[:, i, w].bitcast(F32), ALU.subtract).then_inc(yb_lo_ready, 1)
                if not first and not is_last(b):
                    residual(b, TB, gate1, gate1_first)

            def gate_factors():
                dve.wait_ge(gpost_landed, 32)

            def keep_history(buf, j, n_hist, np_):
                own.step(nc.vector.tensor_copy(buf[:, j, 0:n_hist], buf[:, j, np_:np_ + n_hist]))

            def short_conv(b, j, between):
                nt, first = tiles_of(b), is_first(b)
                c0 = P if first else 0
                np_ = nt * P - c0
                pc = slice(c0, c0 + np_)

                def both(samples, prompt):
                    if first:
                        own.step(samples())
                    return prompt()

                dve.wait_ge(work_read, group(b, ORDER.index(("b", j))) + 1)
                h, c, g = pslot("h", j), pslot("c", j), pslot("b", j)
                at = own.step(both(lambda: tt(su_s[:, j, :, SHIST:], seqs(c[:, 0:P]), seqs(h[:, 0:P]), ALU.mult),
                                   lambda: tt(su[:, j, SHIST:SHIST + np_], c[:, pc], h[:, pc], ALU.mult)))
                between()
                for k in range(STAPS):
                    w = col[:, Q_WSC + j * STAPS + k:Q_WSC + j * STAPS + k + 1]
                    after(at)
                    if k == 0:
                        at = own.step(both(
                            lambda: nc.vector.tensor_scalar(seqs(c[:, 0:P]), su_s[:, j, :, 0:STEPS], w, None, ALU.mult),
                            lambda: nc.vector.tensor_scalar(c[:, pc], su[:, j, 0:np_], w, None, ALU.mult)))
                    else:
                        at = own.step(both(
                            lambda: stt(seqs(c[:, 0:P]), su_s[:, j, :, k:k + STEPS], w, seqs(c[:, 0:P]),
                                        ALU.mult, ALU.add),
                            lambda: stt(c[:, pc], su[:, j, k:k + np_], w, c[:, pc], ALU.mult, ALU.add)))
                    between()
                after(at)
                tt(h[:, 0:nt * P], c[:, 0:nt * P], g[:, 0:nt * P], ALU.mult).then_inc(yc_ready, 1)
                between()
                if not is_last(b):
                    keep_history(su, j, SHIST, np_)

            def residual(r, nt, gate_, gate_first):
                in_b = gate_ is gate2

                def scaled(t):
                    if t < 2:
                        dve.wait_ge(mix_rstd, 2 * r - 1 + t)
                    return own.step(stt(mix_ps(t), mix_ps(t), rstd_m[:, t:t + 1],
                                        (gate_ if t else gate_first)[:, :], ALU.mult, ALU.mult))

                def added(t, at):
                    after(at)
                    if t == 0:
                        dve.wait_ge(res_landed, 16 * (tiles_before(r - 1, in_b) + nt))
                    tt(xr[:, t, :], mix_ps(t), xr[:, t, :], ALU.add).then_inc(res_tiles, 1)

                ats = [scaled(0)]
                after(ats[0])
                own.step(nc.vector.tensor_copy(gate_first[:, :], gate_[:, :]))
                for t in range(nt):
                    if t + 1 < nt:
                        ats.append(scaled(t + 1))
                    added(t, ats[t])

            short_conv(0, 0, lambda: None)
            mixers(0, TB)
            own.enter_loop()
            with dve.Fori(1, NB - 2) as b:
                own.in_loop(b - 1, VEC_STEPS_A)
                mixers(b, TB)
            own.leave_loop(NB - 3, VEC_STEPS_A)
            mixers(NB - 2, LAST_TB)
            mixers(NB - 1, 0)
            for k in range(KD):
                modulate_samples(NB, k, FULL_A + k + 1, 1)

            def lo_up(b, m, par):
                s = 2 * par + 1
                dve.wait_ge(gu_hi, 2 * NF * b + 2 * m + 2)
                tt(wlo[:, s, :], raw[:, s, :], whi[:, s, :].bitcast(F32), ALU.subtract).then_inc(up_lo, 1)

            def lo_dn(b, k):
                dve.wait_ge(dn_hi, NF * b + k + 1)
                s = dn_slot(b, k)
                tt(dn_wlo[s], dn_raw[s], dn_whi[s].bitcast(F32), ALU.subtract).then_inc(dn_lo, 1)

            def hidden(b, m, par, nt, split):
                dve.wait_ge(silu_ready, NF * b + m + 1)
                dve.wait_ge(gu_used, 2 * NF * b + 2 * m + 2)
                tt(g_f[:, par, 0:nt * P], ps[:, 2 * par + 1, 0:nt * P], s_buf[:, par, 0:nt * P], ALU.mult)\
                    .then_inc(g_ready, 1)
                split()
                dve.wait_ge(g_hi_ready, NF * b + m + 1)
                one = bass.ds(m, 1)
                tt(g_lo[:, one, 0:nt * P].rearrange("p a n -> p (a n)"), g_f[:, par, 0:nt * P],
                   g_hi[:, one, 0:nt * P].rearrange("p a n -> p (a n)").bitcast(F32), ALU.subtract)\
                    .then_inc(g_lo_ready, 1)

            def ffn_block(b, nt_next):
                nt = tiles_of(b)
                with dve.Fori(0, NF // 2 - 1) as i:
                    for par in range(2):
                        hidden(b, 2 * i + par, par, nt, lambda: lo_up(b, 2 * i + par + 2, par))
                for par in range(2):
                    hidden(b, NF - 2 + par, par, nt, lambda: lo_dn(b, par))
                ahead = 5 if is_last(b) else 2
                for k in range(2, ahead):
                    lo_dn(b, k)
                for k in range(NF):
                    if k + ahead < NF:
                        lo_dn(b, k + ahead)
                    if nt_next and k >= 6 and k % 2 == 0 and (k - 6) // 2 < KD:
                        h_rest(NB + 1 + b, (k - 6) // 2, nt_next)
                if nt_next:
                    for par in range(2):
                        lo_up(b + 1, par, par)
                residual(NB + 1 + b, nt, gate2, gate2_first)

            for par in range(2):
                lo_up(0, par, par)
            residual(NB, LAST_TB, gate1, gate1_first)
            dve.wait_ge(states_stored, 16 * 2 * NMIX)
            ffn_block(0, TB)
            own.enter_loop()
            with dve.Fori(1, NB - 2) as b:
                own.in_loop(b - 1, VEC_STEPS_B)
                ffn_block(b, TB)
            own.leave_loop(NB - 3, VEC_STEPS_B)
            ffn_block(NB - 2, LAST_TB)
            ffn_block(NB - 1, 0)


def kernel(x_prompt, x_sample, c_prompt, c_sample, state_pool, state_conv, state_sconv,
           w_ada, b_ada, g_pre_mix, g_post_mix, g_pre_ffn, g_post_ffn,
           w_in, w_pool, s_pool, w_dw, b_dw, ln_g, ln_b, w_sc, w_out,
           w_gate, w_up, w_down):
    import numpy as np
    import concourse.bacc as bacc
    from concourse.bass_utils import run_bass_kernel_spmd

    def c(a):
        return np.ascontiguousarray(a)

    def channel_cols(a):
        n, ch = a.shape
        return a.T.reshape(ch // P, P, n).transpose(1, 0, 2)

    x_all = np.concatenate([np.asarray(x_sample).reshape(-1, D), np.asarray(x_prompt).reshape(-1, D)])
    c_all = c(channel_cols(np.concatenate([np.asarray(c_prompt), np.asarray(c_sample)])))

    consts = np.zeros((P, C_END), np.float32)
    consts[:, C_ID:C_ID + P] = np.eye(P)
    consts[:, C_EPS:C_EPS + TB] = EPS
    consts[:, C_NHALF:C_NHALF + TB] = -0.5
    consts_a = np.zeros((P, E_END), np.float32)
    consts_a[:, E_ONES:E_ONES + P] = 1
    for part in range(2):
        consts_a[part * ROWS, E_SELP:E_SELP + P] = 1
        for s in range(SEQS):
            consts_a[part * ROWS + 1 + s, E_SELS + s * STEPS:E_SELS + (s + 1) * STEPS] = 1
    consts_a[2 * ROWS, E_SELP:E_CNT] = 1
    for g, w in enumerate(WINDOWS):
        h, e = 64 * (g % 2), E_CNT + (g // 2) * PAST
        consts_a[h:h + 64, e:e + PAST] = w / np.minimum(np.arange(PAST) + 1, w)

    cols = np.concatenate([
        channel_cols(np.asarray(g_pre_mix)).reshape(P, -1), channel_cols(np.asarray(g_pre_ffn)).reshape(P, -1),
        channel_cols(np.asarray(s_pool)).reshape(P, -1), channel_cols(np.asarray(w_dw)[0]).reshape(P, -1),
        channel_cols(np.asarray(b_dw)).reshape(P, -1), channel_cols(np.asarray(ln_g)).reshape(P, -1),
        channel_cols(np.asarray(ln_b)).reshape(P, -1), channel_cols(np.asarray(w_sc)[0]).reshape(P, -1)], axis=1)
    gpost = np.concatenate([np.asarray(g_post_mix), np.asarray(g_post_ffn)])

    def stationary_units(w):
        return w.reshape(KD, P, -1, P).transpose(2, 1, 0, 3).reshape(-1, P, D)

    wi = stationary_units(np.asarray(w_in)[0])
    w_mix = np.concatenate([np.stack([wi[COL0[kind] // P + j] for kind, j in ORDER]),
                            np.asarray(w_out)[0].reshape(NMIX, P, D)[[Y_ROW[kind] + j for kind, j in Y]]])
    w_gu = np.stack([stationary_units(np.asarray(w_gate)[0]), stationary_units(np.asarray(w_up)[0])], axis=1)\
        .reshape(2 * NF, P, D)
    w_dn = np.asarray(w_down)[0].reshape(NF, P, D)
    wa = np.asarray(w_ada)[0].reshape(KD, P, 6, D).transpose(2, 0, 1, 3).reshape(6 * KD, P, D)

    def state_cols(a):
        bb, rows, ch = a.shape
        return a.transpose(2, 0, 1).reshape(ch // P, P, bb, rows).transpose(1, 0, 2, 3)

    ins = dict(x_all=x_all, c_all=c_all, consts=consts, consts_a=consts_a, cols=cols, gpost=gpost,
               b_ada=np.asarray(b_ada), w_ada=wa, w_mix=w_mix, w_pool=np.asarray(w_pool)[0], w_gu=w_gu, w_dn=w_dn,
               st_pool=state_cols(np.asarray(state_pool)[0]), st_conv=state_cols(np.asarray(state_conv)[0]),
               st_sconv=state_cols(np.asarray(state_sconv)[0]))
    outs = dict(y_all=(TILES * P, D), o_pool_p=(P, NPOOL, PAST), o_conv_p=(P, NCONV, HIST),
                o_sconv_p=(P, NSC, SHIST), o_pool_s=(P, NPOOL, SEQS, PAST), o_conv_s=(P, NCONV, SEQS, HIST),
                o_sconv_s=(P, NSC, SEQS, SHIST))
    nc = bacc.Bacc("TRN2", target_bir_lowering=False, num_devices=1)
    ins = {k: c(v) for k, v in ins.items()}
    aps = [nc.dram_tensor(f"in_{k}", v.shape, F32, kind="ExternalInput").ap() for k, v in ins.items()]
    aps += [nc.dram_tensor(f"out_{k}", s, F32, kind="ExternalOutput").ap() for k, s in outs.items()]
    aps.append(nc.dram_tensor("x1_all", (TILES * P, D), F32, kind="Internal").ap())
    build(nc, *aps)
    r = run_bass_kernel_spmd(nc, [{f"in_{k}": v for k, v in ins.items()}], core_ids=[0]).results[0]

    def state_rows(a, seqs):
        a = a.reshape(P, a.shape[1], seqs, -1)
        return c(a.transpose(2, 3, 1, 0).reshape(1, seqs, a.shape[3], -1))

    y = r["out_y_all"]
    return (c(y[T_SAMPLE:].reshape(1, T_PROMPT, D)), c(y[:T_SAMPLE].reshape(SEQS, STEPS, D)),
            state_rows(r["out_o_pool_p"], 1), state_rows(r["out_o_conv_p"], 1), state_rows(r["out_o_sconv_p"], 1),
            state_rows(r["out_o_pool_s"], SEQS), state_rows(r["out_o_conv_s"], SEQS),
            state_rows(r["out_o_sconv_s"], SEQS))
```
